# Optimizing a Trainium2 kernel written in Bass

```python
import jax, jax.numpy as jnp
from jax import lax
import numpy as np

D_MODEL = 2048
BATCH = 1
SEQ = 256
DEPTH = 1

D_FF = 5632
CONV_WIDTH = 1024
CONV_K = 3
N_HEADS = 16
N_KV = 4
GROUP = N_HEADS // N_KV
HEAD_DIM = 64
ATTN_WIDTH = N_HEADS * HEAD_DIM
MIX_WIDTH = CONV_WIDTH + ATTN_WIDTH
KV_WIDTH = N_KV * HEAD_DIM
CMP_BLOCK = 32
CMP_STRIDE = 16
CMP_HIDDEN = 256
SLC_BLOCK = 64
SLC_TOPK = 16
N_LOCAL = 2
WINDOW = 512
Q_BLOCK = 128
N_GATES = 3
ROPE_THETA = 10000.0
EPS = 1e-6
NEG = -1e30
FORCE = 1e9
IN_WIDTH = 3 * CONV_WIDTH + ATTN_WIDTH + 6 * KV_WIDTH + N_GATES * N_HEADS

kernel_name = "hybrid_conv_nsa_macaron"

def rmsnorm(x, g):
    xf = x.astype(jnp.float32)
    y = xf * lax.rsqrt(jnp.mean(xf * xf, axis=-1, keepdims=True) + EPS)
    return (y * g.astype(jnp.float32)).astype(x.dtype)

def swiglu(h, wg, wu, wd):
    return (jax.nn.silu(h @ wg) * (h @ wu)) @ wd

def rope_tables(s):
    pos = jnp.arange(s, dtype=jnp.float32)
    inv = ROPE_THETA ** (-jnp.arange(0, HEAD_DIM, 2, dtype=jnp.float32) / HEAD_DIM)
    ang = pos[:, None] * inv[None, :]
    return jnp.cos(ang), jnp.sin(ang)

def apply_rope(x, cos, sin):
    x1, x2 = jnp.split(x, 2, axis=-1)
    c = cos[None, :, None, :]
    s = sin[None, :, None, :]
    return jnp.concatenate([x1 * c - x2 * s, x2 * c + x1 * s], axis=-1).astype(x.dtype)

def masked_softmax(s, mask):
    s = jnp.where(mask, s.astype(jnp.float32), NEG)
    return jax.nn.softmax(s, axis=-1) * mask

def short_conv_mixer(h, b_gate, c_gate, conv_w):
    u = c_gate * h
    y = lax.conv_general_dilated(
        u, conv_w[:, None, :].astype(u.dtype), window_strides=(1,),
        padding=[(CONV_K - 1, 0)], dimension_numbers=("NWC", "WIO", "NWC"),
        feature_group_count=CONV_WIDTH)
    return b_gate * y

def compress(tok, w1, w2, pe):
    s = tok.shape[1]
    n_cmp = (s - CMP_BLOCK) // CMP_STRIDE + 1
    idx = jnp.arange(n_cmp)[:, None] * CMP_STRIDE + jnp.arange(CMP_BLOCK)[None, :]
    blocks = tok[:, idx] + pe[None, None, :, None, :]
    hid = jax.nn.gelu(jnp.einsum('bnlhd,ldf->bnhf', blocks, w1))
    return jnp.einsum('bnhf,fd->bnhd', hid, w2)

def nsa_attention(q, kc, vc, ks, vs, kw, vw, gates):
    bsz, s = q.shape[0], q.shape[1]
    n_cmp = kc.shape[1]
    n_slc = s // SLC_BLOCK
    top_k = min(SLC_TOPK, n_slc)
    n_qb = s // Q_BLOCK
    q = (q * (HEAD_DIM ** -0.5)).reshape(bsz, s, N_KV, GROUP, HEAD_DIM)
    gates = gates.reshape(bsz, s, N_KV, GROUP, N_GATES)

    cmp_start = jnp.arange(n_cmp) * CMP_STRIDE
    cmp_end = cmp_start + CMP_BLOCK - 1
    slc_start = jnp.arange(n_slc) * SLC_BLOCK
    overlap = jnp.clip(jnp.minimum(cmp_start[:, None] + CMP_BLOCK, slc_start[None, :] + SLC_BLOCK)
                       - jnp.maximum(cmp_start[:, None], slc_start[None, :]), 0, None)
    overlap = overlap.astype(jnp.float32) / CMP_BLOCK

    ks_blk = ks.reshape(bsz, n_slc, SLC_BLOCK, N_KV, HEAD_DIM).transpose(0, 3, 1, 2, 4)
    vs_blk = vs.reshape(bsz, n_slc, SLC_BLOCK, N_KV, HEAD_DIM).transpose(0, 3, 1, 2, 4)
    kw_pad = jnp.pad(kw, ((0, 0), (WINDOW, 0), (0, 0), (0, 0)))
    vw_pad = jnp.pad(vw, ((0, 0), (WINDOW, 0), (0, 0), (0, 0)))
    bi = jnp.arange(bsz)[:, None, None, None]
    hi = jnp.arange(N_KV)[None, None, :, None]
    jblk = jnp.arange(n_slc)

    def block(c):
        s0 = c * Q_BLOCK
        qc = lax.dynamic_slice_in_dim(q, s0, Q_BLOCK, axis=1)
        gc = lax.dynamic_slice_in_dim(gates, s0, Q_BLOCK, axis=1)
        t = s0 + jnp.arange(Q_BLOCK)

        sc = jnp.einsum('bqhgd,bnhd->bqhgn', qc, kc)
        mc = (cmp_end[None, :] <= t[:, None])[None, :, None, None, :]
        pc = masked_softmax(sc, mc)
        o_cmp = jnp.einsum('bqhgn,bnhd->bqhgd', pc.astype(vc.dtype), vc)

        imp = jnp.einsum('bqhgn,nj->bqhj', pc, overlap)
        tb = t // SLC_BLOCK
        forced = (jblk[None, :] == 0) | ((jblk[None, :] <= tb[:, None])
                                         & (jblk[None, :] > tb[:, None] - N_LOCAL))
        valid = slc_start[None, :] <= t[:, None]
        imp = jnp.where(forced[None, :, None, :], FORCE, imp)
        imp = jnp.where(valid[None, :, None, :], imp, NEG)
        top_val, top_idx = lax.top_k(imp, top_k)
        sel_ok = top_val > 0.5 * NEG
        k_sel = ks_blk[bi, hi, top_idx]
        v_sel = vs_blk[bi, hi, top_idx]
        k_sel = k_sel.reshape(bsz, Q_BLOCK, N_KV, top_k * SLC_BLOCK, HEAD_DIM)
        v_sel = v_sel.reshape(bsz, Q_BLOCK, N_KV, top_k * SLC_BLOCK, HEAD_DIM)
        pos = top_idx[..., None] * SLC_BLOCK + jnp.arange(SLC_BLOCK)
        ms = sel_ok[..., None] & (pos <= t[None, :, None, None, None])
        ms = ms.reshape(bsz, Q_BLOCK, N_KV, 1, top_k * SLC_BLOCK)
        ss = jnp.einsum('bqhgd,bqhmd->bqhgm', qc, k_sel)
        ps = masked_softmax(ss, ms)
        o_slc = jnp.einsum('bqhgm,bqhmd->bqhgd', ps.astype(v_sel.dtype), v_sel)

        kwc = lax.dynamic_slice_in_dim(kw_pad, s0, Q_BLOCK + WINDOW, axis=1)
        vwc = lax.dynamic_slice_in_dim(vw_pad, s0, Q_BLOCK + WINDOW, axis=1)
        p = s0 - WINDOW + jnp.arange(Q_BLOCK + WINDOW)
        dist = t[:, None] - p[None, :]
        mw = ((dist >= 0) & (dist < WINDOW) & (p >= 0)[None, :])[None, :, None, None, :]
        sw = jnp.einsum('bqhgd,bkhd->bqhgk', qc, kwc)
        pw = masked_softmax(sw, mw)
        o_win = jnp.einsum('bqhgk,bkhd->bqhgd', pw.astype(vwc.dtype), vwc)

        o = gc[..., 0:1] * o_cmp + gc[..., 1:2] * o_slc + gc[..., 2:3] * o_win
        return o.reshape(bsz, Q_BLOCK, ATTN_WIDTH)

    out = lax.map(block, jnp.arange(n_qb))
    return out.transpose(1, 0, 2, 3).reshape(bsz, s, ATTN_WIDTH)

def hybrid_mixer(h, w_in, conv_w, cmp_k_w1, cmp_k_w2, cmp_k_pe, cmp_v_w1, cmp_v_w2,
                 cmp_v_pe, conv_out_norm, attn_out_norm, w_out, cos, sin):
    bsz, s, _ = h.shape
    proj = h @ w_in
    sizes = [CONV_WIDTH, CONV_WIDTH, CONV_WIDTH, ATTN_WIDTH] + [KV_WIDTH] * 6
    cuts = list(np.cumsum(sizes))
    (c_h, c_b, c_c, q, k_c, v_c, k_s, v_s, k_w, v_w, g) = jnp.split(proj, cuts, axis=-1)

    y_conv = short_conv_mixer(c_h, c_b, c_c, conv_w)

    hd = lambda a, n: a.reshape(bsz, s, n, HEAD_DIM)
    q = apply_rope(hd(q, N_HEADS), cos, sin)
    k_c = apply_rope(hd(k_c, N_KV), cos, sin)
    k_s = apply_rope(hd(k_s, N_KV), cos, sin)
    k_w = apply_rope(hd(k_w, N_KV), cos, sin)
    kc = compress(k_c, cmp_k_w1, cmp_k_w2, cmp_k_pe)
    vc = compress(hd(v_c, N_KV), cmp_v_w1, cmp_v_w2, cmp_v_pe)
    gates = jax.nn.sigmoid(g).reshape(bsz, s, N_HEADS, N_GATES)
    y_attn = nsa_attention(q, kc, vc, k_s, hd(v_s, N_KV), k_w, hd(v_w, N_KV), gates)

    y = jnp.concatenate([rmsnorm(y_conv, conv_out_norm), rmsnorm(y_attn, attn_out_norm)], axis=-1)
    return y @ w_out

def setup_inputs(seed: int = 0) -> dict:
    key = jax.random.key(seed)
    ks = jax.random.split(key, 24)
    f32 = jnp.float32
    nrm = lambda k, shape, scale: (jax.random.normal(k, shape, f32) * scale)
    gain = lambda k, n: 1.0 + 0.02 * jax.random.normal(k, (DEPTH, n), f32)
    L = DEPTH
    return {
        "x": jax.random.normal(ks[0], (BATCH, SEQ, D_MODEL), f32),
        "ffn1_norm": gain(ks[1], D_MODEL),
        "ffn1_wg": nrm(ks[2], (L, D_MODEL, D_FF), D_MODEL ** -0.5),
        "ffn1_wu": nrm(ks[3], (L, D_MODEL, D_FF), D_MODEL ** -0.5),
        "ffn1_wd": nrm(ks[4], (L, D_FF, D_MODEL), D_FF ** -0.5),
        "mix_norm": gain(ks[5], D_MODEL),
        "w_in": nrm(ks[6], (L, D_MODEL, IN_WIDTH), D_MODEL ** -0.5),
        "conv_w": nrm(ks[7], (L, CONV_K, CONV_WIDTH), CONV_K ** -0.5),
        "cmp_k_w1": nrm(ks[8], (L, CMP_BLOCK, HEAD_DIM, CMP_HIDDEN), (CMP_BLOCK * HEAD_DIM) ** -0.5),
        "cmp_k_w2": nrm(ks[9], (L, CMP_HIDDEN, HEAD_DIM), CMP_HIDDEN ** -0.5),
        "cmp_k_pe": nrm(ks[10], (L, CMP_BLOCK, HEAD_DIM), 0.1),
        "cmp_v_w1": nrm(ks[11], (L, CMP_BLOCK, HEAD_DIM, CMP_HIDDEN), (CMP_BLOCK * HEAD_DIM) ** -0.5),
        "cmp_v_w2": nrm(ks[12], (L, CMP_HIDDEN, HEAD_DIM), CMP_HIDDEN ** -0.5),
        "cmp_v_pe": nrm(ks[13], (L, CMP_BLOCK, HEAD_DIM), 0.1),
        "conv_out_norm": gain(ks[14], CONV_WIDTH),
        "attn_out_norm": gain(ks[15], ATTN_WIDTH),
        "w_out": nrm(ks[16], (L, MIX_WIDTH, D_MODEL), MIX_WIDTH ** -0.5),
        "ffn2_norm": gain(ks[17], D_MODEL),
        "ffn2_wg": nrm(ks[18], (L, D_MODEL, D_FF), D_MODEL ** -0.5),
        "ffn2_wu": nrm(ks[19], (L, D_MODEL, D_FF), D_MODEL ** -0.5),
        "ffn2_wd": nrm(ks[20], (L, D_FF, D_MODEL), D_FF ** -0.5),
        "final_norm": 1.0 + 0.02 * jax.random.normal(ks[21], (D_MODEL,), f32),
    }

def reference(x, ffn1_norm, ffn1_wg, ffn1_wu, ffn1_wd, mix_norm, w_in, conv_w,
              cmp_k_w1, cmp_k_w2, cmp_k_pe, cmp_v_w1, cmp_v_w2, cmp_v_pe,
              conv_out_norm, attn_out_norm, w_out, ffn2_norm, ffn2_wg, ffn2_wu,
              ffn2_wd, final_norm):
    cos, sin = rope_tables(x.shape[1])
    for i in range(DEPTH):
        x = x + 0.5 * swiglu(rmsnorm(x, ffn1_norm[i]), ffn1_wg[i], ffn1_wu[i], ffn1_wd[i])
        x = x + hybrid_mixer(rmsnorm(x, mix_norm[i]), w_in[i], conv_w[i],
                             cmp_k_w1[i], cmp_k_w2[i], cmp_k_pe[i],
                             cmp_v_w1[i], cmp_v_w2[i], cmp_v_pe[i],
                             conv_out_norm[i], attn_out_norm[i], w_out[i], cos, sin)
        x = x + 0.5 * swiglu(rmsnorm(x, ffn2_norm[i]), ffn2_wg[i], ffn2_wu[i], ffn2_wd[i])
    return rmsnorm(x, final_norm)


_drawn_inputs = setup_inputs


def setup_inputs(seed=0):
    import zlib

    import numpy as np

    out = dict(_drawn_inputs(seed))
    spreads = {}
    factors = {'ffn1_norm': 5.03,
     'cmp_k_pe': 5.458,
     'conv_out_norm': 5.827,
     'attn_out_norm': 5.85,
     'ffn2_norm': 8.0,
     'final_norm': 2.747}
    for name, (base, spread) in spreads.items():
        noise = np.random.default_rng([zlib.crc32(name.encode()), seed]).standard_normal(out[name].shape)
        drawn = base * np.exp(spread * noise) if base else spread * noise
        out[name] = __import__('jax').numpy.asarray(drawn.astype(out[name].dtype))
    for name, factor in factors.items():
        out[name] = (out[name] * factor).astype(out[name].dtype)
    return out
```

```python
import concourse.bass as bass
from concourse import mybir
from contextlib import ExitStack

F32 = mybir.dt.float32
F32R = mybir.dt.float32r
BF16 = mybir.dt.bfloat16
ALU = mybir.AluOpType
ACT = mybir.ActivationFunctionType
AX = mybir.AxisListType

P = 128
TOK = 256
NT = TOK // P
DM = 2048
FF = 5632
CH = 512
KD = DM // P
KF = FF // P
NFC = FF // CH
NDC = DM // CH
GK = 2
SLOTS = 4
CONV = 1024
CT = CONV // P
HEADS, KV, GRP, HD = 16, 4, 4, 64
CMP_BLOCK, CMP_STRIDE, CMP_HID = 32, 16, 256
NCMP = (TOK - CMP_BLOCK) // CMP_STRIDE + 1
NCP = 16
EPS = 1e-6
BIG = 1e30

JD = KD // GK
JF = KF // GK
JH = CT // GK
FFN_GROUPS = 2 * NFC * JD + NDC * JF
FFN0 = [0, FFN_GROUPS + 12 * JD + 2 * NDC * JH]
MIX0 = FFN_GROUPS
IN_JOB = [MIX0 + JD * j for j in range(11)]
CMP_JOB = MIX0 + 11 * JD
OUT_JOB = [CMP_JOB + JD + JH * n for n in range(2 * NDC)]
END = FFN0[1] + FFN_GROUPS
IN_COL = [2560, 3072, 3584, 4096, 4608, 5120, 0, 512, 1536, 1024, 2048]
GATE_COL = 5632
NG = 3 * HEADS
CONV_K_ORDER = [2, 3, 0, 1]

V_FFN1, V_MIX, V_FFN2, V_CONVW, V_GC, V_GA, V_PEK, V_PEV, NVEC = 0, 16, 32, 48, 72, 80, 88, 104, 120

C_ID, C_CAUSAL, C_CMASK, C_BMASK, C_VALID, C_COS, C_SIN, C_ONE = 0, 128, 256, 288, 292, 294, 422, 550
NCONST = 551

RS_FFN1, RS_MIX, RS_CONV, RS_ATT, RS_FFN2, RS_FINAL = range(6)


def mixer_banks():
    uses = [(("q", n), 6 + n % 2) for n in range(4)]
    uses += [(("kvd", n), 6 + n % 2) for n in range(4)]
    uses += [(("gates",), 5), (("kT", 0), 6), (("kT", 1), 7)]
    conv = {17: ("cu", 2), 18: ("cu", 3), 22: ("cb", 2), 23: ("cb", 3)}
    for m in range(2 * HEADS + 2):
        if m >= 2 and (m - 2) % GRP == 0:
            uses.append((("O", (m - 2) // GRP), 5))
        if 1 <= m <= 2 * HEADS:
            uses.append((("PT", m - 1), 4))
        if m < 2 * HEADS:
            uses.append((("QK", m), 6 + m % 2))
        if m in conv:
            uses.append((conv[m], 6 + (m + 1) % 2))
    uses += [(("cu", 0), 6), (("cu", 1), 7), (("cb", 0), 6), (("cb", 1), 7), (("css",), 5)]
    uses += [(("hidT",), 6), (("kcvc",), 7), (("cs", 0), 6), (("cs", 1), 7), (("pcT", 0), 6), (("pcT", 1), 7)]
    uses += [(("Oc", 0), 6), (("Oc", 1), 7), (("Oc", 2), 6), (("Oc", 3), 7)]
    uses += [(("aT", n, b), 4 + b) for n in range(2) for b in range(2)]
    first = {4: NDC + NFC + NDC, 5: NDC + NFC + NDC, 6: 0, 7: 0}
    seen, table = dict(first), {}
    for key, bank in uses:
        table[key] = (bank, seen[bank])
        seen[bank] += 1
    return table, conv, seen


def count(c, i=None, per=0):
    return c if i is None else i * per + c


def build_program(nc, a, out):
    USE, CONV_TICK, seen = mixer_banks()
    GU_USE = [NDC, seen[4] + NDC]
    XT_USE = {0: 0, 1: NDC + NFC, 2: seen[4]}
    assert seen[4] == seen[5] or True
    XT_USE5 = {0: 0, 1: NDC + NFC, 2: seen[5]}
    GU_USE5 = [NDC, seen[5] + NDC]

    def operand_use(kind, which, b, n=0, i=None):
        base = {"x": (XT_USE, XT_USE5), "gu": (GU_USE, GU_USE5)}[kind][b][which]
        return base + n, i

    rows = lambda w: w.rearrange("(k p) n -> p k n", p=P)
    wg = [rows(a["ffn1_wg"][0]), rows(a["ffn2_wg"][0])]
    wu = [rows(a["ffn1_wu"][0]), rows(a["ffn2_wu"][0])]
    wd = [rows(a["ffn1_wd"][0]), rows(a["ffn2_wd"][0])]
    w_in = rows(a["w_in"][0])
    w_out = rows(a["w_out"][0])
    w1 = [a[f"cmp_{n}_w1"][0].rearrange("(k l) d f -> (l d) k f", l=2) for n in "kv"]
    w2 = [a[f"cmp_{n}_w2"][0].rearrange("(k p) d -> p k d", p=P) for n in "kv"]
    x_in = a["x"][0].rearrange("(t p) d -> p t d", p=P)
    y_out = out[0].rearrange("(t p) d -> p t d", p=P)

    at = [(nc.sbuf_base + 63) // 64 * 64]
    limit = nc.sbuf_usable_end

    def sb(name, shape, dt=F32):
        size = 2 if dt == BF16 else 4
        for n in shape[1:]:
            size *= n
        t = nc.alloc_sbuf_tensor_at(name, shape, dt, offset=at[0])
        at[0] += (size + 31) // 32 * 32
        assert at[0] <= limit, (name, at[0], limit)
        return t

    consts = sb("consts", [P, NCONST])
    vec_rows = sb("vec_rows", [P, P])
    vecs = sb("vecs", [P, NVEC])
    ident_b = sb("ident_b", [P, P], BF16)
    causal_b = sb("causal_b", [P, 2, P], BF16)
    cmask_b = sb("cmask_b", [P, NT, HEADS, NCP], BF16)
    w2k = sb("w2k", [P, 2, 2, HD])
    w2v = sb("w2v", [P, 2, HD])
    ssq = sb("ssq", [P, 6, NT, NDC])
    var = sb("var", [P, 6, NT])
    rs = sb("rs", [P, 6, NT])
    junk = sb("junk", [P, CONV], BF16)
    x = sb("x", [P, NT, DM])
    raw = sb("raw", [P, SLOTS, GK, CH])
    w_hi = sb("w_hi", [P, SLOTS, GK, CH], F32R)
    w_lo = sb("w_lo", [P, SLOTS, GK, CH], F32R)
    h_at = at[0]
    hT_hi = sb("hT_hi", [P, KD, TOK], F32R)
    hT_lo = sb("hT_lo", [P, KD, TOK], F32R)
    zone = at[0]
    at[0] = h_at
    g_fin = sb("g_fin", [P, DM])
    at[0] = h_at + 4 * KD * TOK
    y_fin = sb("y_fin", [P, NT, DM])
    at[0] = zone
    guT_hi = sb("guT_hi", [P, KF, TOK], F32R)
    guT_lo = sb("guT_lo", [P, KF, TOK], F32R)
    gu = sb("gu", [P, NT, CH])
    at[0] = zone
    y_at = at[0]
    p_cc = sb("p_cc", [P, NT, CH])
    p_kvc = sb("p_kvc", [P, NT, CH])
    p_q = sb("p_q", [P, NT, CONV])
    p_kv = sb("p_kv", [P, NT, 2 * CH])
    p_h = sb("p_h", [P, NT, CONV])
    p_b = sb("p_b", [P, NT, CONV])
    uT = sb("uT", [P, CT, TOK + 2])
    ycT_lo = sb("ycT_lo", [P, CT, TOK], F32R)
    blk_at = at[0]
    blk_hi = sb("blk_hi", [P, KD, P], F32R)
    blk_lo = sb("blk_lo", [P, KD, P], F32R)
    qk_at = at[0]
    qT = sb("qT", [P, 8, TOK])
    kT = sb("kT", [P, 2, 2, TOK])
    p_at = at[0]
    prob = sb("prob", [P, 2, CH])
    probT = sb("probT", [P, 2, CH])
    scr = sb("scr", [P, CONV])
    w_gate = sb("w_gate", [P, KD, NG])
    den = sb("den", [P, NT, HEADS, 3])
    mins = sb("mins", [P, 2 * HEADS, 2])
    sums = sb("sums", [P, 2 * HEADS, 2])
    coef = sb("coef", [P, GRP, 2])
    cmin = sb("cmin", [P, NT, HEADS])
    csum = sb("csum", [P, NT, HEADS])
    top = at[0]
    at[0] = y_at
    ycT_hi = sb("ycT_hi", [P, CT, TOK], F32R)
    y_att = p_q
    blk_f = p_b[:, :, :].rearrange("p t (k m) -> p (t k) m", m=P)
    at[0] = p_at
    kvd = sb("kvd", [P, NT, 2, KV, 2 * HD])
    kT2 = uT[:, :, 0:TOK].rearrange("p (v j) t -> p v j t", v=2)
    at[0] = qk_at
    aT_hi = sb("aT_hi", [P, CT, TOK], F32R)
    aT_lo = sb("aT_lo", [P, CT, TOK], F32R)
    at[0] = blk_at
    hidkT = sb("hidkT", [P, 2, KV * NCP])
    hidvT = sb("hidvT", [P, 2, KV, GRP, NCP])
    kcT = sb("kcT", [P, KV, NCP])
    vcb = sb("vcb", [P, 2, GRP, HD])
    pc = sb("pc", [P, NT, HEADS, NCP])
    pcT = sb("pcT", [P, NT, 2, P])
    assert at[0] <= qk_at
    at[0] = top

    ident = consts[:, C_ID:C_ID + P]
    cos_t = consts[:, C_COS:C_COS + NT * HD].rearrange("p (t d) -> p t d", t=NT)
    sin_t = consts[:, C_SIN:C_SIN + NT * HD].rearrange("p (t d) -> p t d", t=NT)
    ones = consts[:, C_ONE:C_ONE + 1]

    def cv(c, n=1):
        lo = (c // 4) * CH + (c % 2) * TOK
        return p_h[:, (c % 4) // 2, lo:lo + n * TOK]

    ctx = ExitStack()
    with ctx:
        ps = ctx.enter_context(nc.psum_tensor("ps", [P, 8, CH], F32))
        sem = lambda n: ctx.enter_context(nc.semaphore(n))

        landed = [sem(f"landed{s}") for s in range(SLOTS)]
        hi_ready = sem("hi_ready")
        lo_ready = sem("lo_ready")
        group_done = sem("group_done")
        x_landed = [sem(f"x_landed{n}") for n in range(NDC)]
        consts_landed = sem("consts_landed")
        small_landed = sem("small_landed")
        gate_w_landed = sem("gate_w_landed")
        g_fin_landed = sem("g_fin_landed")
        masks_ready = sem("masks_ready")
        vecs_full = sem("vecs_full")
        vecs_ready = sem("vecs_ready")
        full = {b: sem(f"bank_full{b}") for b in (4, 5, 6, 7)}
        free = {b: sem(f"bank_free{b}") for b in (4, 5, 6, 7)}
        operand_hi = sem("operand_hi")
        ssq_done = sem("ssq_done")
        var_done = sem("var_done")
        root_done = sem("root_done")
        rs_done = sem("rs_done")
        silu_done = sem("silu_done")
        gu_done = sem("gu_done")
        resid_done = sem("resid_done")
        proj_done = sem("proj_done")
        q_roped = sem("q_roped")
        kvd_ready = sem("kvd_ready")
        ks_roped = sem("ks_roped")
        kT2_ready = sem("kT2_ready")
        pads_zero = sem("pads_zero")
        blk_ready = sem("blk_ready")
        blk_hi_ready = sem("blk_hi_ready")
        blk_lo_ready = sem("blk_lo_ready")
        gates_scaled = sem("gates_scaled")
        gates_exp = sem("gates_exp")
        mins_ready = sem("mins_ready")
        u_ready = sem("u_ready")
        conv_ready = sem("conv_ready")
        ysq_ready = sem("ysq_ready")
        ycT_hi_ready = sem("ycT_hi_ready")
        ycT_lo_ready = sem("ycT_lo_ready")
        gelu_in = sem("gelu_in")
        gelu_exp = sem("gelu_exp")
        hid_ready = sem("hid_ready")
        cdiff_ready = sem("cdiff_ready")
        cexp_ready = sem("cexp_ready")
        y_att_ready = sem("y_att_ready")
        final_ready = sem("final_ready")
        stored = sem("stored")
        act_step = sem("act_step")
        dve_step = sem("dve_step")

        def landed_value(c, i=None, per=0):
            extra = 0
            if c >= CMP_JOB:
                extra = min((c - CMP_JOB) // SLOTS + 1, JD // SLOTS)
            return count(16 * (c // SLOTS + 1 + extra), i, 16 * per // SLOTS)

        block = ctx.enter_context(nc.Block())

        @block.sync
        def _(sp):
            def load(c, src, i=None, per=0, halves=None):
                if c >= SLOTS:
                    sp.wait_ge(lo_ready, count(c - SLOTS + 1, i, per))
                s = c % SLOTS
                if halves is None:
                    sp.dma_start(raw[:, s, :, :], src).then_inc(landed[s], 16)
                else:
                    sp.dma_start(raw[:, s, :, 0:CMP_HID], halves[0]).then_inc(landed[s], 16)
                    sp.dma_start(raw[:, s, :, CMP_HID:CH], halves[1]).then_inc(landed[s], 16)

            def ffn(f):
                c = FFN0[f]
                for j in range(JD):
                    load(c + j, wg[f][:, GK * j:GK * j + GK, 0:CH])
                c += JD
                with sp.Fori(0, NFC - 1) as i:
                    for j in range(JD):
                        load(c + j, wu[f][:, GK * j:GK * j + GK, bass.ds(i * CH, CH)], i, 2 * JD)
                    for j in range(JD):
                        load(c + JD + j, wg[f][:, GK * j:GK * j + GK, bass.ds(i * CH + CH, CH)], i, 2 * JD)
                c += 2 * JD * (NFC - 1)
                for j in range(JD):
                    load(c + j, wu[f][:, GK * j:GK * j + GK, (NFC - 1) * CH:FF])
                c += JD
                for n in range(NDC):
                    if f == 1 and n == 1:
                        sp.wait_ge(group_done, c)
                        sp.dma_start(g_fin[:, :], a["final_norm"].partition_broadcast(P)).then_inc(g_fin_landed, 16)
                    for j in range(JF):
                        load(c + JF * n + j, wd[f][:, GK * j:GK * j + GK, n * CH:n * CH + CH])

            for n in range(NDC):
                sp.dma_start(x[:, :, n * CH:n * CH + CH], x_in[:, :, n * CH:n * CH + CH]).then_inc(x_landed[n], 16)
            ffn(0)
            for job, (c, col) in enumerate(zip(IN_JOB, IN_COL)):
                if job == 1:
                    sp.wait_ge(group_done, MIX0)
                    sp.dma_start(w_gate[:, :, :], w_in[:, :, GATE_COL:GATE_COL + NG]).then_inc(gate_w_landed, 16)
                for j in range(JD):
                    load(c + j, w_in[:, GK * j:GK * j + GK, col:col + CH])
            for j in range(JD):
                k = slice(GK * j, GK * j + GK)
                load(CMP_JOB + j, None, halves=(w1[0][:, k, :], w1[1][:, k, :]))
            for n, c in enumerate(OUT_JOB):
                for j in range(JH):
                    k = GK * (CONV_K_ORDER[j] if n < NDC else JH + j)
                    load(c + j, w_out[:, k:k + GK, n % NDC * CH:(n % NDC + 1) * CH])
            ffn(1)
            for piece in range(4):
                t, h = piece // 2, piece % 2
                sp.wait_ge(final_ready, piece + 1)
                sp.dma_start(y_out[:, t, h * CONV:(h + 1) * CONV],
                             y_fin[:, t, h * CONV:(h + 1) * CONV]).then_inc(stored, 16)
            sp.wait_ge(stored, 64)

        @block.gpsimd
        def _(pool):
            pool.wait_ge(consts_landed, 16)
            pool.tensor_copy(ident_b[:, :], ident)
            for br in range(2):
                pool.tensor_copy(causal_b[:, br, :], consts[:, C_CAUSAL:C_CAUSAL + P])
            cm = consts[:, C_CMASK:C_CMASK + NT * NCP].rearrange("p (t n) -> p t n", t=NT)
            for t in range(NT):
                ins = pool.tensor_copy(cmask_b[:, t, :, :], cm[:, t, :].unsqueeze(1).to_broadcast([P, HEADS, NCP]))
            ins.then_inc(masks_ready, 1)
            pool.wait_ge(group_done, MIX0)
            pool.memset(blk_f, 0.0).then_inc(pads_zero, 1)

        @block.tensor
        def _(pe):
            mm = nc.tensor.matmul

            def group(c, i, per, hi, lo, k, banks, first, last, cols=TOK):
                pe.wait_ge(lo_ready, count(c + 1, i, per))
                s = c % SLOTS
                for kk in range(GK):
                    for t, bank in enumerate(banks):
                        o = ps[:, bank, :]
                        x_hi = hi[:, k + kk, t * P:t * P + P]
                        x_lo = lo[:, k + kk, t * P:t * P + P]
                        mm(o, x_hi, w_hi[:, s, kk, :], start=first and kk == 0, stop=False)
                        mm(o, x_hi, w_lo[:, s, kk, :], start=False, stop=False)
                        ins = mm(o, x_lo, w_hi[:, s, kk, :], start=False, stop=last and kk == GK - 1)
                ins.then_inc(group_done, 1)

            def job(c, n, hi, lo, pair, i=None, per=0, after={}, before={}, ks=None, banks=None):
                banks = banks or [2 * pair, 2 * pair + 1]
                for j in range(n):
                    for f in before.get(j, ()):
                        f()
                    k = GK * (ks[j] if ks else j)
                    group(c + j, i, per, hi, lo, k, banks, j == 0, j == n - 1)
                    for f in after.get(j, ()):
                        f()

            def to_bank(bank, n, i=None, per=0):
                if n:
                    pe.wait_ge(free[bank], count(n, i, per))

            def transposes(bank, pieces):
                for o, src in pieces:
                    ins = pe.transpose(ps[:, bank, o:o + P], src, ident)
                ins.then_inc(full[bank], 1)

            def x_transposes(which, n):
                if which == 0:
                    pe.wait_ge(x_landed[n], 16)
                else:
                    pe.wait_ge(resid_done, 2 * (NDC * (1 if which == 1 else 3) - NDC + n + 1))
                for b in range(2):
                    to_bank(4 + b, operand_use("x", which, b, n)[0])
                    transposes(4 + b, [(kk * TOK + t * P, x[:, t, (4 * n + 2 * b + kk) * P:][:, 0:P])
                                       for kk in range(2) for t in range(NT)])

            def x_operand(which, n):
                for b in range(2):
                    pe.wait_ge(free[4 + b], operand_use("x", which, b, n)[0] + 1)

            def gu_transposes(f, n, i=None):
                pe.wait_ge(gu_done, count(2 * (NFC * f + n + 1), i, 2))
                for b in range(2):
                    to_bank(4 + b, operand_use("gu", f, b, n)[0], i, 1)
                    transposes(4 + b, [(kk * TOK + t * P, gu[:, t, (2 * b + kk) * P:][:, 0:P])
                                       for kk in range(2) for t in range(NT)])

            def gu_operand(f, n):
                for b in range(2):
                    pe.wait_ge(free[4 + b], operand_use("gu", f, b, n)[0] + 1)

            def ffn(f):
                which = 0 if f == 0 else 2
                c = FFN0[f]
                before = {2 * n: [lambda n=n: x_operand(which, n)] for n in range(NDC)}
                after = {3: [lambda: x_transposes(2, NDC - 1)]} if f else {}
                job(c, JD, hT_hi, hT_lo, 0, after=after, before=before)
                c += JD
                with pe.Fori(0, NFC - 1) as i:
                    job(c, JD, hT_hi, hT_lo, 1, i, 2 * JD)
                    pe.wait_ge(silu_done, count(2 * (NFC * f + 1), i, 2))
                    job(c + JD, JD, hT_hi, hT_lo, 0, i, 2 * JD, after={3: [lambda: gu_transposes(f, 0, i)]})
                c += 2 * JD * (NFC - 1)
                job(c, JD, hT_hi, hT_lo, 1)
                c += JD
                pe.wait_ge(silu_done, 2 * NFC * (f + 1))
                for n in range(NDC):
                    if n == 0:
                        before = {0: [lambda: gu_operand(f, NFC - 2)], JF - 2: [lambda: gu_operand(f, NFC - 1)]}
                        after = {3: [lambda: gu_transposes(f, NFC - 1)]}
                    else:
                        before = {}
                        if f == 0:
                            after = {3: [lambda: x_transposes(1, n - 1)]}
                        else:
                            after = {3: [lambda: pe.wait_ge(resid_done, 2 * (3 * NDC + n))]}
                    job(c + JF * n, JF, guT_hi, guT_lo, n % 2, before=before, after=after)

            def q_transposes(n):
                bank, u = USE["q", n]
                if n == 0:
                    pe.wait_ge(q_roped, NT)
                to_bank(bank, u)
                transposes(bank, [(kk * TOK + t * P, p_q[:, t, (2 * n + kk) * P:][:, 0:P])
                                  for kk in range(2) for t in range(NT)])

            def kvd_transposes(n):
                bank, u = USE["kvd", n]
                pe.wait_ge(kvd_ready, NT)
                to_bank(bank, u)
                transposes(bank, [(kk * TOK + t * P, kvd[:, t, n // 2, 2 * (n % 2) + kk, :])
                                  for kk in range(2) for t in range(NT)])

            def gates():
                bank, u = USE["gates",]
                pe.wait_ge(gate_w_landed, 16)
                to_bank(bank, u)
                for t in range(NT):
                    for k in range(KD):
                        for n, part in enumerate((hT_hi, hT_lo)):
                            ins = mm(ps[:, bank, t * NG:t * NG + NG], part[:, k, t * P:t * P + P].bitcast(F32),
                                     w_gate[:, k, :], start=k == 0 and n == 0, stop=k == KD - 1 and n == 1)
                ins.then_inc(full[bank], 1)

            def kT_transposes(jp):
                bank, u = USE["kT", jp]
                pe.wait_ge(ks_roped, 2)
                to_bank(bank, u)
                transposes(bank, [(br * TOK + t * P, p_kv[:, t, br * CH + jp * P:][:, 0:P])
                                  for br in range(2) for t in range(NT)])

            def scores(m):
                t, h = divmod(m, HEADS)
                j, r = divmod(h, GRP)
                jp, par = divmod(j, 2)
                nk = (t + 1) * P
                rows_ = slice(par * HD, par * HD + HD)
                bank, u = USE["QK", m]
                if m == 0:
                    pe.wait_ge(masks_ready, 1)
                    for key in (("q", 2), ("q", 3), ("kT", 0), ("kT", 1)):
                        pe.wait_ge(free[USE[key][0]], USE[key][1] + 1)
                to_bank(bank, u)
                o = ps[:, bank, 0:2 * nk].rearrange("p (b n) -> p b n", b=2)
                mm(o, qT[rows_, jp * GRP + r, t * P:t * P + P], kT[rows_, jp, :, 0:nk], start=True, stop=False)
                mm(o[:, :, nk - P:nk], ident_b[:, :], causal_b[:, :, :], start=False, stop=True).then_inc(full[bank], 1)

            def prob_transposes(m):
                t = m // HEADS
                qk_bank, qk_u = USE["QK", m]
                bank, u = USE["PT", m]
                pe.wait_ge(free[qk_bank], qk_u + 1)
                to_bank(bank, u)
                transposes(bank, [(n * P, prob[:, m % 2, n * P:n * P + P]) for n in range(2 * (t + 1))])

            def weighted_values(m):
                t, h = divmod(m, HEADS)
                j, r = divmod(h, GRP)
                pe.wait_ge(free[4], USE["PT", m][1] + 1)
                bank, u = USE["O", m // GRP]
                if r == 0:
                    to_bank(bank, u)
                for br in range(2):
                    for kt in range(t + 1):
                        ins = mm(ps[:, bank, r * P + br * HD:][:, 0:HD],
                                 probT[:, m % 2, (br * (t + 1) + kt) * P:][:, 0:P],
                                 p_kv[:, kt, br * CH + KV * HD + j * HD:][:, 0:HD], start=kt == 0, stop=kt == t)
                if r == GRP - 1:
                    ins.then_inc(full[bank], 1)

            def conv_transposes(key):
                kind, n = key
                bank, u = USE[key]
                if kind == "cu":
                    pe.wait_ge(u_ready, 2 if n >= 2 else 4)
                    src = p_h
                else:
                    pe.wait_ge(proj_done, 2 * (9 if n >= 2 else 10))
                    src = p_b
                to_bank(bank, u)
                transposes(bank, [(kk * TOK + t * P, src[:, t, (2 * n + kk) * P:][:, 0:P])
                                  for kk in range(2) for t in range(NT)])

            def tick(m):
                if m >= 2:
                    weighted_values(m - 2)
                if 1 <= m <= 2 * HEADS:
                    prob_transposes(m - 1)
                if m < 2 * HEADS:
                    scores(m)
                if m in CONV_TICK:
                    conv_transposes(CONV_TICK[m])

            def conv_square_sum():
                bank, u = USE["css",]
                pe.wait_ge(ysq_ready, 4)
                to_bank(bank, u)
                for t in range(NT):
                    for c in range(CT):
                        ins = mm(ps[:, bank, t:t + 1], uT[:, c, t * P:t * P + P], ones, start=c == 0, stop=c == CT - 1)
                ins.then_inc(full[bank], 1)

            def hid_transposes():
                bank, u = USE["hidT",]
                pe.wait_ge(hid_ready, 1)
                to_bank(bank, u)
                transposes(bank, [(n * P, scr[:, n * P:n * P + P]) for n in range(4)])

            def compressed_kv():
                bank, u = USE["kcvc",]
                pe.wait_ge(free[USE["hidT",][0]], USE["hidT",][1] + 1)
                to_bank(bank, u)
                for f in range(2):
                    mm(ps[:, bank, 0:HD], w2k[:, f, :, :].rearrange("p a d -> p (a d)"), hidkT[:, f, :],
                       start=f == 0, stop=f == 1)
                for jp in range(2):
                    for f in range(2):
                        ins = mm(ps[:, bank, HD * (jp + 1):][:, 0:HD],
                                 hidvT[:, f, 2 * jp:2 * jp + 2, :, :].rearrange("p j h n -> p (j h n)"), w2v[:, f, :],
                                 start=f == 0, stop=f == 1)
                ins.then_inc(full[bank], 1)

            def compressed_scores(par):
                bank, u = USE["cs", par]
                pe.wait_ge(free[USE["kcvc",][0]], USE["kcvc",][1] + 1)
                to_bank(bank, u)
                half = HEADS // 2 * NCP
                mm(ps[:, bank, 0:NT * half].rearrange("p (t n) -> p t n", t=NT), ident_b[:, :],
                   cmask_b[:, :, 0:HEADS // 2, :].rearrange("p t h n -> p t (h n)"), start=True, stop=True,
                   skip_group_check=True)
                rows_ = slice(par * HD, par * HD + HD)
                for t in range(NT):
                    for q in range(HEADS // 2):
                        ins = mm(ps[:, bank, t * half + q * NCP:][:, 0:NCP], qT[rows_, q, t * P:t * P + P],
                                 kcT[rows_, 2 * (q // GRP) + par, :], start=False,
                                 stop=True, skip_group_check=True)
                ins.then_inc(full[bank], 1)

            def compressed_prob_transposes(t):
                bank, u = USE["pcT", t]
                pe.wait_ge(cexp_ready, 1)
                to_bank(bank, u)
                flat = pc[:, t, :, :].rearrange("p h n -> p (h n)")
                transposes(bank, [(n * P, flat[:, n * P:n * P + P]) for n in range(2)])

            def compressed_values(n):
                t, par = divmod(n, 2)
                rows_ = slice(par * HD, par * HD + HD)
                bank, u = USE["Oc", n]
                pe.wait_ge(free[USE["pcT", t][0]], USE["pcT", t][1] + 1)
                to_bank(bank, u)
                for jp in range(2):
                    ins = mm(ps[:, bank, jp * TOK:jp * TOK + TOK], pcT[rows_, t, jp, :],
                             vcb[rows_, jp, :, :].rearrange("p h d -> p (h d)"), start=True, stop=True)
                ins.then_inc(full[bank], 1)

            def att_transposes(n):
                pe.wait_ge(y_att_ready, 1)
                for b in range(2):
                    bank, u = USE["aT", n, b]
                    to_bank(bank, u)
                    transposes(bank, [(kk * TOK + t * P, y_att[:, t, (4 * n + 2 * b + kk) * P:][:, 0:P])
                                      for kk in range(2) for t in range(NT)])

            def mixer():
                after = {}

                def put(c, *fs):
                    after.setdefault(c, []).extend(fs)

                put(IN_JOB[0] + 3, lambda: x_transposes(1, NDC - 1))
                put(IN_JOB[4] + 2, lambda: q_transposes(0), lambda: q_transposes(1))
                put(IN_JOB[4] + 5, lambda: q_transposes(2), lambda: q_transposes(3))
                put(IN_JOB[5] + 2, lambda: kvd_transposes(0), lambda: kvd_transposes(1))
                put(IN_JOB[5] + 5, lambda: kvd_transposes(2), lambda: kvd_transposes(3))
                put(IN_JOB[6] + 1, gates)
                put(IN_JOB[6] + 6, lambda: kT_transposes(0), lambda: kT_transposes(1))
                for m in range(2 * HEADS + 2):
                    put(IN_JOB[7] + 1 + m, lambda m=m: tick(m))
                put(CMP_JOB + 4, lambda: conv_transposes(("cu", 0)), lambda: conv_transposes(("cu", 1)))
                put(CMP_JOB + 6, lambda: conv_transposes(("cb", 0)), lambda: conv_transposes(("cb", 1)))
                o = OUT_JOB[0]
                put(o + 1, conv_square_sum)
                put(o + 3, hid_transposes)
                put(o + 5, compressed_kv)
                put(o + 7, lambda: compressed_scores(0), lambda: compressed_scores(1))
                put(o + 9, lambda: compressed_prob_transposes(0), lambda: compressed_prob_transposes(1))
                put(o + 11, lambda: compressed_values(0), lambda: compressed_values(1))
                put(o + 12, lambda: compressed_values(2), lambda: compressed_values(3))
                put(o + 15, lambda: att_transposes(0), lambda: att_transposes(1))
                local = lambda c, n: {j: after[c + j] for j in range(n) if c + j in after}

                for jb, c in enumerate(IN_JOB):
                    if jb >= 2:
                        pe.wait_ge(proj_done, 2 * (jb - 1))
                    before = {2 * n: [lambda n=n: x_operand(1, n)] for n in range(NDC)} if jb == 0 else {}
                    job(c, JD, hT_hi, hT_lo, jb % 2, after=local(c, JD), before=before)
                pe.wait_ge(proj_done, 2 * 10)
                pe.wait_ge(blk_lo_ready, 1)
                job(CMP_JOB, JD, blk_hi, blk_lo, 1, after=local(CMP_JOB, JD), banks=[2])
                for n, c in enumerate(OUT_JOB):
                    if n == 0:
                        pe.wait_ge(u_ready, 4)
                    elif n == 1:
                        pe.wait_ge(gelu_in, 1)
                    else:
                        pe.wait_ge(resid_done, 2 * (NDC + n - 1))
                    if n < NDC:
                        before = {0: [lambda: pe.wait_ge(ycT_lo_ready, 4)], 2: [lambda: pe.wait_ge(ycT_lo_ready, 8)]}
                        job(c, JH, ycT_hi, ycT_lo, n % 2, after=local(c, JH), before=before, ks=CONV_K_ORDER)
                    else:
                        before = {}
                        if n == NDC:
                            before = {2 * q: [lambda q=q: [pe.wait_ge(free[4 + b], USE["aT", q, b][1] + 1)
                                                           for b in range(2)]] for q in range(2)}
                        aft = {2: [lambda n=n: x_transposes(2, n - NDC - 1)]} if n > NDC else {}
                        job(c, JH, aT_hi, aT_lo, n % 2, after=aft, before=before)

            pe.wait_ge(consts_landed, 16)
            pe.wait_ge(small_landed, 16 * 11)
            pe.transpose(ps[:, 6, 0:NVEC], vec_rows[0:NVEC, :], consts[0:NVEC, 0:NVEC]).then_inc(vecs_full, 1)
            for n in range(NDC):
                x_transposes(0, n)
            ffn(0)
            mixer()
            ffn(1)

        @block.scalar
        def _(act):
            steps = [0]

            def seq(ins):
                ins.then_inc(act_step, 1)
                steps[0] += 1
                act.wait_ge(act_step, steps[0])

            act.dma_start(consts[:, :], a["shape_consts"]).then_inc(consts_landed, 16)
            small = [(V_FFN1, KD, a["ffn1_norm"].rearrange("l (k p) -> (l k) p", p=P)),
                     (V_MIX, KD, a["mix_norm"].rearrange("l (k p) -> (l k) p", p=P)),
                     (V_FFN2, KD, a["ffn2_norm"].rearrange("l (k p) -> (l k) p", p=P)),
                     (V_CONVW, 3 * CT, a["conv_w"].rearrange("l w (k p) -> (l w k) p", p=P)),
                     (V_GC, CT, a["conv_out_norm"].rearrange("l (k p) -> (l k) p", p=P)),
                     (V_GA, CT, a["attn_out_norm"].rearrange("l (k p) -> (l k) p", p=P)),
                     (V_PEK, KD, a["cmp_k_pe"].rearrange("l (k w) d -> (l k) (w d)", w=2)),
                     (V_PEV, KD, a["cmp_v_pe"].rearrange("l (k w) d -> (l k) (w d)", w=2))]
            for row, n, src in small:
                act.dma_start(vec_rows[row:row + n, :], src).then_inc(small_landed, 16)
            for half in range(2):
                act.dma_start(w2k[:, :, half, :], w2[0]).then_inc(small_landed, 16)
            act.dma_start(w2v[:, :, :], w2[1]).then_inc(small_landed, 16)

            def hi(c, i=None, per=0):
                act.wait_ge(landed[c % SLOTS], landed_value(c, i, per))
                if c >= SLOTS:
                    act.wait_ge(group_done, count(c - SLOTS + 1, i, per))
                act.activation(w_hi[:, c % SLOTS, :, :], raw[:, c % SLOTS, :, :], ACT.Copy).then_inc(hi_ready, 1)

            def job(c, n, i=None, per=0, after={}):
                for j in range(n):
                    hi(c + j, i, per)
                    for f in after.get(j, ()):
                        f()

            def scaled_operand(dst, tile0, vec0, banks):
                for b, (bank, n) in enumerate(banks):
                    act.wait_ge(full[bank], n + 1)
                    for kk in range(2):
                        k = tile0 + 2 * b + kk
                        ins = act.activation(dst[:, k, :], ps[:, bank, kk * TOK:kk * TOK + TOK], ACT.Copy,
                                             scale=vecs[:, vec0 + k:vec0 + k + 1])
                    ins.then_inc(operand_hi, 1)

            def x_operand(which, n):
                vec0 = (V_FFN1, V_MIX, V_FFN2)[which]
                scaled_operand(hT_hi, 4 * n, vec0, [(4 + b, operand_use("x", which, b, n)[0]) for b in range(2)])

            def square(phase, n, src_ready):
                src_ready()
                for t in range(NT):
                    ins = act.activation(junk[:, t * CH:t * CH + CH], x[:, t, n * CH:n * CH + CH], ACT.Square,
                                         accum_out=ssq[:, phase, t, n:n + 1])
                    seq(ins)
                act.sem_inc(ssq_done, 1)

            def x_square(phase, n, resid):
                square(phase, n, lambda: act.wait_ge(resid_done, resid))

            def root(phase):
                act.wait_ge(var_done, phase + 1)
                act.activation(var[:, phase, :], var[:, phase, :], ACT.Sqrt).then_inc(root_done, 1)

            def silu(f, n, done, i=None):
                act.wait_ge(group_done, count(done, i, 2 * JD))
                if n or i is not None or f:
                    prev = NFC * f + n - 1
                    base = operand_use("gu", f, 0, n)[0], operand_use("gu", f, 1, n)[0]
                    for b in range(2):
                        act.wait_ge(full[4 + b], count(base[b], i, 1))
                else:
                    pass
                if n == 0 and i is None:
                    act.wait_ge(rs_done, (RS_FFN2 if f else RS_FFN1) + 1)
                for t in range(NT):
                    act.activation(gu[:, t, :], ps[:, t, :], ACT.Silu,
                                   scale=rs[:, RS_FFN2 if f else RS_FFN1, t:t + 1]).then_inc(silu_done, 1)

            def gu_operand(f, n, i=None):
                for b in range(2):
                    act.wait_ge(full[4 + b], count(operand_use("gu", f, b, n)[0] + 1, i, 1))
                    k = 4 * n + 2 * b
                    dst = guT_hi[:, k:k + 2, :] if i is None else guT_hi[:, bass.ds(i * 4 + k, 2), :]
                    act.activation(dst, ps[:, 4 + b, :].rearrange("p (k t) -> p k t", k=2),
                                   ACT.Copy).then_inc(operand_hi, 1)

            def ffn(f):
                c = FFN0[f]
                phase = RS_FFN2 if f else RS_FFN1
                if f == 0:
                    after = {3: [lambda: root(RS_FFN1)]}
                else:
                    after = {1: [lambda: x_square(RS_FFN2, NDC - 1, 6 * NDC)],
                             4: [lambda: root(RS_FFN2)], 5: [lambda: x_operand(2, NDC - 1)]}
                job(c, JD, after=after)
                c += JD
                with act.Fori(0, NFC - 1) as i:
                    job(c, JD, i, 2 * JD, after={1: [lambda: silu_loop(f, c, i)]})
                    job(c + JD, JD, i, 2 * JD, after={5: [lambda: gu_operand(f, 0, i)]})
                c += 2 * JD * (NFC - 1)
                job(c, JD, after={1: [lambda: silu(f, NFC - 1, c)]})
                c += JD
                for n in range(NDC):
                    if n == 0:
                        after = {5: [lambda: gu_operand(f, NFC - 1)]}
                    elif f == 0:
                        after = {3: [lambda: x_square(RS_MIX, n - 1, 2 * n)], 5: [lambda: x_operand(1, n - 1)]}
                    else:
                        after = {3: [lambda: x_square(RS_FINAL, n - 1, 2 * (3 * NDC + n))]}
                    job(c + JF * n, JF, after=after)

            def silu_loop(f, c, i):
                act.wait_ge(group_done, count(c, i, 2 * JD))
                act.wait_ge(rs_done, (RS_FFN2 if f else RS_FFN1) + 1)
                for b in range(2):
                    base = operand_use("gu", f, b, 0)[0]
                    act.wait_ge(full[4 + b], count(base, i, 1))
                for t in range(NT):
                    act.activation(gu[:, t, :], ps[:, t, :], ACT.Silu,
                                   scale=rs[:, RS_FFN2 if f else RS_FFN1, t:t + 1]).then_inc(silu_done, 1)

            def projected(jb):
                act.wait_ge(group_done, IN_JOB[jb] + JD)
                if jb == 0:
                    act.wait_ge(rs_done, RS_MIX + 1)
                for t in range(NT):
                    src = ps[:, 2 * (jb % 2) + t, :]
                    if jb == 0:
                        dst = p_cc[:, t, :]
                    elif jb in (1, 2):
                        dst = p_q[:, t, (jb - 1) * CH:jb * CH].rearrange("p (r two d) -> p two r d", r=GRP, two=2)
                        src = src.rearrange("p (two r d) -> p two r d", r=GRP, two=2)
                    elif jb == 3:
                        dst = p_kvc[:, t, :]
                    elif jb in (4, 5):
                        dst = p_kv[:, t, (jb - 4) * CH:(jb - 3) * CH]
                    elif jb in (6, 7):
                        dst = p_h[:, t, (jb - 6) * CH:(jb - 5) * CH]
                    else:
                        half = 9 - jb
                        dst = p_b[:, t, half * CH:half * CH + CH]
                    act.activation(dst, src, ACT.Copy, scale=rs[:, RS_MIX, t:t + 1]).then_inc(proj_done, 1)

            def q_operand(n):
                bank, u = USE["q", n]
                act.wait_ge(full[bank], u + 1)
                act.activation(qT[:, 2 * n:2 * n + 2, :], ps[:, bank, :].rearrange("p (k t) -> p k t", k=2),
                               ACT.Copy, scale=-HD ** -0.5).then_inc(free[bank], 1)

            def kT2_operand(n):
                bank, u = USE["kvd", n]
                v, j0 = n // 2, 2 * (n % 2)
                act.wait_ge(full[bank], u + 1)
                src = ps[:, bank, :].rearrange("p (j t) -> p j t", j=2)
                act.activation(kT2[0:HD, v, j0:j0 + 2, :], src[0:HD, :, :], ACT.Copy)
                act.activation(kT2[HD:P, v, j0:j0 + 2, 0:TOK - 1], src[HD:P, :, 1:TOK],
                               ACT.Copy).then_inc(free[bank], 1)

            def kT_operand(jp):
                bank, u = USE["kT", jp]
                act.wait_ge(full[bank], u + 1)
                act.activation(kT[:, jp, :, :], ps[:, bank, :].rearrange("p (b t) -> p b t", b=2),
                               ACT.Copy).then_inc(free[bank], 1)

            def blocks_hi():
                act.wait_ge(blk_ready, 1)
                act.activation(blk_hi[:, :, :], blk_f, ACT.Copy).then_inc(blk_hi_ready, 1)

            def gate_exp():
                act.wait_ge(gates_scaled, 1)
                act.activation(den[:, :, :, :], den[:, :, :, :], ACT.Exp, scale=-1.0).then_inc(gates_exp, 1)

            def exps(m):
                t = m // HEADS
                nk = (t + 1) * P
                bank, u = USE["QK", m]
                act.wait_ge(mins_ready, m + 1)
                if m >= 2:
                    act.wait_ge(full[4], USE["PT", m - 2][1] + 1)
                for br in range(2):
                    ins = act.activation(prob[:, m % 2, br * nk:br * nk + nk], ps[:, bank, br * nk:br * nk + nk],
                                         ACT.Exp, bias=mins[:, m, br:br + 1], scale=-1.0,
                                         accum_out=sums[:, m, br:br + 1])
                ins.then_inc(free[bank], 1)

            def u_operand(n):
                bank, u = USE["cu", n]
                act.wait_ge(full[bank], u + 1)
                if n == 2:
                    act.wait_ge(blk_ready, 1)
                act.activation(uT[:, 2 * n:2 * n + 2, 2:TOK + 2], ps[:, bank, :].rearrange("p (k t) -> p k t", k=2),
                               ACT.Copy).then_inc(free[bank], 1)

            def conv_squares(n):
                act.wait_ge(conv_ready, {2: 1, 3: 2, 0: 3, 1: 4}[n])
                act.activation(uT[:, 2 * n:2 * n + 2, 0:TOK], cv(2 * n, 2).rearrange("p (k t) -> p k t", k=2),
                               ACT.Square).then_inc(ysq_ready, 1)

            def conv_operand(n):
                for c in (2 * n, 2 * n + 1):
                    act.activation(ycT_hi[:, c, :], cv(c), ACT.Copy,
                                   scale=vecs[:, V_GC + c:V_GC + c + 1]).then_inc(ycT_hi_ready, 1)

            def gelu():
                act.wait_ge(gelu_in, 2)
                act.activation(scr[:, CH:2 * CH], scr[:, CH:2 * CH], ACT.Exp,
                               scale=-1.5957691216057308).then_inc(gelu_exp, 1)

            def compressed_exp():
                act.wait_ge(cdiff_ready, 2)
                act.activation(pc[:, :, :, :], pc[:, :, :, :], ACT.Exp, scale=-1.0).then_inc(cexp_ready, 1)

            def compressed_operand(t):
                bank, u = USE["pcT", t]
                act.wait_ge(full[bank], u + 1)
                act.activation(pcT[:, t, :, :], ps[:, bank, 0:TOK].rearrange("p (k t) -> p k t", k=2),
                               ACT.Copy).then_inc(free[bank], 1)

            def att_square():
                act.wait_ge(y_att_ready, 1)
                for t in range(NT):
                    seq(act.activation(junk[:, :], y_att[:, t, :], ACT.Square, accum_out=ssq[:, RS_ATT, t, 0:1]))
                act.sem_inc(ssq_done, 1)

            def att_operand(n):
                scaled_operand(aT_hi, 4 * n, V_GA, [USE["aT", n, b] for b in range(2)])

            def mixer():
                after = {}

                def put(c, *fs):
                    after.setdefault(c, []).extend(fs)

                put(IN_JOB[0] + 1, lambda: x_square(RS_MIX, NDC - 1, 2 * NDC))
                put(IN_JOB[0] + 4, lambda: root(RS_MIX))
                put(IN_JOB[0] + 5, lambda: x_operand(1, NDC - 1))
                for jb in range(10):
                    put(IN_JOB[jb] + JD + 1, lambda jb=jb: projected(jb))
                put(IN_JOB[4] + 4, lambda: q_operand(0), lambda: q_operand(1))
                put(IN_JOB[4] + 7, lambda: q_operand(2), lambda: q_operand(3))
                put(IN_JOB[5] + 4, lambda: kT2_operand(0), lambda: kT2_operand(1))
                put(IN_JOB[5] + 7, lambda: kT2_operand(2), lambda: kT2_operand(3))
                put(IN_JOB[6] + 6, gate_exp)
                put(IN_JOB[6] + 8, lambda: kT_operand(0), lambda: kT_operand(1))
                put(IN_JOB[7] + 2, blocks_hi)
                for m in range(2 * HEADS):
                    put(IN_JOB[7] + 3 + m, lambda m=m: exps(m))
                    if m in CONV_TICK and CONV_TICK[m][0] == "cu":
                        put(IN_JOB[7] + 3 + m, lambda n=CONV_TICK[m][1]: u_operand(n))
                for m, key in CONV_TICK.items():
                    if key[0] == "cb":
                        put(IN_JOB[7] + 4 + m, lambda n=key[1]: conv_squares(n), lambda n=key[1]: conv_operand(n))
                put(CMP_JOB + 6, lambda: u_operand(0), lambda: u_operand(1))
                o = OUT_JOB[0]
                put(o, lambda: conv_squares(0), lambda: conv_operand(0), lambda: conv_squares(1),
                    lambda: conv_operand(1))
                put(o + 2, gelu)
                put(o + 4, lambda: root(RS_CONV))
                put(o + 9, compressed_exp)
                put(o + 11, lambda: compressed_operand(0), lambda: compressed_operand(1))
                put(o + 15, att_square)
                put(o + 17, lambda: att_operand(0), lambda: att_operand(1))
                put(o + 18, lambda: root(RS_ATT))
                for n in range(NDC - 1):
                    put(OUT_JOB[NDC + n + 1] + 2, lambda n=n: x_square(RS_FFN2, n, 2 * (2 * NDC + n + 1)))
                    put(OUT_JOB[NDC + n + 2] + 0 if n < 2 else FFN0[1], lambda n=n: x_operand(2, n))
                return after

            act.wait_ge(vecs_full, 1)
            act.activation(vecs[:, :], ps[:, 6, 0:NVEC], ACT.Copy).then_inc(vecs_ready, 1)
            act.wait_ge(vecs_ready, 1)
            for n in range(NDC):
                x_operand(0, n)
            for n in range(NDC):
                square(RS_FFN1, n, lambda n=n: act.wait_ge(x_landed[n], 16))
            ffn(0)
            mix_after = mixer()
            for c in range(MIX0, FFN0[1]):
                hi(c)
                for f in mix_after.pop(c, ()):
                    f()
            for c in sorted(mix_after):
                for f in mix_after[c]:
                    f()
            ffn(1)
            x_square(RS_FINAL, NDC - 1, 8 * NDC)
            root(RS_FINAL)

        @block.vector
        def _(dve):
            steps = [0]

            def seq(ins):
                ins.then_inc(dve_step, 1)
                steps[0] += 1
                dve.wait_ge(dve_step, steps[0])

            tt = nc.vector.tensor_tensor
            stt = nc.vector.scalar_tensor_tensor

            def lo(c, i=None, per=0):
                dve.wait_ge(hi_ready, count(c + 1, i, per))
                s = c % SLOTS
                tt(w_lo[:, s, :, :], raw[:, s, :, :], w_hi[:, s, :, :].bitcast(F32),
                   ALU.subtract).then_inc(lo_ready, 1)

            def job(c, n, i=None, per=0, after={}):
                for j in range(n):
                    lo(c + j, i, per)
                    for f in after.get(j, ()):
                        f()

            OP_X = {0: 0, 1: 2 * (NDC + NFC), 2: 2 * (NDC + NFC + NDC + 2)}
            OP_GU = [2 * NDC, OP_X[2] + 2 * NDC]
            OP_ATT = 2 * (NDC + NFC + NDC)

            def scaled_operand(hi_t, lo_t, tile0, vec0, banks, op0):
                for b, bank in enumerate(banks):
                    dve.wait_ge(operand_hi, op0 + b + 1)
                    for kk in range(2):
                        k = tile0 + 2 * b + kk
                        ins = stt(out=lo_t[:, k, :], in0=ps[:, bank, kk * TOK:kk * TOK + TOK],
                                  scalar=vecs[:, vec0 + k:vec0 + k + 1], in1=hi_t[:, k, :].bitcast(F32),
                                  op0=ALU.mult, op1=ALU.subtract)
                    ins.then_inc(free[bank], 1)

            def x_operand(which, n):
                vec0 = (V_FFN1, V_MIX, V_FFN2)[which]
                scaled_operand(hT_hi, hT_lo, 4 * n, vec0, (4, 5), OP_X[which] + 2 * n)

            def variance(phase, width, ssq_count, cols=NDC):
                dve.wait_ge(ssq_done, ssq_count)
                if cols > 1:
                    seq(nc.vector.tensor_reduce(var[:, phase, :], ssq[:, phase, :, 0:cols], axis=AX.X, op=ALU.add))
                    src = var[:, phase, :]
                else:
                    src = ssq[:, phase, :, 0]
                nc.vector.tensor_scalar(var[:, phase, :], src, 1.0 / width, EPS, ALU.mult,
                                        ALU.add).then_inc(var_done, 1)

            def inverse_root(phase):
                dve.wait_ge(root_done, phase + 1)
                nc.vector.reciprocal(rs[:, phase, :], var[:, phase, :]).then_inc(rs_done, 1)
                dve.wait_ge(rs_done, phase + 1)

            def up(f, n, done, i=None):
                dve.wait_ge(group_done, count(done, i, 2 * JD))
                dve.wait_ge(silu_done, count(2 * (NFC * f + n + 1), i, 2))
                for t in range(NT):
                    stt(out=gu[:, t, :], in0=ps[:, 2 + t, :], scalar=rs[:, RS_FFN2 if f else RS_FFN1, t:t + 1],
                        in1=gu[:, t, :], op0=ALU.mult, op1=ALU.mult).then_inc(gu_done, 1)

            def gu_operand(f, n, i=None):
                for b in range(2):
                    dve.wait_ge(operand_hi, count(OP_GU[f] + 2 * n + b + 1, i, 2))
                    k = 4 * n + 2 * b
                    sl = slice(k, k + 2) if i is None else bass.ds(i * 4 + k, 2)
                    tt(guT_lo[:, sl, :], ps[:, 4 + b, :].rearrange("p (k t) -> p k t", k=2),
                       guT_hi[:, sl, :].bitcast(F32), ALU.subtract).then_inc(free[4 + b], 1)

            def residual(n, done, pair, scale):
                dve.wait_ge(group_done, done)
                for t in range(NT):
                    xs = x[:, t, n * CH:n * CH + CH]
                    stt(out=xs, in0=ps[:, 2 * pair + t, :], scalar=scale(t), in1=xs,
                        op0=ALU.mult, op1=ALU.add).then_inc(resid_done, 1)

            half = lambda t: 0.5

            def ffn(f):
                c = FFN0[f]
                if f == 0:
                    after = {3: [lambda: variance(RS_FFN1, DM, NDC)], 5: [lambda: inverse_root(RS_FFN1)]}
                else:
                    after = {1: [lambda: residual(NDC - 1, FFN0[1], 1, att_scale)],
                             3: [lambda: variance(RS_FFN2, DM, 3 * NDC + 1)],
                             5: [lambda: x_operand(2, NDC - 1)], 6: [lambda: inverse_root(RS_FFN2)]}
                job(c, JD, after=after)
                c += JD
                with dve.Fori(0, NFC - 1) as i:
                    job(c, JD, i, 2 * JD)
                    job(c + JD, JD, i, 2 * JD, after={1: [lambda: up(f, 0, c + JD, i)],
                                                      5: [lambda: gu_operand(f, 0, i)]})
                c += 2 * JD * (NFC - 1)
                job(c, JD)
                c += JD
                for n in range(NDC):
                    if n == 0:
                        after = {1: [lambda: up(f, NFC - 1, c)], 5: [lambda: gu_operand(f, NFC - 1)]}
                    else:
                        after = {1: [lambda: residual(n - 1, c + JF * n, (n - 1) % 2, half)]}
                        if f == 0:
                            after[5] = [lambda: x_operand(1, n - 1)]
                    job(c + JF * n, JF, after=after)

            def rope(x_lo, x_hi, x_all, s_lo, s_hi, s_all, cos, sin, shape_half, shape_all, last_out=None,
                     last_in=None):
                seq(tt(s_lo, x_hi, sin[0].to_broadcast(shape_half), ALU.mult))
                seq(tt(s_hi, x_lo, sin[1].to_broadcast(shape_half), ALU.mult))
                seq(tt(x_all, x_all, cos.to_broadcast(shape_all), ALU.mult))
                if last_out is None:
                    return tt(x_all, x_all, s_all, ALU.add)
                return tt(last_out, last_in(x_all), last_in(s_all), ALU.add)

            def rope_q(t):
                if t == 0:
                    dve.wait_ge(proj_done, 2 * 3)
                v = p_q[:, t, :].rearrange("p (h d) -> p h d", d=HD)
                s = scr[:, :].rearrange("p (h d) -> p h d", d=HD)
                sh, sa = [P, HEADS, HD // 2], [P, HEADS, HD]
                sin = [sin_t[:, t, 0:HD // 2].unsqueeze(1), sin_t[:, t, HD // 2:HD].unsqueeze(1)]
                seq_ins = rope(v[:, :, 0:HD // 2], v[:, :, HD // 2:HD], v, s[:, :, 0:HD // 2], s[:, :, HD // 2:HD], s,
                               cos_t[:, t, :].unsqueeze(1), sin, sh, sa)
                seq_ins.then_inc(q_roped, 1)
                dve.wait_ge(q_roped, t + 1)

            def rope_kc(t):
                if t == 0:
                    dve.wait_ge(proj_done, 2 * 4)
                v = p_kvc[:, t, 0:KV * HD].rearrange("p (h d) -> p h d", d=HD)
                s = scr[:, 0:KV * HD].rearrange("p (h d) -> p h d", d=HD)
                sh, sa = [P, KV, HD // 2], [P, KV, HD]
                sin = [sin_t[:, t, 0:HD // 2].unsqueeze(1), sin_t[:, t, HD // 2:HD].unsqueeze(1)]
                twice = lambda u: u.unsqueeze(2).to_broadcast([P, KV, 2, HD])
                dst = kvd[:, t, :, :, :].rearrange("p v j (a d) -> p v j a d", a=2)
                rope(v[:, :, 0:HD // 2], v[:, :, HD // 2:HD], v, s[:, :, 0:HD // 2], s[:, :, HD // 2:HD], s,
                     cos_t[:, t, :].unsqueeze(1), sin, sh, sa, dst[:, 0, :, :, :], twice)
                vv = p_kvc[:, t, KV * HD:2 * KV * HD].rearrange("p (h d) -> p h d", d=HD)
                nc.vector.tensor_copy(dst[:, 1, :, :, :], twice(vv)).then_inc(kvd_ready, 1)
                dve.wait_ge(kvd_ready, t + 1)

            def rope_ks(br, t):
                if t == 0:
                    dve.wait_ge(proj_done, 2 * (5 + br))
                v = p_kv[:, t, br * CH:br * CH + KV * HD].rearrange("p (h d) -> p h d", d=HD)
                s = scr[:, 0:KV * HD].rearrange("p (h d) -> p h d", d=HD)
                sh, sa = [P, KV, HD // 2], [P, KV, HD]
                sin = [sin_t[:, t, 0:HD // 2].unsqueeze(1), sin_t[:, t, HD // 2:HD].unsqueeze(1)]
                ins = rope(v[:, :, 0:HD // 2], v[:, :, HD // 2:HD], v, s[:, :, 0:HD // 2], s[:, :, HD // 2:HD], s,
                           cos_t[:, t, :].unsqueeze(1), sin, sh, sa)
                if t:
                    ins.then_inc(ks_roped, 1)
                    dve.wait_ge(ks_roped, br + 1)
                else:
                    seq(ins)

            def blocks():
                for n in range(4):
                    bank, u = USE["kvd", n]
                    dve.wait_ge(free[bank], u + 1)
                dve.wait_ge(pads_zero, 1)
                for v in range(2):
                    toks = kT2[:, v, :, :].rearrange("p j (n s w) -> p s j n w", s=8, w=2)
                    for h in range(2):
                        pe_col = (V_PEK, V_PEV)[v] + 8 * h
                        o = blk_f[:, 8 * h:8 * h + 8, v * KV * NCP:(v + 1) * KV * NCP].rearrange(
                            "p k (j n) -> p k j n", j=KV)[:, :, :, 0:NCMP]
                        pos = vecs[:, pe_col:pe_col + 8].unsqueeze(2).unsqueeze(3).to_broadcast([P, 8, KV, NCMP])
                        ins = tt(o, toks[:, :, :, h:h + NCMP, 0], pos, ALU.add)
                ins.then_inc(blk_ready, 1)

            def blocks_lo():
                dve.wait_ge(blk_hi_ready, 1)
                tt(blk_lo[:, :, :], blk_f, blk_hi[:, :, :].bitcast(F32), ALU.subtract).then_inc(blk_lo_ready, 1)

            def gates_in():
                bank, u = USE["gates",]
                dve.wait_ge(full[bank], u + 1)
                for t in range(NT):
                    ins = nc.vector.tensor_scalar(den[:, t, :, :].rearrange("p h g -> p (h g)"),
                                                  ps[:, bank, t * NG:t * NG + NG], rs[:, RS_MIX, t:t + 1], None,
                                                  ALU.mult)
                ins.then_inc(gates_scaled, 1)
                dve.wait_ge(gates_scaled, 1)
                dve.sem_inc(free[bank], 1)

            def gates_den():
                dve.wait_ge(gates_exp, 1)
                seq(nc.vector.tensor_scalar(den[:, :, :, :], den[:, :, :, :], 1.0, None, ALU.add))

            def score_min(m):
                t = m // HEADS
                nk = (t + 1) * P
                bank, u = USE["QK", m]
                dve.wait_ge(full[bank], u + 1)
                nc.vector.tensor_reduce(mins[:, m, :], ps[:, bank, 0:2 * nk].rearrange("p (b n) -> p b n", b=2),
                                        axis=AX.X, op=ALU.min).then_inc(mins_ready, 1)

            def prob_operand(m):
                t = m // HEADS
                n = 2 * (t + 1) * P
                bank, u = USE["PT", m]
                dve.wait_ge(full[bank], u + 1)
                nc.vector.tensor_copy(probT[:, m % 2, 0:n], ps[:, bank, 0:n]).then_inc(free[bank], 1)

            def weighted(n):
                t, j = divmod(n, KV)
                m = GRP * n
                bank, u = USE["O", n]
                dve.wait_ge(full[bank], u + 1)
                seq(tt(coef[:, :, :], den[:, t, GRP * j:GRP * j + GRP, 1:3], sums[:, m:m + GRP, :], ALU.mult))
                seq(nc.vector.reciprocal(coef[:, :, :], coef[:, :, :]))
                s = scr[:, 0:CH].rearrange("p (h b d) -> p h b d", h=GRP, b=2)
                o = ps[:, bank, :].rearrange("p (h b d) -> p h b d", h=GRP, b=2)
                tt(s, o, coef[:, :, :].unsqueeze(3).to_broadcast([P, GRP, 2, HD]), ALU.mult).then_inc(free[bank], 1)
                dve.wait_ge(free[bank], u + 1)
                seq(tt(y_att[:, t, j * TOK:(j + 1) * TOK].rearrange("p (h d) -> p h d", h=GRP),
                       s[:, :, 0, :], s[:, :, 1, :], ALU.add))

            def conv_input_upper():
                dve.wait_ge(proj_done, 2 * 8)
                for t in range(NT):
                    xs = p_h[:, t, CH:2 * CH]
                    tt(xs, p_cc[:, t, :], xs, ALU.mult).then_inc(u_ready, 1)

            def conv_input_lower():
                dve.wait_ge(group_done, IN_JOB[10] + JD)
                for t in range(NT):
                    xs = p_h[:, t, 0:CH]
                    stt(out=xs, in0=ps[:, t, :], scalar=rs[:, RS_MIX, t:t + 1], in1=xs, op0=ALU.mult,
                        op1=ALU.mult).then_inc(u_ready, 1)

            def conv_taps(tiles):
                for n in (tiles[0] // 2, tiles[-1] // 2):
                    bank, u = USE["cu", n]
                    dve.wait_ge(free[bank], u + 1)
                w = lambda tap, c: vecs[:, V_CONVW + tap * CT + c:V_CONVW + tap * CT + c + 1]
                if tiles[0] == 4:
                    seq(nc.vector.memset(uT[:, :, 0:2], 0.0))
                for tap in range(3):
                    for c in tiles:
                        if tap == 0:
                            ins = nc.vector.tensor_scalar(cv(c), uT[:, c, 0:TOK], w(0, c), None, ALU.mult)
                        else:
                            ins = stt(out=cv(c), in0=uT[:, c, tap:tap + TOK], scalar=w(tap, c), in1=cv(c),
                                      op0=ALU.mult, op1=ALU.add)
                    seq(ins)

            def conv_gate(n):
                bank, u = USE["cb", n]
                dve.wait_ge(full[bank], u + 1)
                tt(cv(2 * n, 2), ps[:, bank, :], cv(2 * n, 2), ALU.mult).then_inc(conv_ready, 1)
                dve.wait_ge(conv_ready, {2: 1, 3: 2, 0: 3, 1: 4}[n])
                dve.sem_inc(free[bank], 1)

            def conv_operand(n):
                for q, c in enumerate((2 * n, 2 * n + 1)):
                    dve.wait_ge(ycT_hi_ready, {2: 0, 3: 2, 0: 4, 1: 6}[n] + q + 1)
                    stt(out=ycT_lo[:, c, :], in0=cv(c), scalar=vecs[:, V_GC + c:V_GC + c + 1],
                        in1=ycT_hi[:, c, :].bitcast(F32), op0=ALU.mult, op1=ALU.subtract).then_inc(ycT_lo_ready, 1)

            def conv_variance():
                bank, u = USE["css",]
                dve.wait_ge(full[bank], u + 1)
                nc.vector.tensor_scalar(var[:, RS_CONV, :], ps[:, bank, 0:NT], 1.0 / CONV, EPS, ALU.mult,
                                        ALU.add).then_inc(var_done, 1)
                dve.wait_ge(var_done, RS_CONV + 1)
                dve.sem_inc(free[bank], 1)

            hx, hq = scr[:, 0:CH], scr[:, CH:2 * CH]

            def gelu_in_():
                dve.wait_ge(group_done, CMP_JOB + JD)
                nc.vector.tensor_copy(hx, ps[:, 2, :]).then_inc(gelu_in, 1)
                dve.wait_ge(gelu_in, 1)
                seq(tt(hq, hx, hx, ALU.mult))
                seq(nc.vector.tensor_scalar(hq, hq, 0.044715, 1.0, ALU.mult, ALU.add))
                tt(hq, hq, hx, ALU.mult).then_inc(gelu_in, 1)

            def gelu_out():
                dve.wait_ge(gelu_exp, 1)
                seq(nc.vector.tensor_scalar(hq, hq, 1.0, None, ALU.add))
                seq(nc.vector.reciprocal(hq, hq))
                tt(hx, hx, hq, ALU.mult).then_inc(hid_ready, 1)

            def hidden_operand():
                bank, u = USE["hidT",]
                dve.wait_ge(full[bank], u + 1)
                src = ps[:, bank, :].rearrange("p (f m) -> p f m", f=4)
                nc.vector.tensor_copy(hidkT[:, :, :], src[:, 0:2, 0:KV * NCP])
                for f in range(2):
                    v = src[:, 2 + f, KV * NCP:2 * KV * NCP].rearrange("p (j n) -> p j n", j=KV)
                    ins = nc.vector.tensor_copy(hidvT[:, f, :, :, :], v.unsqueeze(2).to_broadcast([P, KV, GRP, NCP]))
                ins.then_inc(free[bank], 1)

            def compressed_operands():
                bank, u = USE["kcvc",]
                dve.wait_ge(full[bank], u + 1)
                nc.vector.tensor_copy(kcT[:, :, :].rearrange("p j n -> p (j n)"), ps[:, bank, 0:KV * NCP])
                sel = consts[:, C_BMASK:C_BMASK + GRP].unsqueeze(2).to_broadcast([P, GRP, HD])
                for jp in range(2):
                    v = ps[:, bank, HD * (jp + 1):][:, 0:HD]
                    ins = tt(vcb[:, jp, :, :], v.unsqueeze(1).to_broadcast([P, GRP, HD]), sel, ALU.mult)
                ins.then_inc(free[bank], 1)

            def compressed_min(par):
                bank, u = USE["cs", par]
                dve.wait_ge(full[bank], u + 1)
                s = ps[:, bank, 0:HEADS * NCP].rearrange("p (q r n) -> p q r n", q=4, r=GRP)
                lows = cmin[:, par, :].rearrange("p (q r) -> p q r", q=4)
                seq(nc.vector.tensor_reduce(lows, s, axis=AX.X, op=ALU.min))
                dst = pc[:, :, :, :].rearrange("p t (jp two r) n -> p two (t jp) r n", two=2, r=GRP)[:, par, :, :, :]
                tt(dst, s, lows.unsqueeze(3).to_broadcast([P, 4, GRP, NCP]), ALU.subtract).then_inc(cdiff_ready, 1)
                dve.wait_ge(cdiff_ready, par + 1)
                dve.sem_inc(free[bank], 1)

            def compressed_coef(t):
                dve.wait_ge(cexp_ready, 1)
                seq(nc.vector.tensor_reduce(csum[:, t, :], pc[:, t, :, :], axis=AX.X, op=ALU.add))
                seq(tt(csum[:, t, :], csum[:, t, :], den[:, t, :, 0], ALU.mult))
                seq(nc.vector.reciprocal(csum[:, t, :], csum[:, t, :]))
                seq(nc.vector.tensor_scalar(csum[:, t, :], csum[:, t, :], consts[:, C_VALID + t:C_VALID + t + 1], None,
                                            ALU.mult))

            def compressed_weighted(n):
                t, par = divmod(n, 2)
                bank, u = USE["Oc", n]
                dve.wait_ge(full[bank], u + 1)
                s = scr[:, 0:CH].rearrange("p (jp r d) -> p jp r d", jp=2, d=HD)
                o = ps[:, bank, :].rearrange("p (jp r d) -> p jp r d", jp=2, d=HD)
                c = csum[:, t, :].rearrange("p (jp two r) -> p two jp r", two=2, r=GRP)[:, par, :, :]
                tt(s, o, c.unsqueeze(3).to_broadcast([P, 2, GRP, HD]), ALU.mult).then_inc(free[bank], 1)
                dve.wait_ge(free[bank], u + 1)
                y = y_att[:, t, :].rearrange("p (jp two m) -> p two jp m", two=2, m=GRP * HD)[:, par, :, :]
                ins = tt(y, y, scr[:, 0:CH].rearrange("p (jp m) -> p jp m", jp=2), ALU.add)
                if n == 3:
                    ins.then_inc(y_att_ready, 1)
                else:
                    seq(ins)

            def att_operand(n):
                scaled_operand(aT_hi, aT_lo, 4 * n, V_GA, (4, 5), OP_ATT + 2 * n)

            conv_scale = lambda t: rs[:, RS_CONV, t:t + 1]
            att_scale = lambda t: rs[:, RS_ATT, t:t + 1]

            def mixer():
                after = {}

                def put(c, *fs):
                    after.setdefault(c, []).extend(fs)

                put(IN_JOB[0] + 1, lambda: residual(NDC - 1, MIX0, 1, half))
                put(IN_JOB[0] + 3, lambda: variance(RS_MIX, DM, 2 * NDC))
                put(IN_JOB[0] + 5, lambda: x_operand(1, NDC - 1))
                put(IN_JOB[0] + 6, lambda: inverse_root(RS_MIX))
                put(IN_JOB[3] + 3, lambda: rope_q(0))
                put(IN_JOB[3] + 6, lambda: rope_q(1))
                put(IN_JOB[4] + 3, lambda: rope_kc(0))
                put(IN_JOB[4] + 5, lambda: rope_kc(1))
                put(IN_JOB[5] + 3, lambda: rope_ks(0, 0))
                put(IN_JOB[5] + 4, lambda: rope_ks(0, 1))
                put(IN_JOB[6] + 3, lambda: rope_ks(1, 0))
                put(IN_JOB[6] + 4, lambda: rope_ks(1, 1))
                put(IN_JOB[6] + 5, gates_in)
                put(IN_JOB[6] + 7, blocks)
                put(IN_JOB[7] + 1, gates_den)
                put(IN_JOB[7] + 3, blocks_lo)
                for m in range(2 * HEADS + 2):
                    c = IN_JOB[7] + 3 + m
                    if m >= 2 and (m - 2) % GRP == GRP - 1:
                        put(c, lambda n=(m - 2) // GRP: weighted(n))
                    if 1 <= m <= 2 * HEADS:
                        put(c, lambda m=m: prob_operand(m - 1))
                    if m < 2 * HEADS:
                        put(c, lambda m=m: score_min(m))
                put(IN_JOB[8] + 4, conv_input_upper)
                ticks = {key: m for m, key in CONV_TICK.items()}
                put(IN_JOB[7] + 3 + ticks["cu", 3] + 1, lambda: conv_taps([4, 5, 6, 7]))
                for n in (2, 3):
                    put(IN_JOB[7] + 3 + ticks["cb", n], lambda n=n: conv_gate(n))
                    put(IN_JOB[7] + 5 + ticks["cb", n], lambda n=n: conv_operand(n))
                put(CMP_JOB + 2, conv_input_lower)
                put(CMP_JOB + 7, lambda: conv_taps([0, 1, 2, 3]))
                o = OUT_JOB[0]
                put(o, lambda: conv_gate(0), lambda: conv_gate(1))
                put(o + 1, lambda: conv_operand(0), lambda: conv_operand(1))
                put(o + 2, gelu_in_)
                put(o + 3, conv_variance)
                put(o + 4, gelu_out)
                put(o + 5, lambda: inverse_root(RS_CONV), hidden_operand)
                put(o + 7, compressed_operands)
                put(o + 9, lambda: compressed_min(0), lambda: compressed_min(1))
                put(o + 11, lambda: compressed_coef(0), lambda: compressed_coef(1))
                put(o + 13, lambda: compressed_weighted(0), lambda: compressed_weighted(1))
                put(o + 14, lambda: compressed_weighted(2), lambda: compressed_weighted(3))
                put(o + 17, lambda: att_operand(0), lambda: att_operand(1))
                put(o + 18, lambda: variance(RS_ATT, CONV, 2 * NDC + 1, cols=1))
                put(o + 19, lambda: inverse_root(RS_ATT))
                for n in range(2 * NDC - 1):
                    nxt = OUT_JOB[n + 1]
                    scale = conv_scale if n < NDC else att_scale
                    off = 1
                    put(nxt + off if n != 0 else nxt + 2,
                        lambda n=n, scale=scale, nxt=nxt: residual(n % NDC, nxt, n % 2, scale))
                for n in range(NDC - 1):
                    put(OUT_JOB[NDC + n + 2] + 0 if n < 2 else FFN0[1], lambda n=n: x_operand(2, n))
                return after

            for n in range(NDC):
                x_operand(0, n)
            ffn(0)
            mix_after = mixer()
            for c in range(MIX0, FFN0[1]):
                lo(c)
                for f in mix_after.pop(c, ()):
                    f()
            for c in sorted(mix_after):
                for f in mix_after[c]:
                    f()
            ffn(1)
            residual(NDC - 1, END, 1, half)
            variance(RS_FINAL, DM, 4 * NDC + 1)
            inverse_root(RS_FINAL)
            dve.wait_ge(g_fin_landed, 16)
            for piece in range(4):
                t, h = piece // 2, piece % 2
                cols = slice(h * CONV, (h + 1) * CONV)
                stt(out=y_fin[:, t, cols], in0=x[:, t, cols], scalar=rs[:, RS_FINAL, t:t + 1], in1=g_fin[:, cols],
                    op0=ALU.mult, op1=ALU.mult).then_inc(final_ready, 1)


def shape_constants():
    import numpy as np
    c = np.zeros((P, NCONST), np.float32)
    row = np.arange(P)
    c[:, C_ID:C_ID + P] = np.eye(P, dtype=np.float32)
    c[:, C_CAUSAL:C_CAUSAL + P] = np.where(row[None, :] > row[:, None], BIG, 0.0)
    for t in range(NT):
        pos = t * P + row
        end = np.arange(NCP) * CMP_STRIDE + CMP_BLOCK - 1
        masked = (end[None, :] > pos[:, None]) | (np.arange(NCP) >= NCMP)[None, :]
        c[:, C_CMASK + t * NCP:C_CMASK + (t + 1) * NCP] = np.where(masked, BIG, 0.0)
        c[:, C_VALID + t] = pos >= CMP_BLOCK - 1
        inv = np.float32(10000.0) ** (-np.arange(0, HD, 2, dtype=np.float32) / np.float32(HD))
        ang = pos.astype(np.float32)[:, None] * inv[None, :]
        cos, sin = np.cos(ang), np.sin(ang)
        c[:, C_COS + t * HD:C_COS + (t + 1) * HD] = np.concatenate([cos, cos], 1)
        c[:, C_SIN + t * HD:C_SIN + (t + 1) * HD] = np.concatenate([-sin, sin], 1)
    for h in range(GRP):
        c[:, C_BMASK + h] = (row // NCP) % GRP == h
    c[:, C_ONE] = 1.0
    return c


_INS = ['x', 'ffn1_norm', 'ffn1_wg', 'ffn1_wu', 'ffn1_wd', 'mix_norm', 'w_in', 'conv_w', 'cmp_k_w1', 'cmp_k_w2',
        'cmp_k_pe', 'cmp_v_w1', 'cmp_v_w2', 'cmp_v_pe', 'conv_out_norm', 'attn_out_norm', 'w_out', 'ffn2_norm',
        'ffn2_wg', 'ffn2_wu', 'ffn2_wd', 'final_norm']


def kernel(**inputs):
    import numpy as _np
    import concourse.bacc as _bacc
    from concourse import mybir as _mybir
    from concourse.bass_utils import run_bass_kernel_spmd as _run

    nc = _bacc.Bacc("TRN2", target_bir_lowering=False, num_devices=1)
    arrays, args = {}, {}
    for name in _INS + ["shape_consts"]:
        v = shape_constants() if name == "shape_consts" else _np.ascontiguousarray(inputs[name])
        arrays[f"in_{name}_dram"] = v
        args[name] = nc.dram_tensor(f"in_{name}_dram", v.shape, _mybir.dt.from_np(v.dtype), kind="ExternalInput").ap()
    out = nc.dram_tensor("out_0_dram", (1, TOK, DM), _mybir.dt.from_np(_np.dtype("float32")),
                         kind="ExternalOutput").ap()
    build_program(nc, args, out)
    r = _run(nc, [arrays], core_ids=[0])
    return r.results[0]["out_0_dram"]
```

```python
import concourse.bass as bass
from concourse import mybir
from contextlib import ExitStack

F32 = mybir.dt.float32
F32R = mybir.dt.float32r
BF16 = mybir.dt.bfloat16
ALU = mybir.AluOpType
ACT = mybir.ActivationFunctionType
AX = mybir.AxisListType

P = 128
TOK = 256
NT = TOK // P
DM = 2048
FF = 5632
CH = 512
KD = DM // P
KF = FF // P
NFC = FF // CH
NDC = DM // CH
GK = 2
SLOTS = 4
CONV = 1024
CT = CONV // P
HEADS, KV, GRP, HD = 16, 4, 4, 64
CMP_BLOCK, CMP_STRIDE, CMP_HID = 32, 16, 256
NCMP = (TOK - CMP_BLOCK) // CMP_STRIDE + 1
NCP = 16
EPS = 1e-6
BIG = 1e30

JD = KD // GK
JF = KF // GK
JH = CT // GK
FFN_GROUPS = 2 * NFC * JD + NDC * JF
MIX0 = FFN_GROUPS
N_IN = 11

IN_COL = [3072, 3584, 4608, 5120, 4096, 2560, 512, 1536, 0, 1024, 2048]
Q0, Q1, KS, KW, KC, CC_UP, CH_UP, CB_UP, CH_LO, CB_LO, CC_LO = range(N_IN)


def mixer_order():
    order = [(("in", jb), j) for jb in range(N_IN - 1) for j in range(JD)]
    order += [(("in", N_IN - 1), j) for j in range(JD // 2)]
    for j in range(JD // 2):
        order += [(("in", N_IN - 1), JD // 2 + j), (("cmp",), j)]
    order += [(("cmp",), j) for j in range(JD // 2, JD)]
    for half in range(2):
        order += [(("out", n), 2 * half + j) for n in range(2) for j in range(JH // 2)]
    order += [(("out", n), j) for n in range(2, 2 * NDC) for j in range(JH)]
    return order


MIX_ORDER = mixer_order()
AT = {key: MIX0 + n for n, key in enumerate(MIX_ORDER)}
FFN0 = [0, MIX0 + len(MIX_ORDER)]
END = FFN0[1] + FFN_GROUPS
OUT0 = AT[("out", 0), 0]


TICK0 = AT[("in", CC_UP), 1]


def started(jb):
    return AT[("in", jb), 0]


def done(*job):
    return max(c for (jb, _), c in AT.items() if jb == job) + 1


GATE_COL = 5632
NG = 3 * HEADS
CONV_K_ORDER = [2, 3, 0, 1]

V_FFN1, V_MIX, V_FFN2, V_CONVW, V_GC, V_GA, V_PEK, V_PEV, NVEC = 0, 16, 32, 48, 72, 80, 88, 104, 120

C_ID, C_CAUSAL, C_CMASK, C_BMASK, C_VALID, C_COS, C_SIN, C_ONE = 0, 128, 256, 288, 292, 294, 422, 550
NCONST = 551

RS_FFN1, RS_MIX, RS_CONV, RS_ATT, RS_FFN2, RS_FINAL = range(6)


def mixer_banks():
    uses = [(("gates",), 5), (("gatesT",), 5)]
    uses += [(("q", n), 6 + n % 2) for n in range(4)]
    uses += [(("kT", 0), 6), (("kT", 1), 7)]
    extra = {8 + n: ("kvd", n) for n in range(4)}
    extra.update({21: ("cu", 2), 22: ("cu", 3), 27: ("cb", 2), 28: ("cb", 3)})
    for m in range(2 * HEADS + 2):
        if m >= 2 and (m - 2) % GRP == 0:
            uses.append((("O", (m - 2) // GRP), 5))
        if 1 <= m <= 2 * HEADS:
            uses.append((("PT", m - 1), 4))
        if m < 2 * HEADS:
            uses.append((("QK", m), 6 + m % 2))
        if m in extra:
            uses.append((extra[m], 6 + (m + 1) % 2))
    uses += [(("cb", 0), 6), (("cb", 1), 7), (("cu", 0), 4), (("cu", 1), 5), (("css",), 5)]
    uses += [(("hidT",), 6), (("kcvc",), 7), (("cs",), 6), (("pcT", 0), 7), (("pcT", 1), 6)]
    uses += [(("Oc", 0), 7), (("Oc", 1), 6), (("Oc", 2), 7), (("Oc", 3), 6)]
    uses += [(("aT", n, b), 4 + b) for n in range(2) for b in range(2)]
    first = {4: NDC + NFC + NDC, 5: NDC + NFC + NDC, 6: 0, 7: 0}
    seen, table = dict(first), {}
    for key, bank in uses:
        table[key] = (bank, seen[bank])
        seen[bank] += 1
    return table, extra, seen


def count(c, i=None, per=0):
    return c if i is None else i * per + c


def build_program(nc, a, out):
    USE, EXTRA, seen = mixer_banks()
    GU_USE = [NDC, seen[4] + NDC]
    XT_USE = {0: 0, 1: NDC + NFC, 2: seen[4]}
    XT_USE5 = {0: 0, 1: NDC + NFC, 2: seen[5]}
    GU_USE5 = [NDC, seen[5] + NDC]

    def operand_use(kind, which, b, n=0, i=None):
        base = {"x": (XT_USE, XT_USE5), "gu": (GU_USE, GU_USE5)}[kind][b][which]
        return base + n, i

    rows = lambda w: w.rearrange("(k p) n -> p k n", p=P)
    wg = [rows(a["ffn1_wg"][0]), rows(a["ffn2_wg"][0])]
    wu = [rows(a["ffn1_wu"][0]), rows(a["ffn2_wu"][0])]
    wd = [rows(a["ffn1_wd"][0]), rows(a["ffn2_wd"][0])]
    w_in = rows(a["w_in"][0])
    w_out = rows(a["w_out"][0])
    w1 = [a[f"cmp_{n}_w1"][0].rearrange("(k l) d f -> (l d) k f", l=2) for n in "kv"]
    w2 = [a[f"cmp_{n}_w2"][0].rearrange("(k p) d -> p k d", p=P) for n in "kv"]
    x_in = a["x"][0].rearrange("(t p) d -> p t d", p=P)
    y_out = out[0].rearrange("(t p) d -> p t d", p=P)

    at = [(nc.sbuf_base + 63) // 64 * 64]
    limit = nc.sbuf_usable_end

    def sb(name, shape, dt=F32):
        size = 2 if dt == BF16 else 4
        for n in shape[1:]:
            size *= n
        t = nc.alloc_sbuf_tensor_at(name, shape, dt, offset=at[0])
        at[0] += (size + 31) // 32 * 32
        assert at[0] <= limit, (name, at[0], limit)
        return t

    consts = sb("consts", [P, NCONST])
    vec_rows = sb("vec_rows", [P, P])
    vecs = sb("vecs", [P, NVEC])
    ident_b = sb("ident_b", [P, P], BF16)
    causal_b = sb("causal_b", [P, 2, P], BF16)
    cmask_b = sb("cmask_b", [P, NT, HEADS, NCP], BF16)
    w2k = sb("w2k", [P, 2, 2, HD])
    w2v = sb("w2v", [P, 2, HD])
    ssq = sb("ssq", [P, 6, NT, NDC])
    var = sb("var", [P, 6, NT])
    rs = sb("rs", [P, 6, NT])
    junk = sb("junk", [P, CONV], BF16)
    x = sb("x", [P, NT, DM])
    raw = sb("raw", [P, SLOTS, GK, CH])
    w_hi = sb("w_hi", [P, SLOTS, GK, CH], F32R)
    w_lo = sb("w_lo", [P, SLOTS, GK, CH], F32R)
    h_at = at[0]
    hT_hi = sb("hT_hi", [P, KD, TOK], F32R)
    hT_lo = sb("hT_lo", [P, KD, TOK], F32R)
    zone = at[0]
    at[0] = h_at
    g_fin = sb("g_fin", [P, DM])
    at[0] = h_at + 4 * KD * TOK
    y_fin = sb("y_fin", [P, NT, DM])
    at[0] = zone
    guT_hi = sb("guT_hi", [P, KF, TOK], F32R)
    guT_lo = sb("guT_lo", [P, KF, TOK], F32R)
    gu = sb("gu", [P, NT, CH])
    at[0] = zone
    y_at = at[0]
    p_cc = sb("p_cc", [P, NT, CH])
    p_kvc = sb("p_kvc", [P, NT, CH])
    p_q = sb("p_q", [P, NT, CONV])
    p_kv = sb("p_kv", [P, NT, 2 * CH])
    p_h = sb("p_h", [P, NT, CONV])
    p_b = sb("p_b", [P, NT, CONV])
    uT = sb("uT", [P, CT, TOK + 2])
    ycT_lo = sb("ycT_lo", [P, CT, TOK], F32R)
    blk_at = at[0]
    blk_hi = sb("blk_hi", [P, KD, P], F32R)
    blk_lo = sb("blk_lo", [P, KD, P], F32R)
    qk_at = at[0]
    qT = sb("qT", [P, 8, TOK])
    kT = sb("kT", [P, 2, 2, TOK])
    p_at = at[0]
    prob = sb("prob", [P, 2, CH])
    probT = sb("probT", [P, 2, CH])
    scr = sb("scr", [P, CONV])
    den = sb("den", [P, NT, HEADS, 3])
    mins = sb("mins", [P, 2 * HEADS, 2])
    sums = sb("sums", [P, 2 * HEADS, 2])
    coef = sb("coef", [P, GRP, 2])
    cmin = sb("cmin", [P, NT, HEADS])
    csum = sb("csum", [P, NT, HEADS])
    top = at[0]
    at[0] = y_at
    ycT_hi = sb("ycT_hi", [P, CT, TOK], F32R)
    y_att = p_q
    blk_f = p_b[:, :, :].rearrange("p t (k m) -> p (t k) m", m=P)
    kvd = p_h[:, :, :].rearrange("p t (v j d) -> p t v j d", v=2, j=KV)
    kT2 = uT[:, :, 0:TOK].rearrange("p (v j) t -> p v j t", v=2)
    at[0] = qk_at
    aT_hi = sb("aT_hi", [P, CT, TOK], F32R)
    aT_lo = sb("aT_lo", [P, CT, TOK], F32R)
    at[0] = blk_at
    w_gate = sb("w_gate", [P, KD, NG])
    wg_hi = sb("wg_hi", [P, KD, NG], F32R)
    wg_lo = sb("wg_lo", [P, KD, NG], F32R)
    gT = sb("gT", [P, TOK])
    at[0] = blk_at
    hidkT = sb("hidkT", [P, 2, KV * NCP])
    hidvT = sb("hidvT", [P, 2, KV, GRP, NCP])
    kcT = sb("kcT", [P, 2, 2, NCP])
    vcb = sb("vcb", [P, 2, GRP, HD])
    pc = sb("pc", [P, NT, HEADS, NCP])
    pcT = sb("pcT", [P, NT, 2, P])
    assert at[0] <= qk_at
    at[0] = top

    ident = consts[:, C_ID:C_ID + P]
    cos_t = consts[:, C_COS:C_COS + NT * HD].rearrange("p (t d) -> p t d", t=NT)
    sin_t = consts[:, C_SIN:C_SIN + NT * HD].rearrange("p (t d) -> p t d", t=NT)
    ones = consts[:, C_ONE:C_ONE + 1]

    def cv(c, n=1):
        lo = (c // 4) * CH + (c % 2) * TOK
        return p_h[:, (c % 4) // 2, lo:lo + n * TOK]

    ctx = ExitStack()
    with ctx:
        ps = ctx.enter_context(nc.psum_tensor("ps", [P, 8, CH], F32))
        sem = lambda n: ctx.enter_context(nc.semaphore(n))

        landed = [sem(f"landed{s}") for s in range(SLOTS)]
        hi_ready = sem("hi_ready")
        lo_ready = sem("lo_ready")
        group_done = sem("group_done")
        x_landed = [sem(f"x_landed{n}") for n in range(NDC)]
        first_landed = sem("first_landed")
        consts_landed = sem("consts_landed")
        small_landed = sem("small_landed")
        gate_w_landed = sem("gate_w_landed")
        g_fin_landed = sem("g_fin_landed")
        masks_ready = sem("masks_ready")
        vecs_full = sem("vecs_full")
        vecs_ready = sem("vecs_ready")
        full = {b: sem(f"bank_full{b}") for b in (4, 5, 6, 7)}
        free = {b: sem(f"bank_free{b}") for b in (4, 5, 6, 7)}
        operand_hi = sem("operand_hi")
        ssq_done = sem("ssq_done")
        var_done = sem("var_done")
        root_done = sem("root_done")
        rs_done = sem("rs_done")
        silu_done = sem("silu_done")
        gu_done = sem("gu_done")
        resid_done = sem("resid_done")
        proj_done = sem("proj_done")
        q_roped = sem("q_roped")
        kvd_ready = sem("kvd_ready")
        ks_roped = sem("ks_roped")
        kT2_ready = sem("kT2_ready")
        pads_zero = sem("pads_zero")
        blk_ready = sem("blk_ready")
        blk_hi_ready = sem("blk_hi_ready")
        blk_lo_ready = sem("blk_lo_ready")
        gates_scaled = sem("gates_scaled")
        gate_w_hi = sem("gate_w_hi")
        gate_w_lo = sem("gate_w_lo")
        gates_exp = sem("gates_exp")
        mins_ready = sem("mins_ready")
        u_ready = sem("u_ready")
        conv_ready = sem("conv_ready")
        ysq_ready = sem("ysq_ready")
        ysum_ready = sem("ysum_ready")
        pool_step = sem("pool_step")
        ycT_hi_ready = sem("ycT_hi_ready")
        ycT_lo_ready = sem("ycT_lo_ready")
        gelu_in = sem("gelu_in")
        gelu_exp = sem("gelu_exp")
        hid_ready = sem("hid_ready")
        cdiff_ready = sem("cdiff_ready")
        cexp_ready = sem("cexp_ready")
        y_att_ready = sem("y_att_ready")
        final_ready = sem("final_ready")
        stored = sem("stored")
        act_step = sem("act_step")
        dve_step = sem("dve_step")

        def landed_value(c, i=None, per=0):
            extra = sum(AT[("cmp",), j] <= c and AT[("cmp",), j] % SLOTS == c % SLOTS for j in range(JD))
            return count(16 * (c // SLOTS + 1 + extra), i, 16 * per // SLOTS)

        block = ctx.enter_context(nc.Block())

        @block.sync
        def _(sp):
            def load(c, src, i=None, per=0, halves=None):
                if c >= SLOTS:
                    sp.wait_ge(lo_ready, count(c - SLOTS + 1, i, per))
                s = c % SLOTS
                if halves is None:
                    sp.dma_start(raw[:, s, :, :], src).then_inc(landed[s], 16)
                else:
                    sp.dma_start(raw[:, s, :, 0:CMP_HID], halves[0]).then_inc(landed[s], 16)
                    sp.dma_start(raw[:, s, :, CMP_HID:CH], halves[1]).then_inc(landed[s], 16)

            def load_x(n):
                sp.dma_start(x[:, :, n * CH:n * CH + CH], x_in[:, :, n * CH:n * CH + CH]).then_inc(x_landed[n], 16)

            def ffn(f):
                c = FFN0[f]
                for j in range(JD):
                    if f == 0 and j % 2 == 0:
                        load_x(j // 2)
                    load(c + j, wg[f][:, GK * j:GK * j + GK, 0:CH])
                c += JD
                with sp.Fori(0, NFC - 1) as i:
                    for j in range(JD):
                        load(c + j, wu[f][:, GK * j:GK * j + GK, bass.ds(i * CH, CH)], i, 2 * JD)
                    for j in range(JD):
                        load(c + JD + j, wg[f][:, GK * j:GK * j + GK, bass.ds(i * CH + CH, CH)], i, 2 * JD)
                c += 2 * JD * (NFC - 1)
                for j in range(JD):
                    load(c + j, wu[f][:, GK * j:GK * j + GK, (NFC - 1) * CH:FF])
                c += JD
                for n in range(NDC):
                    if f == 1 and n == 1:
                        sp.wait_ge(group_done, c)
                        sp.dma_start(g_fin[:, :], a["final_norm"].partition_broadcast(P)).then_inc(g_fin_landed, 16)
                    for j in range(JF):
                        load(c + JF * n + j, wd[f][:, GK * j:GK * j + GK, n * CH:n * CH + CH])

            ffn(0)
            for (job, j), c in AT.items():
                k = slice(GK * j, GK * j + GK)
                if job[0] == "in":
                    load(c, w_in[:, k, IN_COL[job[1]]:IN_COL[job[1]] + CH])
                elif job[0] == "cmp":
                    load(c, None, halves=(w1[0][:, k, :], w1[1][:, k, :]))
                else:
                    half, n = divmod(job[1], NDC)
                    k = GK * (JH + j if half else CONV_K_ORDER[j])
                    load(c, w_out[:, k:k + GK, n * CH:(n + 1) * CH])
            ffn(1)
            for piece in range(4):
                t, h = piece // 2, piece % 2
                sp.wait_ge(final_ready, piece + 1)
                sp.dma_start(y_out[:, t, h * CONV:(h + 1) * CONV],
                             y_fin[:, t, h * CONV:(h + 1) * CONV]).then_inc(stored, 16)
            sp.wait_ge(stored, 64)

        @block.gpsimd
        def _(pool):
            small = [(V_MIX, KD, a["mix_norm"].rearrange("l (k p) -> (l k) p", p=P)),
                     (V_FFN2, KD, a["ffn2_norm"].rearrange("l (k p) -> (l k) p", p=P)),
                     (V_CONVW, 3 * CT, a["conv_w"].rearrange("l w (k p) -> (l w k) p", p=P)),
                     (V_GC, CT, a["conv_out_norm"].rearrange("l (k p) -> (l k) p", p=P)),
                     (V_GA, CT, a["attn_out_norm"].rearrange("l (k p) -> (l k) p", p=P)),
                     (V_PEK, KD, a["cmp_k_pe"].rearrange("l (k w) d -> (l k) (w d)", w=2)),
                     (V_PEV, KD, a["cmp_v_pe"].rearrange("l (k w) d -> (l k) (w d)", w=2))]
            pool.wait_ge(hi_ready, JD - 2)
            pool.dma_start(consts[:, P:NCONST], a["shape_consts"][:, P:NCONST]).then_inc(consts_landed, 16)
            for row, n, src in small:
                pool.dma_start(vec_rows[row:row + n, :], src).then_inc(small_landed, 16)
            for half in range(2):
                pool.dma_start(w2k[:, :, half, :], w2[0]).then_inc(small_landed, 16)
            pool.dma_start(w2v[:, :, :], w2[1]).then_inc(small_landed, 16)
            pool.wait_ge(first_landed, 32)
            pool.wait_ge(consts_landed, 16)
            pool.tensor_copy(ident_b[:, :], ident)
            for br in range(2):
                pool.tensor_copy(causal_b[:, br, :], consts[:, C_CAUSAL:C_CAUSAL + P])
            cm = consts[:, C_CMASK:C_CMASK + NT * NCP].rearrange("p (t n) -> p t n", t=NT)
            for t in range(NT):
                ins = pool.tensor_copy(cmask_b[:, t, :, :], cm[:, t, :].unsqueeze(1).to_broadcast([P, HEADS, NCP]))
            ins.then_inc(masks_ready, 1)
            pool.wait_ge(group_done, MIX0)
            pool.memset(blk_f, 0.0).then_inc(pads_zero, 1)
            ysq = lambda c: uT[:, c:c + 2, 0:TOK]
            pool.wait_ge(ysq_ready, 2)
            pool.tensor_tensor(ysq(4), ysq(4), ysq(6), ALU.add).then_inc(pool_step, 1)
            pool.wait_ge(ysq_ready, 4)
            pool.tensor_tensor(ysq(0), ysq(0), ysq(2), ALU.add).then_inc(pool_step, 1)
            pool.wait_ge(pool_step, 2)
            pool.tensor_tensor(ysq(0), ysq(0), ysq(4), ALU.add).then_inc(ysum_ready, 1)

        @block.tensor
        def _(pe):
            mm = nc.tensor.matmul

            def group(c, i, per, hi, lo, k, banks, first, last, cols=TOK):
                pe.wait_ge(lo_ready, count(c + 1, i, per))
                s = c % SLOTS
                for kk in range(GK):
                    for t, bank in enumerate(banks):
                        o = ps[:, bank, :]
                        x_hi = hi[:, k + kk, t * P:t * P + P]
                        x_lo = lo[:, k + kk, t * P:t * P + P]
                        mm(o, x_hi, w_hi[:, s, kk, :], start=first and kk == 0, stop=False)
                        mm(o, x_hi, w_lo[:, s, kk, :], start=False, stop=False)
                        ins = mm(o, x_lo, w_hi[:, s, kk, :], start=False, stop=last and kk == GK - 1)
                ins.then_inc(group_done, 1)

            def job(c, n, hi, lo, pair, i=None, per=0, after={}, before={}, ks=None, banks=None):
                banks = banks or [2 * pair, 2 * pair + 1]
                for j in range(n):
                    for f in before.get(j, ()):
                        f()
                    k = GK * (ks[j] if ks else j)
                    group(c + j, i, per, hi, lo, k, banks, j == 0, j == n - 1)
                    for f in after.get(j, ()):
                        f()

            def to_bank(bank, n, i=None, per=0):
                if n:
                    pe.wait_ge(free[bank], count(n, i, per))

            def transposes(bank, pieces):
                for o, src in pieces:
                    ins = pe.transpose(ps[:, bank, o:o + P], src, ident)
                ins.then_inc(full[bank], 1)

            def x_transposes(which, n):
                if which == 0:
                    pe.wait_ge(x_landed[n], 16)
                else:
                    pe.wait_ge(resid_done, 2 * (NDC * (1 if which == 1 else 3) - NDC + n + 1))
                for b in range(2):
                    to_bank(4 + b, operand_use("x", which, b, n)[0])
                    transposes(4 + b, [(kk * TOK + t * P, x[:, t, (4 * n + 2 * b + kk) * P:][:, 0:P])
                                       for kk in range(2) for t in range(NT)])

            def x_operand(which, n):
                for b in range(2):
                    pe.wait_ge(free[4 + b], operand_use("x", which, b, n)[0] + 1)

            def gu_transposes(f, n, i=None):
                pe.wait_ge(gu_done, count(2 * (NFC * f + n + 1), i, 2))
                for b in range(2):
                    to_bank(4 + b, operand_use("gu", f, b, n)[0], i, 1)
                    transposes(4 + b, [(kk * TOK + t * P, gu[:, t, (2 * b + kk) * P:][:, 0:P])
                                       for kk in range(2) for t in range(NT)])

            def gu_operand(f, n):
                for b in range(2):
                    pe.wait_ge(free[4 + b], operand_use("gu", f, b, n)[0] + 1)

            def vector_transposes():
                pe.wait_ge(small_landed, 16 * 10)
                pe.transpose(ps[:, 7, 0:NVEC], vec_rows[0:NVEC, :], consts[0:NVEC, 0:NVEC]).then_inc(vecs_full, 1)

            def ffn(f):
                which = 0 if f == 0 else 2
                c = FFN0[f]
                before = {2 * n: [lambda n=n: x_operand(which, n)] for n in range(NDC)}
                if f == 0:
                    x_transposes(0, 0)
                    after = {2 * n - 2: [lambda n=n: x_transposes(0, n)] for n in range(1, NDC)}
                else:
                    after = {3: [lambda: x_transposes(2, NDC - 1)]}
                job(c, JD, hT_hi, hT_lo, 0, after=after, before=before)
                c += JD
                with pe.Fori(0, NFC - 1) as i:
                    job(c, JD, hT_hi, hT_lo, 1, i, 2 * JD)
                    pe.wait_ge(silu_done, count(2 * (NFC * f + 1), i, 2))
                    job(c + JD, JD, hT_hi, hT_lo, 0, i, 2 * JD, after={3: [lambda: gu_transposes(f, 0, i)]})
                c += 2 * JD * (NFC - 1)
                job(c, JD, hT_hi, hT_lo, 1)
                c += JD
                pe.wait_ge(silu_done, 2 * NFC * (f + 1))
                for n in range(NDC):
                    if n == 0:
                        before = {0: [lambda: gu_operand(f, NFC - 2)], JF - 2: [lambda: gu_operand(f, NFC - 1)]}
                        after = {3: [lambda: gu_transposes(f, NFC - 1)]}
                        if f == 0:
                            after[6] = [vector_transposes]
                    else:
                        before = {}
                        if f == 0:
                            after = {3: [lambda: x_transposes(1, n - 1)]}
                        else:
                            after = {3: [lambda: pe.wait_ge(resid_done, 2 * (3 * NDC + n))]}
                    job(c + JF * n, JF, guT_hi, guT_lo, n % 2, before=before, after=after)

            def q_transposes(n):
                bank, u = USE["q", n]
                if n == 0:
                    pe.wait_ge(q_roped, NT)
                to_bank(bank, u)
                transposes(bank, [(kk * TOK + t * P, p_q[:, t, (2 * n + kk) * P:][:, 0:P])
                                  for kk in range(2) for t in range(NT)])

            def kvd_transposes(n):
                bank, u = USE["kvd", n]
                pe.wait_ge(kvd_ready, NT)
                to_bank(bank, u)
                transposes(bank, [(kk * TOK + t * P, kvd[:, t, n // 2, 2 * (n % 2) + kk, :])
                                  for kk in range(2) for t in range(NT)])

            def gates():
                bank, u = USE["gates",]
                pe.wait_ge(gate_w_lo, 1)
                to_bank(bank, u)
                for k in range(KD):
                    o = ps[0:NG, bank, 0:TOK]
                    mm(o, wg_hi[:, k, :], hT_hi[:, k, :], start=k == 0, stop=False)
                    mm(o, wg_lo[:, k, :], hT_hi[:, k, :], start=False, stop=False)
                    ins = mm(o, wg_hi[:, k, :], hT_lo[:, k, :], start=False, stop=k == KD - 1)
                ins.then_inc(full[bank], 1)

            def gate_transposes():
                bank, u = USE["gatesT",]
                to_bank(bank, u)
                for t in range(NT):
                    ins = pe.transpose(ps[:, bank, t * NG:t * NG + NG], gT[0:NG, t * P:t * P + P],
                                       consts[0:NG, 0:NG])
                ins.then_inc(full[bank], 1)

            def kT_transposes(jp):
                bank, u = USE["kT", jp]
                pe.wait_ge(ks_roped, 2)
                to_bank(bank, u)
                transposes(bank, [(br * TOK + t * P, p_kv[:, t, br * CH + jp * P:][:, 0:P])
                                  for br in range(2) for t in range(NT)])

            def scores(m):
                t, h = divmod(m, HEADS)
                j, r = divmod(h, GRP)
                jp, par = divmod(j, 2)
                nk = (t + 1) * P
                rows_ = slice(par * HD, par * HD + HD)
                bank, u = USE["QK", m]
                if m == 0:
                    pe.wait_ge(masks_ready, 1)
                    for key in (("q", 2), ("q", 3), ("kT", 0), ("kT", 1)):
                        pe.wait_ge(free[USE[key][0]], USE[key][1] + 1)
                to_bank(bank, u)
                o = ps[:, bank, 0:2 * nk].rearrange("p (b n) -> p b n", b=2)
                mm(o, qT[rows_, jp * GRP + r, t * P:t * P + P], kT[rows_, jp, :, 0:nk], start=True, stop=False)
                mm(o[:, :, nk - P:nk], ident_b[:, :], causal_b[:, :, :], start=False, stop=True).then_inc(full[bank], 1)

            def prob_transposes(m):
                t = m // HEADS
                qk_bank, qk_u = USE["QK", m]
                bank, u = USE["PT", m]
                pe.wait_ge(free[qk_bank], qk_u + 1)
                to_bank(bank, u)
                transposes(bank, [(n * P, prob[:, m % 2, n * P:n * P + P]) for n in range(2 * (t + 1))])

            def weighted_values(m):
                t, h = divmod(m, HEADS)
                j, r = divmod(h, GRP)
                pe.wait_ge(free[4], USE["PT", m][1] + 1)
                bank, u = USE["O", m // GRP]
                if r == 0:
                    to_bank(bank, u)
                for br in range(2):
                    for kt in range(t + 1):
                        ins = mm(ps[:, bank, r * P + br * HD:][:, 0:HD],
                                 probT[:, m % 2, (br * (t + 1) + kt) * P:][:, 0:P],
                                 p_kv[:, kt, br * CH + KV * HD + j * HD:][:, 0:HD], start=kt == 0, stop=kt == t)
                if r == GRP - 1:
                    ins.then_inc(full[bank], 1)

            def conv_transposes(key):
                kind, n = key
                bank, u = USE[key]
                if kind == "cu":
                    pe.wait_ge(u_ready, 2 if n >= 2 else 4)
                    src = p_h
                else:
                    pe.wait_ge(proj_done, 2 * ((CB_UP if n >= 2 else CB_LO) + 1))
                    src = p_b
                to_bank(bank, u)
                transposes(bank, [(kk * TOK + t * P, src[:, t, (2 * n + kk) * P:][:, 0:P])
                                  for kk in range(2) for t in range(NT)])

            def tick(m):
                if m >= 2:
                    weighted_values(m - 2)
                if 1 <= m <= 2 * HEADS:
                    prob_transposes(m - 1)
                if m < 2 * HEADS:
                    scores(m)
                if m in EXTRA:
                    if EXTRA[m][0] == "kvd":
                        kvd_transposes(EXTRA[m][1])
                    else:
                        conv_transposes(EXTRA[m])

            def conv_square_sum():
                bank, u = USE["css",]
                pe.wait_ge(ysum_ready, 1)
                to_bank(bank, u)
                for t in range(NT):
                    for c in range(2):
                        ins = mm(ps[:, bank, t:t + 1], uT[:, c, t * P:t * P + P], ones, start=c == 0, stop=c == 1)
                ins.then_inc(full[bank], 1)

            def hid_transposes():
                bank, u = USE["hidT",]
                pe.wait_ge(hid_ready, 1)
                to_bank(bank, u)
                transposes(bank, [(n * P, scr[:, n * P:n * P + P]) for n in range(4)])

            def compressed_kv():
                bank, u = USE["kcvc",]
                pe.wait_ge(free[USE["hidT",][0]], USE["hidT",][1] + 1)
                to_bank(bank, u)
                for f in range(2):
                    mm(ps[:, bank, 0:HD], w2k[:, f, :, :].rearrange("p a d -> p (a d)"), hidkT[:, f, :],
                       start=f == 0, stop=f == 1)
                for jp in range(2):
                    for f in range(2):
                        ins = mm(ps[:, bank, HD * (jp + 1):][:, 0:HD],
                                 hidvT[:, f, 2 * jp:2 * jp + 2, :, :].rearrange("p j h n -> p (j h n)"), w2v[:, f, :],
                                 start=f == 0, stop=f == 1)
                ins.then_inc(full[bank], 1)

            def compressed_scores():
                bank, u = USE["cs",]
                pe.wait_ge(free[USE["kcvc",][0]], USE["kcvc",][1] + 1)
                to_bank(bank, u)
                mm(ps[:, bank, :].rearrange("p (t n) -> p t n", t=NT), ident_b[:, :],
                   cmask_b[:, :, :, :].rearrange("p t h n -> p t (h n)"), start=True, stop=True,
                   skip_group_check=True)
                for t in range(NT):
                    for q in range(HEADS // 2):
                        ins = mm(ps[:, bank, (t * (HEADS // 2) + q) * 2 * NCP:][:, 0:2 * NCP],
                                 qT[:, q, t * P:t * P + P], kcT[:, q // GRP, :, :].rearrange("p a n -> p (a n)"),
                                 start=False, stop=True, skip_group_check=True)
                ins.then_inc(full[bank], 1)

            def compressed_prob_transposes(t):
                bank, u = USE["pcT", t]
                pe.wait_ge(cexp_ready, 1)
                to_bank(bank, u)
                flat = pc[:, t, :, :].rearrange("p h n -> p (h n)")
                transposes(bank, [(n * P, flat[:, n * P:n * P + P]) for n in range(2)])

            def compressed_values(n):
                t, par = divmod(n, 2)
                rows_ = slice(par * HD, par * HD + HD)
                bank, u = USE["Oc", n]
                pe.wait_ge(free[USE["pcT", t][0]], USE["pcT", t][1] + 1)
                to_bank(bank, u)
                for jp in range(2):
                    ins = mm(ps[:, bank, jp * TOK:jp * TOK + TOK], pcT[rows_, t, jp, :],
                             vcb[rows_, jp, :, :].rearrange("p h d -> p (h d)"), start=True, stop=True)
                ins.then_inc(full[bank], 1)

            def att_transposes(n):
                pe.wait_ge(y_att_ready, 1)
                for b in range(2):
                    bank, u = USE["aT", n, b]
                    to_bank(bank, u)
                    transposes(bank, [(kk * TOK + t * P, y_att[:, t, (4 * n + 2 * b + kk) * P:][:, 0:P])
                                      for kk in range(2) for t in range(NT)])

            def mixer():
                after = {}

                def put(c, *fs):
                    after.setdefault(c, []).extend(fs)

                put(MIX0 + 3, lambda: x_transposes(1, NDC - 1))
                put(started(KS) + 0, gates)
                put(started(KS) + 3, gate_transposes)
                put(started(KW) + 2, lambda: q_transposes(0), lambda: q_transposes(1))
                put(started(KW) + 5, lambda: q_transposes(2), lambda: q_transposes(3))
                put(started(KC) + 6, lambda: kT_transposes(0), lambda: kT_transposes(1))
                for m in range(2 * HEADS + 2):
                    put(TICK0 + m, lambda m=m: tick(m))
                put(started(CC_LO) + 3, lambda: conv_transposes(("cb", 0)), lambda: conv_transposes(("cb", 1)))
                put(OUT0 - 3, lambda: conv_transposes(("cu", 0)), lambda: conv_transposes(("cu", 1)))
                o = OUT0
                put(o + 5, conv_square_sum)
                put(o + 6, hid_transposes)
                put(o + 8, compressed_kv)
                put(o + 9, compressed_scores)
                put(o + 11, lambda: compressed_prob_transposes(0), lambda: compressed_prob_transposes(1))
                put(o + 13, lambda: compressed_values(0), lambda: compressed_values(1))
                put(o + 14, lambda: compressed_values(2), lambda: compressed_values(3))
                put(o + 15, lambda: att_transposes(0), lambda: att_transposes(1))
                for n in range(NDC - 1):
                    put(AT[("out", NDC + n + 1), 2], lambda n=n: x_transposes(2, n))

                for (job, j), c in AT.items():
                    n = job[-1]
                    if job[0] == "in":
                        if j == 0 and n >= 2:
                            pe.wait_ge(proj_done, 2 * (n - 1))
                        if n == 0 and j % 2 == 0:
                            x_operand(1, j // 2)
                        banks = [2 * (n % 2), 2 * (n % 2) + 1]
                        group(c, None, 0, hT_hi, hT_lo, GK * j, banks, j == 0, j == JD - 1)
                    elif job[0] == "cmp":
                        if j == 0:
                            pe.wait_ge(proj_done, 2 * (CB_LO + 1))
                            pe.wait_ge(blk_lo_ready, 1)
                        group(c, None, 0, blk_hi, blk_lo, GK * j, [2], j == 0, j == JD - 1)
                    else:
                        if j == 0:
                            if n == 0:
                                pe.wait_ge(u_ready, 4)
                            elif n == 1:
                                pe.wait_ge(gelu_in, 1)
                            else:
                                pe.wait_ge(resid_done, 2 * (NDC + n - 1))
                        if n == 0 and j % 2 == 0:
                            pe.wait_ge(ycT_lo_ready, 4 * (j // 2 + 1))
                        if n == NDC and j % 2 == 0:
                            for b in range(2):
                                pe.wait_ge(free[4 + b], USE["aT", j // 2, b][1] + 1)
                        hi, lo, k = (ycT_hi, ycT_lo, CONV_K_ORDER[j]) if n < NDC else (aT_hi, aT_lo, j)
                        group(c, None, 0, hi, lo, GK * k, [2 * (n % 2), 2 * (n % 2) + 1], j == 0, j == JH - 1)
                    for f in after.get(c, ()):
                        f()

            pe.wait_ge(first_landed, 32)
            pe.transpose(ps[:, 6, 0:KD], vec_rows[0:KD, :], consts[0:KD, 0:KD]).then_inc(vecs_full, 1)
            ffn(0)
            mixer()
            ffn(1)

        @block.scalar
        def _(act):
            steps = [0]

            def seq(ins):
                ins.then_inc(act_step, 1)
                steps[0] += 1
                act.wait_ge(act_step, steps[0])

            act.dma_start(consts[:, C_ID:C_ID + P], a["shape_consts"][:, C_ID:C_ID + P]).then_inc(first_landed, 16)
            act.dma_start(vec_rows[V_FFN1:V_FFN1 + KD, :],
                          a["ffn1_norm"].rearrange("l (k p) -> (l k) p", p=P)).then_inc(first_landed, 16)
            def vectors():
                act.wait_ge(vecs_full, 2)
                act.activation(vecs[:, KD:NVEC], ps[:, 7, KD:NVEC], ACT.Copy).then_inc(vecs_ready, 1)
                act.wait_ge(vecs_ready, 2)

            def hi(c, i=None, per=0):
                act.wait_ge(landed[c % SLOTS], landed_value(c, i, per))
                if c >= SLOTS:
                    act.wait_ge(group_done, count(c - SLOTS + 1, i, per))
                act.activation(w_hi[:, c % SLOTS, :, :], raw[:, c % SLOTS, :, :], ACT.Copy).then_inc(hi_ready, 1)

            def job(c, n, i=None, per=0, after={}):
                for j in range(n):
                    hi(c + j, i, per)
                    for f in after.get(j, ()):
                        f()

            def scaled_operand(dst, tile0, vec0, banks):
                for b, (bank, n) in enumerate(banks):
                    act.wait_ge(full[bank], n + 1)
                    for kk in range(2):
                        k = tile0 + 2 * b + kk
                        ins = act.activation(dst[:, k, :], ps[:, bank, kk * TOK:kk * TOK + TOK], ACT.Copy,
                                             scale=vecs[:, vec0 + k:vec0 + k + 1])
                    ins.then_inc(operand_hi, 1)

            def x_operand(which, n):
                vec0 = (V_FFN1, V_MIX, V_FFN2)[which]
                scaled_operand(hT_hi, 4 * n, vec0, [(4 + b, operand_use("x", which, b, n)[0]) for b in range(2)])

            def square(phase, n, src_ready):
                src_ready()
                for t in range(NT):
                    ins = act.activation(junk[:, t * CH:t * CH + CH], x[:, t, n * CH:n * CH + CH], ACT.Square,
                                         accum_out=ssq[:, phase, t, n:n + 1])
                    seq(ins)
                act.sem_inc(ssq_done, 1)

            def x_square(phase, n, resid):
                square(phase, n, lambda: act.wait_ge(resid_done, resid))

            def root(phase):
                act.wait_ge(var_done, phase + 1)
                act.activation(var[:, phase, :], var[:, phase, :], ACT.Sqrt).then_inc(root_done, 1)

            def silu(f, n, done, i=None):
                act.wait_ge(group_done, count(done, i, 2 * JD))
                if n or i is not None or f:
                    prev = NFC * f + n - 1
                    base = operand_use("gu", f, 0, n)[0], operand_use("gu", f, 1, n)[0]
                    for b in range(2):
                        act.wait_ge(full[4 + b], count(base[b], i, 1))
                else:
                    pass
                if n == 0 and i is None:
                    act.wait_ge(rs_done, (RS_FFN2 if f else RS_FFN1) + 1)
                for t in range(NT):
                    act.activation(gu[:, t, :], ps[:, t, :], ACT.Silu,
                                   scale=rs[:, RS_FFN2 if f else RS_FFN1, t:t + 1]).then_inc(silu_done, 1)

            def gu_operand(f, n, i=None):
                for b in range(2):
                    act.wait_ge(full[4 + b], count(operand_use("gu", f, b, n)[0] + 1, i, 1))
                    k = 4 * n + 2 * b
                    dst = guT_hi[:, k:k + 2, :] if i is None else guT_hi[:, bass.ds(i * 4 + k, 2), :]
                    act.activation(dst, ps[:, 4 + b, :].rearrange("p (k t) -> p k t", k=2),
                                   ACT.Copy).then_inc(operand_hi, 1)

            def ffn(f):
                c = FFN0[f]
                phase = RS_FFN2 if f else RS_FFN1
                if f == 0:
                    sq = [lambda n=n: square(RS_FFN1, n, lambda: act.wait_ge(x_landed[n], 16)) for n in range(NDC)]
                    x_operand(0, 0)
                    after = {1: [sq[0]], 2: [lambda: x_operand(0, 1)], 3: [sq[1]], 4: [lambda: x_operand(0, 2)],
                             5: [sq[2]], 6: [lambda: x_operand(0, 3), sq[3]],
                             7: [lambda: root(RS_FFN1)]}
                else:
                    after = {1: [lambda: x_square(RS_FFN2, NDC - 1, 6 * NDC)],
                             4: [lambda: root(RS_FFN2)], 5: [lambda: x_operand(2, NDC - 1)]}
                job(c, JD, after=after)
                c += JD
                with act.Fori(0, NFC - 1) as i:
                    job(c, JD, i, 2 * JD, after={1: [lambda: silu_loop(f, c, i)]})
                    job(c + JD, JD, i, 2 * JD, after={5: [lambda: gu_operand(f, 0, i)]})
                c += 2 * JD * (NFC - 1)
                job(c, JD, after={1: [lambda: silu(f, NFC - 1, c)]})
                c += JD
                for n in range(NDC):
                    if n == 0:
                        after = {5: [lambda: gu_operand(f, NFC - 1)]}
                        if f == 0:
                            after[8] = [vectors]
                    elif f == 0:
                        after = {3: [lambda: x_square(RS_MIX, n - 1, 2 * n)], 5: [lambda: x_operand(1, n - 1)]}
                    else:
                        after = {3: [lambda: x_square(RS_FINAL, n - 1, 2 * (3 * NDC + n))]}
                    job(c + JF * n, JF, after=after)

            def silu_loop(f, c, i):
                act.wait_ge(group_done, count(c, i, 2 * JD))
                act.wait_ge(rs_done, (RS_FFN2 if f else RS_FFN1) + 1)
                for b in range(2):
                    base = operand_use("gu", f, b, 0)[0]
                    act.wait_ge(full[4 + b], count(base, i, 1))
                for t in range(NT):
                    act.activation(gu[:, t, :], ps[:, t, :], ACT.Silu,
                                   scale=rs[:, RS_FFN2 if f else RS_FFN1, t:t + 1]).then_inc(silu_done, 1)

            def projected(jb):
                act.wait_ge(group_done, done("in", jb))
                if jb == 0:
                    act.wait_ge(rs_done, RS_MIX + 1)
                if jb == CB_UP:
                    act.wait_ge(blk_lo_ready, 1)
                for t in range(NT):
                    src = ps[:, 2 * (jb % 2) + t, :]
                    if jb in (Q0, Q1):
                        dst = p_q[:, t, jb * CH:jb * CH + CH].rearrange("p (r two d) -> p two r d", r=GRP, two=2)
                        src = src.rearrange("p (two r d) -> p two r d", r=GRP, two=2)
                    else:
                        buf, half = {KS: (p_kv, 0), KW: (p_kv, 1), KC: (p_kvc, 0), CC_UP: (p_cc, 0), CH_UP: (p_h, 1),
                                     CB_UP: (p_b, 1), CH_LO: (p_h, 0), CB_LO: (p_b, 0)}[jb]
                        dst = buf[:, t, half * CH:half * CH + CH]
                    act.activation(dst, src, ACT.Copy, scale=rs[:, RS_MIX, t:t + 1]).then_inc(proj_done, 1)

            def q_operand(n):
                bank, u = USE["q", n]
                act.wait_ge(full[bank], u + 1)
                act.activation(qT[:, 2 * n:2 * n + 2, :], ps[:, bank, :].rearrange("p (k t) -> p k t", k=2),
                               ACT.Copy, scale=-HD ** -0.5).then_inc(free[bank], 1)

            def kT2_operand(n):
                bank, u = USE["kvd", n]
                v, j0 = n // 2, 2 * (n % 2)
                act.wait_ge(full[bank], u + 1)
                src = ps[:, bank, :].rearrange("p (j t) -> p j t", j=2)
                act.activation(kT2[0:HD, v, j0:j0 + 2, :], src[0:HD, :, :], ACT.Copy)
                act.activation(kT2[HD:P, v, j0:j0 + 2, 0:TOK - 1], src[HD:P, :, 1:TOK],
                               ACT.Copy).then_inc(free[bank], 1)

            def kT_operand(jp):
                bank, u = USE["kT", jp]
                act.wait_ge(full[bank], u + 1)
                act.activation(kT[:, jp, :, :], ps[:, bank, :].rearrange("p (b t) -> p b t", b=2),
                               ACT.Copy).then_inc(free[bank], 1)

            def gate_w_load():
                act.wait_ge(group_done, MIX0)
                act.dma_start(w_gate[:, :, :], w_in[:, :, GATE_COL:GATE_COL + NG]).then_inc(gate_w_landed, 16)

            def gate_weights():
                act.wait_ge(gate_w_landed, 16)
                act.activation(wg_hi[:, :, :], w_gate[:, :, :], ACT.Copy).then_inc(gate_w_hi, 1)

            def gate_rows():
                bank, u = USE["gates",]
                act.wait_ge(full[bank], u + 1)
                act.activation(gT[0:NG, :], ps[0:NG, bank, 0:TOK], ACT.Copy).then_inc(free[bank], 1)

            def blocks_hi():
                act.wait_ge(blk_ready, 1)
                act.activation(blk_hi[:, :, :], blk_f, ACT.Copy).then_inc(blk_hi_ready, 1)

            def gate_exp():
                act.wait_ge(gates_scaled, 1)
                act.activation(den[:, :, :, :], den[:, :, :, :], ACT.Exp, scale=-1.0).then_inc(gates_exp, 1)

            def exps(m):
                t = m // HEADS
                nk = (t + 1) * P
                bank, u = USE["QK", m]
                act.wait_ge(mins_ready, m + 1)
                if m >= 2:
                    act.wait_ge(full[4], USE["PT", m - 2][1] + 1)
                for br in range(2):
                    ins = act.activation(prob[:, m % 2, br * nk:br * nk + nk], ps[:, bank, br * nk:br * nk + nk],
                                         ACT.Exp, bias=mins[:, m, br:br + 1], scale=-1.0,
                                         accum_out=sums[:, m, br:br + 1])
                ins.then_inc(free[bank], 1)

            def u_operand(n):
                bank, u = USE["cu", n]
                act.wait_ge(full[bank], u + 1)
                if n == 2:
                    act.wait_ge(blk_ready, 1)
                act.activation(uT[:, 2 * n:2 * n + 2, 2:TOK + 2], ps[:, bank, :].rearrange("p (k t) -> p k t", k=2),
                               ACT.Copy).then_inc(free[bank], 1)

            def conv_squares(n):
                act.wait_ge(conv_ready, {2: 1, 3: 2, 0: 3, 1: 4}[n])
                act.activation(uT[:, 2 * n:2 * n + 2, 0:TOK], cv(2 * n, 2).rearrange("p (k t) -> p k t", k=2),
                               ACT.Square).then_inc(ysq_ready, 1)

            def conv_operand(n):
                act.wait_ge(conv_ready, {2: 1, 3: 2, 0: 3, 1: 4}[n])
                for c in (2 * n, 2 * n + 1):
                    act.activation(ycT_hi[:, c, :], cv(c), ACT.Copy,
                                   scale=vecs[:, V_GC + c:V_GC + c + 1]).then_inc(ycT_hi_ready, 1)

            def gelu():
                act.wait_ge(gelu_in, 2)
                act.activation(scr[:, CH:2 * CH], scr[:, CH:2 * CH], ACT.Exp,
                               scale=-1.5957691216057308).then_inc(gelu_exp, 1)

            def compressed_exp():
                act.wait_ge(cdiff_ready, 2)
                act.activation(pc[:, :, :, :], pc[:, :, :, :], ACT.Exp, scale=-1.0).then_inc(cexp_ready, 1)

            def compressed_operand(t):
                bank, u = USE["pcT", t]
                act.wait_ge(full[bank], u + 1)
                act.activation(pcT[:, t, :, :], ps[:, bank, 0:TOK].rearrange("p (k t) -> p k t", k=2),
                               ACT.Copy).then_inc(free[bank], 1)

            def att_square():
                act.wait_ge(y_att_ready, 1)
                for t in range(NT):
                    seq(act.activation(junk[:, :], y_att[:, t, :], ACT.Square, accum_out=ssq[:, RS_ATT, t, 0:1]))
                act.sem_inc(ssq_done, 1)

            def att_operand(n):
                scaled_operand(aT_hi, 4 * n, V_GA, [USE["aT", n, b] for b in range(2)])

            def mixer():
                after = {}

                def put(c, *fs):
                    after.setdefault(c, []).extend(fs)

                put(MIX0 + 1, lambda: x_square(RS_MIX, NDC - 1, 2 * NDC))
                put(MIX0 + 4, lambda: root(RS_MIX), gate_w_load)
                put(MIX0 + 5, lambda: x_operand(1, NDC - 1))
                for jb in range(10):
                    put(started(jb) + JD + 1, lambda jb=jb: projected(jb))
                put(started(Q1) + 2, gate_weights)
                put(started(KS) + 3, gate_rows)
                put(started(KS) + 7, gate_exp)
                put(started(KW) + 4, lambda: q_operand(0), lambda: q_operand(1))
                put(started(KW) + 7, lambda: q_operand(2), lambda: q_operand(3))
                put(started(KC) + 8, lambda: kT_operand(0), lambda: kT_operand(1))
                for m in range(2 * HEADS):
                    put(TICK0 + 2 + m, lambda m=m: exps(m))
                    if m in EXTRA:
                        kind, n = EXTRA[m]
                        if kind == "kvd":
                            put(TICK0 + 2 + m, lambda n=n: kT2_operand(n))
                        elif kind == "cu":
                            put(TICK0 + 2 + m, lambda n=n: u_operand(n))
                        else:
                            put(TICK0 + 3 + m, lambda n=n: conv_squares(n), lambda n=n: conv_operand(n))
                put(started(CB_UP) + 1, blocks_hi)
                o = OUT0
                put(o - 1, lambda: u_operand(0), lambda: u_operand(1))
                put(o + 2, lambda: conv_operand(0), lambda: conv_operand(1))
                put(o + 3, lambda: conv_squares(0), lambda: conv_squares(1))
                put(o + 4, gelu)
                put(o + 6, lambda: root(RS_CONV))
                put(o + 11, compressed_exp)
                put(o + 12, lambda: compressed_operand(0), lambda: compressed_operand(1))
                put(o + 15, att_square)
                put(o + 17, lambda: att_operand(0), lambda: att_operand(1))
                put(o + 18, lambda: root(RS_ATT))
                for n in range(NDC - 1):
                    put(AT[("out", NDC + n + 1), 2], lambda n=n: x_square(RS_FFN2, n, 2 * (2 * NDC + n + 1)))
                    put(AT[("out", NDC + n + 1), 0] + JH, lambda n=n: x_operand(2, n))
                return after

            act.wait_ge(vecs_full, 1)
            act.activation(vecs[:, 0:KD], ps[:, 6, 0:KD], ACT.Copy).then_inc(vecs_ready, 1)
            act.wait_ge(vecs_ready, 1)
            ffn(0)
            mix_after = mixer()
            for c in range(MIX0, FFN0[1]):
                hi(c)
                for f in mix_after.pop(c, ()):
                    f()
            for c in sorted(mix_after):
                for f in mix_after[c]:
                    f()
            ffn(1)
            x_square(RS_FINAL, NDC - 1, 8 * NDC)
            root(RS_FINAL)

        @block.vector
        def _(dve):
            steps = [0]

            def seq(ins):
                ins.then_inc(dve_step, 1)
                steps[0] += 1
                dve.wait_ge(dve_step, steps[0])

            tt = nc.vector.tensor_tensor
            stt = nc.vector.scalar_tensor_tensor

            def lo(c, i=None, per=0):
                dve.wait_ge(hi_ready, count(c + 1, i, per))
                s = c % SLOTS
                tt(w_lo[:, s, :, :], raw[:, s, :, :], w_hi[:, s, :, :].bitcast(F32),
                   ALU.subtract).then_inc(lo_ready, 1)

            def job(c, n, i=None, per=0, after={}):
                for j in range(n):
                    lo(c + j, i, per)
                    for f in after.get(j, ()):
                        f()

            OP_X = {0: 0, 1: 2 * (NDC + NFC), 2: 2 * (NDC + NFC + NDC + 2)}
            OP_GU = [2 * NDC, OP_X[2] + 2 * NDC]
            OP_ATT = 2 * (NDC + NFC + NDC)

            def scaled_operand(hi_t, lo_t, tile0, vec0, banks, op0):
                for b, bank in enumerate(banks):
                    dve.wait_ge(operand_hi, op0 + b + 1)
                    for kk in range(2):
                        k = tile0 + 2 * b + kk
                        ins = stt(out=lo_t[:, k, :], in0=ps[:, bank, kk * TOK:kk * TOK + TOK],
                                  scalar=vecs[:, vec0 + k:vec0 + k + 1], in1=hi_t[:, k, :].bitcast(F32),
                                  op0=ALU.mult, op1=ALU.subtract)
                    ins.then_inc(free[bank], 1)

            def x_operand(which, n):
                vec0 = (V_FFN1, V_MIX, V_FFN2)[which]
                scaled_operand(hT_hi, hT_lo, 4 * n, vec0, (4, 5), OP_X[which] + 2 * n)

            def variance(phase, width, ssq_count, cols=NDC):
                dve.wait_ge(ssq_done, ssq_count)
                if cols > 1:
                    seq(nc.vector.tensor_reduce(var[:, phase, :], ssq[:, phase, :, 0:cols], axis=AX.X, op=ALU.add))
                    src = var[:, phase, :]
                else:
                    src = ssq[:, phase, :, 0]
                nc.vector.tensor_scalar(var[:, phase, :], src, 1.0 / width, EPS, ALU.mult,
                                        ALU.add).then_inc(var_done, 1)

            def inverse_root(phase):
                dve.wait_ge(root_done, phase + 1)
                nc.vector.reciprocal(rs[:, phase, :], var[:, phase, :]).then_inc(rs_done, 1)
                dve.wait_ge(rs_done, phase + 1)

            def up(f, n, done, i=None):
                dve.wait_ge(group_done, count(done, i, 2 * JD))
                dve.wait_ge(silu_done, count(2 * (NFC * f + n + 1), i, 2))
                for t in range(NT):
                    stt(out=gu[:, t, :], in0=ps[:, 2 + t, :], scalar=rs[:, RS_FFN2 if f else RS_FFN1, t:t + 1],
                        in1=gu[:, t, :], op0=ALU.mult, op1=ALU.mult).then_inc(gu_done, 1)

            def gu_operand(f, n, i=None):
                for b in range(2):
                    dve.wait_ge(operand_hi, count(OP_GU[f] + 2 * n + b + 1, i, 2))
                    k = 4 * n + 2 * b
                    sl = slice(k, k + 2) if i is None else bass.ds(i * 4 + k, 2)
                    tt(guT_lo[:, sl, :], ps[:, 4 + b, :].rearrange("p (k t) -> p k t", k=2),
                       guT_hi[:, sl, :].bitcast(F32), ALU.subtract).then_inc(free[4 + b], 1)

            def residual(n, done, pair, scale):
                dve.wait_ge(group_done, done)
                for t in range(NT):
                    xs = x[:, t, n * CH:n * CH + CH]
                    stt(out=xs, in0=ps[:, 2 * pair + t, :], scalar=scale(t), in1=xs,
                        op0=ALU.mult, op1=ALU.add).then_inc(resid_done, 1)

            half = lambda t: 0.5

            def ffn(f):
                c = FFN0[f]
                if f == 0:
                    x_operand(0, 0)
                    after = {2: [lambda: x_operand(0, 1)], 4: [lambda: x_operand(0, 2)],
                             6: [lambda: x_operand(0, 3)],
                             7: [lambda: variance(RS_FFN1, DM, NDC), lambda: inverse_root(RS_FFN1)]}
                else:
                    after = {1: [lambda: residual(NDC - 1, FFN0[1], 1, att_scale)],
                             3: [lambda: variance(RS_FFN2, DM, 3 * NDC + 1)],
                             5: [lambda: x_operand(2, NDC - 1)], 6: [lambda: inverse_root(RS_FFN2)]}
                job(c, JD, after=after)
                c += JD
                with dve.Fori(0, NFC - 1) as i:
                    job(c, JD, i, 2 * JD)
                    job(c + JD, JD, i, 2 * JD, after={1: [lambda: up(f, 0, c + JD, i)],
                                                      5: [lambda: gu_operand(f, 0, i)]})
                c += 2 * JD * (NFC - 1)
                job(c, JD)
                c += JD
                for n in range(NDC):
                    if n == 0:
                        after = {1: [lambda: up(f, NFC - 1, c)], 5: [lambda: gu_operand(f, NFC - 1)]}
                    else:
                        after = {1: [lambda: residual(n - 1, c + JF * n, (n - 1) % 2, half)]}
                        if f == 0:
                            after[5] = [lambda: x_operand(1, n - 1)]
                    job(c + JF * n, JF, after=after)

            def rope(x_lo, x_hi, x_all, s_lo, s_hi, s_all, cos, sin, shape_half, shape_all, last_out=None,
                     last_in=None):
                seq(tt(s_lo, x_hi, sin[0].to_broadcast(shape_half), ALU.mult))
                seq(tt(s_hi, x_lo, sin[1].to_broadcast(shape_half), ALU.mult))
                seq(tt(x_all, x_all, cos.to_broadcast(shape_all), ALU.mult))
                if last_out is None:
                    return tt(x_all, x_all, s_all, ALU.add)
                return tt(last_out, last_in(x_all), last_in(s_all), ALU.add)

            def rope_q(t):
                if t == 0:
                    dve.wait_ge(proj_done, 2 * (Q1 + 1))
                v = p_q[:, t, :].rearrange("p (h d) -> p h d", d=HD)
                s = scr[:, :].rearrange("p (h d) -> p h d", d=HD)
                sh, sa = [P, HEADS, HD // 2], [P, HEADS, HD]
                sin = [sin_t[:, t, 0:HD // 2].unsqueeze(1), sin_t[:, t, HD // 2:HD].unsqueeze(1)]
                seq_ins = rope(v[:, :, 0:HD // 2], v[:, :, HD // 2:HD], v, s[:, :, 0:HD // 2], s[:, :, HD // 2:HD], s,
                               cos_t[:, t, :].unsqueeze(1), sin, sh, sa)
                seq_ins.then_inc(q_roped, 1)
                dve.wait_ge(q_roped, t + 1)

            def rope_kc(t):
                if t == 0:
                    dve.wait_ge(proj_done, 2 * (KC + 1))
                v = p_kvc[:, t, 0:KV * HD].rearrange("p (h d) -> p h d", d=HD)
                s = scr[:, 0:KV * HD].rearrange("p (h d) -> p h d", d=HD)
                sh, sa = [P, KV, HD // 2], [P, KV, HD]
                sin = [sin_t[:, t, 0:HD // 2].unsqueeze(1), sin_t[:, t, HD // 2:HD].unsqueeze(1)]
                twice = lambda u: u.unsqueeze(2).to_broadcast([P, KV, 2, HD])
                dst = kvd[:, t, :, :, :].rearrange("p v j (a d) -> p v j a d", a=2)
                rope(v[:, :, 0:HD // 2], v[:, :, HD // 2:HD], v, s[:, :, 0:HD // 2], s[:, :, HD // 2:HD], s,
                     cos_t[:, t, :].unsqueeze(1), sin, sh, sa, dst[:, 0, :, :, :], twice)
                vv = p_kvc[:, t, KV * HD:2 * KV * HD].rearrange("p (h d) -> p h d", d=HD)
                nc.vector.tensor_copy(dst[:, 1, :, :, :], twice(vv)).then_inc(kvd_ready, 1)
                dve.wait_ge(kvd_ready, t + 1)

            def rope_ks(br, t):
                if t == 0:
                    dve.wait_ge(proj_done, 2 * (KS + br + 1))
                v = p_kv[:, t, br * CH:br * CH + KV * HD].rearrange("p (h d) -> p h d", d=HD)
                s = scr[:, 0:KV * HD].rearrange("p (h d) -> p h d", d=HD)
                sh, sa = [P, KV, HD // 2], [P, KV, HD]
                sin = [sin_t[:, t, 0:HD // 2].unsqueeze(1), sin_t[:, t, HD // 2:HD].unsqueeze(1)]
                ins = rope(v[:, :, 0:HD // 2], v[:, :, HD // 2:HD], v, s[:, :, 0:HD // 2], s[:, :, HD // 2:HD], s,
                           cos_t[:, t, :].unsqueeze(1), sin, sh, sa)
                if t:
                    ins.then_inc(ks_roped, 1)
                    dve.wait_ge(ks_roped, br + 1)
                else:
                    seq(ins)

            def blocks():
                for n in range(4):
                    bank, u = USE["kvd", n]
                    dve.wait_ge(free[bank], u + 1)
                dve.wait_ge(pads_zero, 1)
                for v in range(2):
                    toks = kT2[:, v, :, :].rearrange("p j (n s w) -> p s j n w", s=8, w=2)
                    for h in range(2):
                        pe_col = (V_PEK, V_PEV)[v] + 8 * h
                        o = blk_f[:, 8 * h:8 * h + 8, v * KV * NCP:(v + 1) * KV * NCP].rearrange(
                            "p k (j n) -> p k j n", j=KV)[:, :, :, 0:NCMP]
                        pos = vecs[:, pe_col:pe_col + 8].unsqueeze(2).unsqueeze(3).to_broadcast([P, 8, KV, NCMP])
                        ins = tt(o, toks[:, :, :, h:h + NCMP, 0], pos, ALU.add)
                ins.then_inc(blk_ready, 1)

            def gate_weights():
                dve.wait_ge(gate_w_hi, 1)
                tt(wg_lo[:, :, :], w_gate[:, :, :], wg_hi[:, :, :].bitcast(F32), ALU.subtract).then_inc(gate_w_lo, 1)

            def blocks_lo():
                dve.wait_ge(blk_hi_ready, 1)
                tt(blk_lo[:, :, :], blk_f, blk_hi[:, :, :].bitcast(F32), ALU.subtract).then_inc(blk_lo_ready, 1)

            def gates_in():
                bank, u = USE["gatesT",]
                dve.wait_ge(full[bank], u + 1)
                for t in range(NT):
                    ins = nc.vector.tensor_scalar(den[:, t, :, :].rearrange("p h g -> p (h g)"),
                                                  ps[:, bank, t * NG:t * NG + NG], rs[:, RS_MIX, t:t + 1], None,
                                                  ALU.mult)
                ins.then_inc(gates_scaled, 1)
                dve.wait_ge(gates_scaled, 1)
                dve.sem_inc(free[bank], 1)

            def gates_den():
                dve.wait_ge(gates_exp, 1)
                seq(nc.vector.tensor_scalar(den[:, :, :, :], den[:, :, :, :], 1.0, None, ALU.add))

            def score_min(m):
                t = m // HEADS
                nk = (t + 1) * P
                bank, u = USE["QK", m]
                dve.wait_ge(full[bank], u + 1)
                nc.vector.tensor_reduce(mins[:, m, :], ps[:, bank, 0:2 * nk].rearrange("p (b n) -> p b n", b=2),
                                        axis=AX.X, op=ALU.min).then_inc(mins_ready, 1)

            def prob_operand(m):
                t = m // HEADS
                n = 2 * (t + 1) * P
                bank, u = USE["PT", m]
                dve.wait_ge(full[bank], u + 1)
                nc.vector.tensor_copy(probT[:, m % 2, 0:n], ps[:, bank, 0:n]).then_inc(free[bank], 1)

            def weighted(n):
                t, j = divmod(n, KV)
                m = GRP * n
                bank, u = USE["O", n]
                dve.wait_ge(full[bank], u + 1)
                seq(tt(coef[:, :, :], den[:, t, GRP * j:GRP * j + GRP, 1:3], sums[:, m:m + GRP, :], ALU.mult))
                seq(nc.vector.reciprocal(coef[:, :, :], coef[:, :, :]))
                s = scr[:, 0:CH].rearrange("p (h b d) -> p h b d", h=GRP, b=2)
                o = ps[:, bank, :].rearrange("p (h b d) -> p h b d", h=GRP, b=2)
                tt(s, o, coef[:, :, :].unsqueeze(3).to_broadcast([P, GRP, 2, HD]), ALU.mult).then_inc(free[bank], 1)
                dve.wait_ge(free[bank], u + 1)
                seq(tt(y_att[:, t, j * TOK:(j + 1) * TOK].rearrange("p (h d) -> p h d", h=GRP),
                       s[:, :, 0, :], s[:, :, 1, :], ALU.add))

            def conv_input_upper():
                dve.wait_ge(proj_done, 2 * (CH_UP + 1))
                for t in range(NT):
                    xs = p_h[:, t, CH:2 * CH]
                    tt(xs, p_cc[:, t, :], xs, ALU.mult).then_inc(u_ready, 1)

            def conv_input_lower():
                dve.wait_ge(proj_done, 2 * (CH_LO + 1))
                dve.wait_ge(group_done, done("in", CC_LO))
                for t in range(NT):
                    xs = p_h[:, t, 0:CH]
                    stt(out=xs, in0=ps[:, t, :], scalar=rs[:, RS_MIX, t:t + 1], in1=xs, op0=ALU.mult,
                        op1=ALU.mult).then_inc(u_ready, 1)

            def conv_taps(tiles):
                for n in (tiles[0] // 2, tiles[-1] // 2):
                    bank, u = USE["cu", n]
                    dve.wait_ge(free[bank], u + 1)
                w = lambda tap, c: vecs[:, V_CONVW + tap * CT + c:V_CONVW + tap * CT + c + 1]
                if tiles[0] == 4:
                    seq(nc.vector.memset(uT[:, :, 0:2], 0.0))
                for tap in range(3):
                    for c in tiles:
                        if tap == 0:
                            ins = nc.vector.tensor_scalar(cv(c), uT[:, c, 0:TOK], w(0, c), None, ALU.mult)
                        else:
                            ins = stt(out=cv(c), in0=uT[:, c, tap:tap + TOK], scalar=w(tap, c), in1=cv(c),
                                      op0=ALU.mult, op1=ALU.add)
                    seq(ins)

            def conv_gate(n):
                bank, u = USE["cb", n]
                dve.wait_ge(full[bank], u + 1)
                tt(cv(2 * n, 2), ps[:, bank, :], cv(2 * n, 2), ALU.mult).then_inc(conv_ready, 1)
                dve.wait_ge(conv_ready, {2: 1, 3: 2, 0: 3, 1: 4}[n])
                dve.sem_inc(free[bank], 1)

            def conv_operand(n):
                for q, c in enumerate((2 * n, 2 * n + 1)):
                    dve.wait_ge(ycT_hi_ready, {2: 0, 3: 2, 0: 4, 1: 6}[n] + q + 1)
                    stt(out=ycT_lo[:, c, :], in0=cv(c), scalar=vecs[:, V_GC + c:V_GC + c + 1],
                        in1=ycT_hi[:, c, :].bitcast(F32), op0=ALU.mult, op1=ALU.subtract).then_inc(ycT_lo_ready, 1)

            def conv_variance():
                bank, u = USE["css",]
                dve.wait_ge(full[bank], u + 1)
                nc.vector.tensor_scalar(var[:, RS_CONV, :], ps[:, bank, 0:NT], 1.0 / CONV, EPS, ALU.mult,
                                        ALU.add).then_inc(var_done, 1)
                dve.wait_ge(var_done, RS_CONV + 1)
                dve.sem_inc(free[bank], 1)

            hx, hq = scr[:, 0:CH], scr[:, CH:2 * CH]

            def gelu_copy():
                dve.wait_ge(group_done, done("cmp"))
                nc.vector.tensor_copy(hx, ps[:, 2, :]).then_inc(gelu_in, 1)

            def gelu_cube():
                dve.wait_ge(gelu_in, 1)
                seq(tt(hq, hx, hx, ALU.mult))
                seq(nc.vector.tensor_scalar(hq, hq, 0.044715, 1.0, ALU.mult, ALU.add))
                tt(hq, hq, hx, ALU.mult).then_inc(gelu_in, 1)

            def gelu_out():
                dve.wait_ge(gelu_exp, 1)
                seq(nc.vector.tensor_scalar(hq, hq, 1.0, None, ALU.add))
                seq(nc.vector.reciprocal(hq, hq))
                tt(hx, hx, hq, ALU.mult).then_inc(hid_ready, 1)

            def hidden_operand():
                bank, u = USE["hidT",]
                dve.wait_ge(full[bank], u + 1)
                src = ps[:, bank, :].rearrange("p (f m) -> p f m", f=4)
                nc.vector.tensor_copy(hidkT[:, :, :], src[:, 0:2, 0:KV * NCP])
                for f in range(2):
                    v = src[:, 2 + f, KV * NCP:2 * KV * NCP].rearrange("p (j n) -> p j n", j=KV)
                    ins = nc.vector.tensor_copy(hidvT[:, f, :, :, :], v.unsqueeze(2).to_broadcast([P, KV, GRP, NCP]))
                ins.then_inc(free[bank], 1)

            def compressed_operands():
                bank, u = USE["kcvc",]
                dve.wait_ge(full[bank], u + 1)
                seq(nc.vector.memset(kcT[:, :, :, :], 0.0))
                for par in range(2):
                    rows_ = slice(par * HD, par * HD + HD)
                    kc = ps[:, bank, 0:KV * NCP].rearrange("p (jp a n) -> p jp a n", jp=2, a=2)
                    nc.vector.tensor_copy(kcT[rows_, :, par, :], kc[rows_, :, par, :])
                sel = consts[:, C_BMASK:C_BMASK + GRP].unsqueeze(2).to_broadcast([P, GRP, HD])
                for jp in range(2):
                    v = ps[:, bank, HD * (jp + 1):][:, 0:HD]
                    ins = tt(vcb[:, jp, :, :], v.unsqueeze(1).to_broadcast([P, GRP, HD]), sel, ALU.mult)
                ins.then_inc(free[bank], 1)

            def compressed_min():
                bank, u = USE["cs",]
                dve.wait_ge(full[bank], u + 1)
                lows = cmin[:, :, :].rearrange("p t h -> p (t h)")
                seq(nc.vector.tensor_reduce(lows, ps[:, bank, :].rearrange("p (h n) -> p h n", n=NCP), axis=AX.X,
                                            op=ALU.min))
                s = ps[:, bank, :].rearrange("p (q r two n) -> p two q r n", r=GRP, two=2, n=NCP)
                low = lows.rearrange("p (q r two) -> p two q r", r=GRP, two=2)
                dst = pc[:, :, :, :].rearrange("p t (jp two r) n -> p two (t jp) r n", two=2, r=GRP)
                for par in range(2):
                    tt(dst[:, par, :, :, :], s[:, par, :, :, :], low[:, par, :, :].unsqueeze(3).to_broadcast(
                        [P, 4, GRP, NCP]), ALU.subtract).then_inc(cdiff_ready, 1)
                dve.wait_ge(cdiff_ready, 2)
                dve.sem_inc(free[bank], 1)

            def compressed_coef(t):
                dve.wait_ge(cexp_ready, 1)
                seq(nc.vector.tensor_reduce(csum[:, t, :], pc[:, t, :, :], axis=AX.X, op=ALU.add))
                seq(tt(csum[:, t, :], csum[:, t, :], den[:, t, :, 0], ALU.mult))
                seq(nc.vector.reciprocal(csum[:, t, :], csum[:, t, :]))
                seq(nc.vector.tensor_scalar(csum[:, t, :], csum[:, t, :], consts[:, C_VALID + t:C_VALID + t + 1], None,
                                            ALU.mult))

            def compressed_weighted(n):
                t, par = divmod(n, 2)
                bank, u = USE["Oc", n]
                dve.wait_ge(full[bank], u + 1)
                s = scr[:, 0:CH].rearrange("p (jp r d) -> p jp r d", jp=2, d=HD)
                o = ps[:, bank, :].rearrange("p (jp r d) -> p jp r d", jp=2, d=HD)
                c = csum[:, t, :].rearrange("p (jp two r) -> p two jp r", two=2, r=GRP)[:, par, :, :]
                tt(s, o, c.unsqueeze(3).to_broadcast([P, 2, GRP, HD]), ALU.mult).then_inc(free[bank], 1)
                dve.wait_ge(free[bank], u + 1)
                y = y_att[:, t, :].rearrange("p (jp two m) -> p two jp m", two=2, m=GRP * HD)[:, par, :, :]
                ins = tt(y, y, scr[:, 0:CH].rearrange("p (jp m) -> p jp m", jp=2), ALU.add)
                if n == 3:
                    ins.then_inc(y_att_ready, 1)
                else:
                    seq(ins)

            def att_operand(n):
                scaled_operand(aT_hi, aT_lo, 4 * n, V_GA, (4, 5), OP_ATT + 2 * n)

            conv_scale = lambda t: rs[:, RS_CONV, t:t + 1]
            att_scale = lambda t: rs[:, RS_ATT, t:t + 1]

            def mixer():
                after = {}

                def put(c, *fs):
                    after.setdefault(c, []).extend(fs)

                put(MIX0 + 1, lambda: residual(NDC - 1, MIX0, 1, half))
                put(MIX0 + 3, lambda: variance(RS_MIX, DM, 2 * NDC))
                put(MIX0 + 5, lambda: x_operand(1, NDC - 1))
                put(MIX0 + 6, lambda: inverse_root(RS_MIX))
                put(started(Q1) + 3, gate_weights)
                put(started(KS) + 3, lambda: rope_q(0))
                put(started(KS) + 6, lambda: rope_q(1))
                put(started(KS) + 7, gates_in)
                put(started(KW) + 1, gates_den)
                for t in range(NT):
                    put(started(KW) + 3 + t, lambda t=t: rope_ks(0, t))
                    put(started(KC) + 3 + t, lambda t=t: rope_ks(1, t))
                for m in range(2 * HEADS + 2):
                    c = TICK0 + 2 + m
                    if 1 <= m <= 2 * HEADS:
                        put(c, lambda m=m: prob_operand(m - 1))
                    if m < 2 * HEADS:
                        put(c, lambda m=m: score_min(m))
                    if m >= 2 and (m - 2) % GRP == GRP - 1:
                        put(c, lambda n=(m - 2) // GRP: weighted(n))
                    if m in EXTRA and EXTRA[m][0] == "cb":
                        put(c, lambda n=EXTRA[m][1]: conv_gate(n))
                        put(c + 2, lambda n=EXTRA[m][1]: conv_operand(n))
                put(started(CC_UP) + 3, lambda: rope_kc(0))
                put(started(CC_UP) + 5, lambda: rope_kc(1))
                put(started(CB_UP) - 1, blocks)
                put(started(CB_UP) + 2, blocks_lo)
                put(started(CB_UP) + 4, conv_input_upper)
                put(TICK0 + 3 + max(m for m in EXTRA if EXTRA[m][0] == "cu"), lambda: conv_taps([4, 5, 6, 7]))
                o = OUT0
                put(o - 4, conv_input_lower)
                put(o + 1, gelu_copy, lambda: conv_taps([0, 1, 2, 3]), lambda: conv_gate(0), lambda: conv_gate(1))
                put(o + 2, lambda: conv_operand(0), lambda: conv_operand(1))
                put(o + 4, gelu_cube)
                put(o + 5, gelu_out)
                put(o + 6, conv_variance)
                put(o + 7, lambda: inverse_root(RS_CONV), lambda: residual(0, done("out", 0), 0, conv_scale),
                    hidden_operand)
                put(o + 9, compressed_operands)
                put(o + 10, compressed_min)
                put(o + 12, lambda: compressed_coef(0), lambda: compressed_coef(1))
                put(o + 14, lambda: compressed_weighted(0), lambda: compressed_weighted(1))
                put(o + 15, lambda: compressed_weighted(2), lambda: compressed_weighted(3))
                put(o + 17, lambda: att_operand(0), lambda: att_operand(1))
                put(o + 18, lambda: variance(RS_ATT, CONV, 2 * NDC + 1, cols=1))
                put(o + 19, lambda: inverse_root(RS_ATT))
                for n in range(1, 2 * NDC - 1):
                    put(done("out", n) + (0 if n == 1 else 1), lambda n=n: residual(
                        n % NDC, done("out", n), n % 2, conv_scale if n < NDC else att_scale))
                for n in range(NDC - 1):
                    put(AT[("out", NDC + n + 1), 0] + JH, lambda n=n: x_operand(2, n))
                return after

            ffn(0)
            mix_after = mixer()
            for c in range(MIX0, FFN0[1]):
                lo(c)
                for f in mix_after.pop(c, ()):
                    f()
            for c in sorted(mix_after):
                for f in mix_after[c]:
                    f()
            ffn(1)
            residual(NDC - 1, END, 1, half)
            variance(RS_FINAL, DM, 4 * NDC + 1)
            inverse_root(RS_FINAL)
            dve.wait_ge(g_fin_landed, 16)
            for piece in range(4):
                t, h = piece // 2, piece % 2
                cols = slice(h * CONV, (h + 1) * CONV)
                stt(out=y_fin[:, t, cols], in0=x[:, t, cols], scalar=rs[:, RS_FINAL, t:t + 1], in1=g_fin[:, cols],
                    op0=ALU.mult, op1=ALU.mult).then_inc(final_ready, 1)


def shape_constants():
    import numpy as np
    c = np.zeros((P, NCONST), np.float32)
    row = np.arange(P)
    c[:, C_ID:C_ID + P] = np.eye(P, dtype=np.float32)
    c[:, C_CAUSAL:C_CAUSAL + P] = np.where(row[None, :] > row[:, None], BIG, 0.0)
    for t in range(NT):
        pos = t * P + row
        end = np.arange(NCP) * CMP_STRIDE + CMP_BLOCK - 1
        masked = (end[None, :] > pos[:, None]) | (np.arange(NCP) >= NCMP)[None, :]
        c[:, C_CMASK + t * NCP:C_CMASK + (t + 1) * NCP] = np.where(masked, BIG, 0.0)
        c[:, C_VALID + t] = pos >= CMP_BLOCK - 1
        inv = np.float32(10000.0) ** (-np.arange(0, HD, 2, dtype=np.float32) / np.float32(HD))
        ang = pos.astype(np.float32)[:, None] * inv[None, :]
        cos, sin = np.cos(ang), np.sin(ang)
        c[:, C_COS + t * HD:C_COS + (t + 1) * HD] = np.concatenate([cos, cos], 1)
        c[:, C_SIN + t * HD:C_SIN + (t + 1) * HD] = np.concatenate([-sin, sin], 1)
    for h in range(GRP):
        c[:, C_BMASK + h] = (row // NCP) % GRP == h
    c[:, C_ONE] = 1.0
    return c


_INS = ['x', 'ffn1_norm', 'ffn1_wg', 'ffn1_wu', 'ffn1_wd', 'mix_norm', 'w_in', 'conv_w', 'cmp_k_w1', 'cmp_k_w2',
        'cmp_k_pe', 'cmp_v_w1', 'cmp_v_w2', 'cmp_v_pe', 'conv_out_norm', 'attn_out_norm', 'w_out', 'ffn2_norm',
        'ffn2_wg', 'ffn2_wu', 'ffn2_wd', 'final_norm']


def kernel(**inputs):
    import numpy as _np
    import concourse.bacc as _bacc
    from concourse import mybir as _mybir
    from concourse.bass_utils import run_bass_kernel_spmd as _run

    nc = _bacc.Bacc("TRN2", target_bir_lowering=False, num_devices=1)
    arrays, args = {}, {}
    for name in _INS + ["shape_consts"]:
        v = shape_constants() if name == "shape_consts" else _np.ascontiguousarray(inputs[name])
        arrays[f"in_{name}_dram"] = v
        args[name] = nc.dram_tensor(f"in_{name}_dram", v.shape, _mybir.dt.from_np(v.dtype), kind="ExternalInput").ap()
    out = nc.dram_tensor("out_0_dram", (1, TOK, DM), _mybir.dt.from_np(_np.dtype("float32")),
                         kind="ExternalOutput").ap()
    build_program(nc, args, out)
    r = _run(nc, [arrays], core_ids=[0])
    return r.results[0]["out_0_dram"]
```

```python
import concourse.bass as bass
from concourse import mybir
from contextlib import ExitStack

F32 = mybir.dt.float32
F32R = mybir.dt.float32r
BF16 = mybir.dt.bfloat16
ALU = mybir.AluOpType
ACT = mybir.ActivationFunctionType
AX = mybir.AxisListType

P = 128
TOK = 256
NT = TOK // P
DM = 2048
FF = 5632
CH = 512
KD = DM // P
KF = FF // P
NFC = FF // CH
NDC = DM // CH
GK = 2
SLOTS = 4
CONV = 1024
CT = CONV // P
HEADS, KV, GRP, HD = 16, 4, 4, 64
CMP_BLOCK, CMP_STRIDE, CMP_HID = 32, 16, 256
NCMP = (TOK - CMP_BLOCK) // CMP_STRIDE + 1
NCP = 16
EPS = 1e-6
BIG = 1e30

JD = KD // GK
JF = KF // GK
JH = CT // GK
FFN_GROUPS = 2 * NFC * JD + NDC * JF
MIX0 = FFN_GROUPS
N_IN = 11

IN_COL = [3072, 3584, 4608, 5120, 4096, 2560, 512, 1536, 0, 1024, 2048]
Q0, Q1, KS, KW, KC, CC_UP, CH_UP, CB_UP, CH_LO, CB_LO, CC_LO = range(N_IN)


def mixer_order():
    order = [(("in", jb), j) for jb in range(N_IN - 1) for j in range(JD)]
    order += [(("in", N_IN - 1), j) for j in range(JD // 2)]
    for j in range(JD // 2):
        order += [(("in", N_IN - 1), JD // 2 + j), (("cmp",), j)]
    order += [(("cmp",), j) for j in range(JD // 2, JD)]
    for half in range(2):
        order += [(("out", n), 2 * half + j) for n in range(2) for j in range(JH // 2)]
    order += [(("out", n), j) for n in range(2, 2 * NDC) for j in range(JH)]
    return order


MIX_ORDER = mixer_order()
AT = {key: MIX0 + n for n, key in enumerate(MIX_ORDER)}
FFN0 = [0, MIX0 + len(MIX_ORDER)]
END = FFN0[1] + FFN_GROUPS
OUT0 = AT[("out", 0), 0]


WARM = [9, 11]
TICK0 = AT[("in", CC_UP), 1]


def started(jb):
    return AT[("in", jb), 0]


def done(*job):
    return max(c for (jb, _), c in AT.items() if jb == job) + 1


GATE_COL = 5632
NG = 3 * HEADS
CONV_K_ORDER = [2, 3, 0, 1]

V_FFN1, V_MIX, V_FFN2, V_CONVW, V_GC, V_GA, V_PEK, V_PEV, NVEC = 0, 16, 32, 48, 72, 80, 88, 104, 120

C_ID, C_CAUSAL, C_CMASK, C_BMASK, C_VALID, C_COS, C_SIN, C_ONE = 0, 128, 256, 288, 292, 294, 422, 550
NCONST = 551

RS_FFN1, RS_MIX, RS_CONV, RS_ATT, RS_FFN2, RS_FINAL = range(6)


def mixer_banks():
    uses = [(("gates",), 5), (("gatesT",), 5)]
    uses += [(("q", n), 6 + n % 2) for n in range(4)]
    uses += [(("kT", 0), 6), (("kT", 1), 7)]
    extra = {8 + n: ("kvd", n) for n in range(4)}
    extra.update({21: ("cu", 2), 22: ("cu", 3), 27: ("cb", 2), 28: ("cb", 3)})
    for m in range(2 * HEADS + 2):
        if m >= 2 and (m - 2) % GRP == 0:
            uses.append((("O", (m - 2) // GRP), 5))
        if 1 <= m <= 2 * HEADS:
            uses.append((("PT", m - 1), 4))
        if m < 2 * HEADS:
            uses.append((("QK", m), 6 + m % 2))
        if m in extra:
            uses.append((extra[m], 6 + (m + 1) % 2))
    uses += [(("cb", 0), 6), (("cb", 1), 7), (("cu", 0), 4), (("cu", 1), 5), (("css",), 5), (("hidT",), 6)]
    uses += [ (("kcvc",), 7), (("cs",), 6), (("pcT", 0), 7), (("pcT", 1), 6)]
    uses += [(("Oc", 0), 7), (("Oc", 1), 6), (("Oc", 2), 7), (("Oc", 3), 6)]
    uses += [(("aT", n, b), 4 + 2 * n + b) for n in range(2) for b in range(2)]
    first = {4: NDC + NFC + NDC, 5: NDC + NFC + NDC, 6: 0, 7: 0}
    seen, table = dict(first), {}
    for key, bank in uses:
        table[key] = (bank, seen[bank])
        seen[bank] += 1
    return table, extra, seen


def count(c, i=None, per=0):
    return c if i is None else i * per + c


def build_program(nc, a, out):
    USE, EXTRA, seen = mixer_banks()
    X_USE = {4: (0, NDC + NFC, seen[4]), 5: (0, NDC + NFC, seen[5])}
    GU_USE = {4: (NDC, seen[4] + NDC), 5: (NDC, seen[5] + NDC)}

    def operand_use(kind, which, b, n=0):
        return {"x": X_USE, "gu": GU_USE}[kind][4 + b][which] + n

    rows = lambda w: w.rearrange("(k p) n -> p k n", p=P)
    wg = [rows(a["ffn1_wg"][0]), rows(a["ffn2_wg"][0])]
    wu = [rows(a["ffn1_wu"][0]), rows(a["ffn2_wu"][0])]
    wd = [rows(a["ffn1_wd"][0]), rows(a["ffn2_wd"][0])]
    w_in = rows(a["w_in"][0])
    w_out = rows(a["w_out"][0])
    w1 = [a[f"cmp_{n}_w1"][0].rearrange("(k l) d f -> (l d) k f", l=2) for n in "kv"]
    w2 = [a[f"cmp_{n}_w2"][0].rearrange("(k p) d -> p k d", p=P) for n in "kv"]
    x_in = a["x"][0].rearrange("(t p) d -> p t d", p=P)
    y_out = out[0].rearrange("(t p) d -> p t d", p=P)

    at = [(nc.sbuf_base + 63) // 64 * 64]
    limit = nc.sbuf_usable_end

    def sb(name, shape, dt=F32):
        size = 2 if dt == BF16 else 4
        for n in shape[1:]:
            size *= n
        t = nc.alloc_sbuf_tensor_at(name, shape, dt, offset=at[0])
        at[0] += (size + 31) // 32 * 32
        assert at[0] <= limit, (name, at[0], limit)
        return t

    consts = sb("consts", [P, NCONST])
    vec_rows = sb("vec_rows", [P, P])
    vecs = sb("vecs", [P, NVEC])
    ident_b = sb("ident_b", [P, P], BF16)
    causal_b = sb("causal_b", [P, 2, P], BF16)
    cmask_b = sb("cmask_b", [P, NT, HEADS, NCP], BF16)
    w2k = sb("w2k", [P, 2, 2, HD])
    w2v = sb("w2v", [P, 2, HD])
    ssq = sb("ssq", [P, 6, NT, NDC])
    var = sb("var", [P, 6, NT])
    rs = sb("rs", [P, 6, NT])
    junk = sb("junk", [P, CONV], BF16)
    x = sb("x", [P, NT, DM])
    raw = sb("raw", [P, SLOTS, GK, CH])
    w_hi = sb("w_hi", [P, SLOTS, GK, CH], F32R)
    w_lo = sb("w_lo", [P, SLOTS, GK, CH], F32R)
    h_at = at[0]
    hT_hi = sb("hT_hi", [P, KD, TOK], F32R)
    hT_lo = sb("hT_lo", [P, KD, TOK], F32R)
    zone = at[0]
    at[0] = h_at
    g_fin = sb("g_fin", [P, DM])
    at[0] = h_at + 4 * KD * TOK
    y_fin = sb("y_fin", [P, NT, DM])
    at[0] = zone
    guT_hi = sb("guT_hi", [P, KF, TOK], F32R)
    guT_lo = sb("guT_lo", [P, KF, TOK], F32R)
    gu = sb("gu", [P, NT, CH])
    at[0] = zone
    y_at = at[0]
    p_cc = sb("p_cc", [P, NT, CH])
    p_kvc = sb("p_kvc", [P, NT, CH])
    p_q = sb("p_q", [P, NT, CONV])
    p_kv = sb("p_kv", [P, NT, 2 * CH])
    p_h = sb("p_h", [P, NT, CONV])
    p_b = sb("p_b", [P, NT, CONV])
    uT = sb("uT", [P, CT, TOK + 2])
    ycT_lo = sb("ycT_lo", [P, CT, TOK], F32R)
    blk_at = at[0]
    blk_hi = sb("blk_hi", [P, KD, P], F32R)
    blk_lo = sb("blk_lo", [P, KD, P], F32R)
    qk_at = at[0]
    qT = sb("qT", [P, 8, TOK])
    kT = sb("kT", [P, 2, 2, TOK])
    prob = sb("prob", [P, 2, CH])
    probT = sb("probT", [P, 2, CH])
    scr = sb("scr", [P, CONV])
    den = sb("den", [P, NT, HEADS, 3])
    mins = sb("mins", [P, 2 * HEADS, 2])
    sums = sb("sums", [P, 2 * HEADS, 2])
    coef = sb("coef", [P, GRP, 2])
    cmin = sb("cmin", [P, NT, HEADS])
    csum = sb("csum", [P, NT, HEADS])
    top = at[0]
    at[0] = y_at
    ycT_hi = sb("ycT_hi", [P, CT, TOK], F32R)
    y_att = p_q
    blk_f = p_b[:, :, :].rearrange("p t (k m) -> p (t k) m", m=P)
    kvd = p_h[:, :, :].rearrange("p t (v j d) -> p t v j d", v=2, j=KV)
    kT2 = uT[:, :, 0:TOK].rearrange("p (v j) t -> p v j t", v=2)
    at[0] = qk_at
    aT_hi = sb("aT_hi", [P, CT, TOK], F32R)
    aT_lo = sb("aT_lo", [P, CT, TOK], F32R)
    at[0] = blk_at
    w_gate = sb("w_gate", [P, KD, NG])
    wg_hi = sb("wg_hi", [P, KD, NG], F32R)
    wg_lo = sb("wg_lo", [P, KD, NG], F32R)
    gT = sb("gT", [P, TOK])
    at[0] = blk_at
    hidkT = sb("hidkT", [P, 2, KV * NCP])
    hidvT = sb("hidvT", [P, 2, KV, GRP, NCP])
    kcT = sb("kcT", [P, 2, 2, NCP])
    vcb = sb("vcb", [P, 2, GRP, HD])
    pc = sb("pc", [P, NT, HEADS, NCP])
    pcT = sb("pcT", [P, NT, 2, P])
    assert at[0] <= qk_at
    at[0] = top

    ident = consts[:, C_ID:C_ID + P]
    cos_t = consts[:, C_COS:C_COS + NT * HD].rearrange("p (t d) -> p t d", t=NT)
    sin_t = consts[:, C_SIN:C_SIN + NT * HD].rearrange("p (t d) -> p t d", t=NT)
    ones = consts[:, C_ONE:C_ONE + 1]

    def cv(c):
        return p_h[:, c % 2, c // 2 * TOK:c // 2 * TOK + TOK]

    def cv_pair(n):
        return p_h[:, :, n * TOK:n * TOK + TOK]

    ctx = ExitStack()
    with ctx:
        ps = ctx.enter_context(nc.psum_tensor("ps", [P, 8, CH], F32))
        sem = lambda n: ctx.enter_context(nc.semaphore(n))

        landed = [sem(f"landed{s}") for s in range(SLOTS)]
        hi_ready = sem("hi_ready")
        lo_ready = sem("lo_ready")
        group_done = sem("group_done")
        x_half_landed = sem("x_half_landed")
        x_landed = [sem(f"x_landed{n}") for n in range(NDC)]
        warm_ready = sem("warm_ready")
        warm_done = sem("warm_done")
        ident_landed = sem("ident_landed")
        gains_landed = sem("gains_landed")
        consts_landed = sem("consts_landed")
        small_landed = sem("small_landed")
        gate_w_landed = sem("gate_w_landed")
        g_fin_landed = sem("g_fin_landed")
        masks_ready = sem("masks_ready")
        vecs_full = sem("vecs_full")
        vecs_ready = sem("vecs_ready")
        full = {b: sem(f"bank_full{b}") for b in (4, 5, 6, 7)}
        free = {b: sem(f"bank_free{b}") for b in (4, 5, 6, 7)}
        operand_hi = sem("operand_hi")
        ssq_done = sem("ssq_done")
        var_done = sem("var_done")
        root_done = sem("root_done")
        rs_done = sem("rs_done")
        silu_done = sem("silu_done")
        gu_done = sem("gu_done")
        resid_done = sem("resid_done")
        proj_done = sem("proj_done")
        q_roped = sem("q_roped")
        kvd_ready = sem("kvd_ready")
        ks_roped = sem("ks_roped")
        kT2_ready = sem("kT2_ready")
        pads_zero = sem("pads_zero")
        blk_ready = sem("blk_ready")
        blk_hi_ready = sem("blk_hi_ready")
        blk_lo_ready = sem("blk_lo_ready")
        gates_scaled = sem("gates_scaled")
        gate_w_hi = sem("gate_w_hi")
        gate_w_lo = sem("gate_w_lo")
        gates_exp = sem("gates_exp")
        mins_ready = sem("mins_ready")
        u_ready = sem("u_ready")
        tap0_ready = sem("tap0_ready")
        conv_ready = sem("conv_ready")
        ysq_ready = sem("ysq_ready")
        ysum_ready = sem("ysum_ready")
        pool_step = sem("pool_step")
        ycT_hi_ready = sem("ycT_hi_ready")
        ycT_lo_ready = sem("ycT_lo_ready")
        gelu_in = sem("gelu_in")
        gelu_exp = sem("gelu_exp")
        hid_ready = sem("hid_ready")
        cdiff_ready = sem("cdiff_ready")
        cexp_ready = sem("cexp_ready")
        y_att_ready = sem("y_att_ready")
        first_tile_done = sem("first_tile_done")
        final_ssq = [sem(f"final_ssq{t}") for t in range(NT)]
        final_var = [sem(f"final_var{t}") for t in range(NT)]
        final_root = [sem(f"final_root{t}") for t in range(NT)]
        final_rs = [sem(f"final_rs{t}") for t in range(NT)]
        xg_ready = sem("xg_ready")
        final_act = sem("final_act")
        final_dve = sem("final_dve")
        stored = sem("stored")
        act_step = sem("act_step")
        dve_step = sem("dve_step")

        def landed_value(c, i=None, per=0):
            extra = sum(AT[("cmp",), j] <= c and AT[("cmp",), j] % SLOTS == c % SLOTS for j in range(JD))
            return count(16 * (c // SLOTS + 1 + extra), i, 16 * per // SLOTS)

        block = ctx.enter_context(nc.Block())

        @block.sync
        def _(sp):
            def load(c, src, i=None, per=0, halves=None):
                if c >= SLOTS:
                    sp.wait_ge(lo_ready, count(c - SLOTS + 1, i, per))
                s = c % SLOTS
                if halves is None:
                    sp.dma_start(raw[:, s, :, :], src).then_inc(landed[s], 16)
                else:
                    sp.dma_start(raw[:, s, :, 0:CMP_HID], halves[0]).then_inc(landed[s], 16)
                    sp.dma_start(raw[:, s, :, CMP_HID:CH], halves[1]).then_inc(landed[s], 16)

            def load_x(n):
                lo = n * CH
                if n == 0:
                    lo = CH // 2
                    sp.dma_start(x[:, :, 0:lo], x_in[:, :, 0:lo]).then_inc(x_half_landed, 16)
                sp.dma_start(x[:, :, lo:n * CH + CH], x_in[:, :, lo:n * CH + CH]).then_inc(x_landed[n], 16)

            def ffn(f):
                c = FFN0[f]
                for j in range(JD):
                    if f == 0 and j % 2 == 0:
                        load_x(j // 2)
                    load(c + j, wg[f][:, GK * j:GK * j + GK, 0:CH])
                c += JD
                with sp.Fori(0, NFC - 1) as i:
                    for j in range(JD):
                        load(c + j, wu[f][:, GK * j:GK * j + GK, bass.ds(i * CH, CH)], i, 2 * JD)
                    for j in range(JD):
                        load(c + JD + j, wg[f][:, GK * j:GK * j + GK, bass.ds(i * CH + CH, CH)], i, 2 * JD)
                c += 2 * JD * (NFC - 1)
                for j in range(JD):
                    load(c + j, wu[f][:, GK * j:GK * j + GK, (NFC - 1) * CH:FF])
                c += JD
                for n in range(NDC):
                    if f == 1 and n == 1:
                        sp.wait_ge(group_done, c)
                        sp.dma_start(g_fin[:, :], a["final_norm"].partition_broadcast(P)).then_inc(g_fin_landed, 16)
                    for j in range(JF):
                        load(c + JF * n + j, wd[f][:, GK * j:GK * j + GK, n * CH:n * CH + CH])

            ffn(0)
            for (job, j), c in AT.items():
                k = slice(GK * j, GK * j + GK)
                if job[0] == "in":
                    load(c, w_in[:, k, IN_COL[job[1]]:IN_COL[job[1]] + CH])
                elif job[0] == "cmp":
                    load(c, None, halves=(w1[0][:, k, :], w1[1][:, k, :]))
                else:
                    half, n = divmod(job[1], NDC)
                    k = GK * (JH + j if half else CONV_K_ORDER[j])
                    load(c, w_out[:, k:k + GK, n * CH:(n + 1) * CH])
            ffn(1)
            for t in range(NT):
                for h in range(2):
                    for q in range(2):
                        sp.wait_ge((final_dve, final_act)[h], 2 * t + q + 1)
                        cols = slice((2 * h + q) * CH, (2 * h + q + 1) * CH)
                        sp.dma_start(y_out[:, t, cols], y_fin[:, t, cols]).then_inc(stored, 16)
            sp.wait_ge(stored, 16 * 4 * NT)

        @block.gpsimd
        def _(pool):
            small = [(V_MIX, KD, a["mix_norm"].rearrange("l (k p) -> (l k) p", p=P)),
                     (V_FFN2, KD, a["ffn2_norm"].rearrange("l (k p) -> (l k) p", p=P)),
                     (V_CONVW, 3 * CT, a["conv_w"].rearrange("l w (k p) -> (l w k) p", p=P)),
                     (V_GC, CT, a["conv_out_norm"].rearrange("l (k p) -> (l k) p", p=P)),
                     (V_GA, CT, a["attn_out_norm"].rearrange("l (k p) -> (l k) p", p=P)),
                     (V_PEK, KD, a["cmp_k_pe"].rearrange("l (k w) d -> (l k) (w d)", w=2)),
                     (V_PEV, KD, a["cmp_v_pe"].rearrange("l (k w) d -> (l k) (w d)", w=2))]
            pool.wait_ge(hi_ready, JD - 2)
            pool.dma_start(consts[:, P:NCONST], a["shape_consts"][:, P:NCONST]).then_inc(consts_landed, 16)
            for row, n, src in small:
                pool.dma_start(vec_rows[row:row + n, :], src).then_inc(small_landed, 16)
            for half in range(2):
                pool.dma_start(w2k[:, :, half, :], w2[0]).then_inc(small_landed, 16)
            pool.dma_start(w2v[:, :, :], w2[1]).then_inc(small_landed, 16)
            pool.wait_ge(ident_landed, 16)
            pool.wait_ge(consts_landed, 16)
            pool.tensor_copy(ident_b[:, :], ident)
            for br in range(2):
                pool.tensor_copy(causal_b[:, br, :], consts[:, C_CAUSAL:C_CAUSAL + P])
            cm = consts[:, C_CMASK:C_CMASK + NT * NCP].rearrange("p (t n) -> p t n", t=NT)
            for t in range(NT):
                ins = pool.tensor_copy(cmask_b[:, t, :, :], cm[:, t, :].unsqueeze(1).to_broadcast([P, HEADS, NCP]))
            ins.then_inc(masks_ready, 1)
            pool.wait_ge(group_done, MIX0)
            pool.memset(blk_f, 0.0).then_inc(pads_zero, 1)
            ysq = lambda c: uT[:, c:c + 2, 0:TOK]
            pool.wait_ge(ysq_ready, 2)
            pool.tensor_tensor(ysq(4), ysq(4), ysq(6), ALU.add).then_inc(pool_step, 1)
            pool.wait_ge(ysq_ready, 4)
            pool.tensor_tensor(ysq(0), ysq(0), ysq(2), ALU.add).then_inc(pool_step, 1)
            pool.wait_ge(pool_step, 2)
            pool.tensor_tensor(ysq(0), ysq(0), ysq(4), ALU.add).then_inc(ysum_ready, 1)

        @block.tensor
        def _(pe):
            mm = nc.tensor.matmul

            def group(c, i, per, hi, lo, k, banks, first, last, tiles=range(NT), signal=group_done):
                pe.wait_ge(lo_ready, count(c + 1, i, per))
                s = c % SLOTS
                for kk in range(GK):
                    for t, bank in enumerate(banks):
                        if t not in tiles:
                            continue
                        o = ps[:, bank, :]
                        x_hi = hi[:, k + kk, t * P:t * P + P]
                        x_lo = lo[:, k + kk, t * P:t * P + P]
                        mm(o, x_hi, w_hi[:, s, kk, :], start=first and kk == 0, stop=False)
                        mm(o, x_hi, w_lo[:, s, kk, :], start=False, stop=False)
                        ins = mm(o, x_lo, w_hi[:, s, kk, :], start=False, stop=last and kk == GK - 1)
                if signal is not None:
                    ins.then_inc(signal, 1)

            def job(c, n, hi, lo, pair, i=None, per=0, after={}, before={}, ends=True):
                for j in range(n):
                    for f in before.get(j, ()):
                        f()
                    group(c + j, i, per, hi, lo, GK * j, [2 * pair, 2 * pair + 1], j == 0, ends and j == n - 1)
                    for f in after.get(j, ()):
                        f()

            def to_bank(bank, n, i=None, per=0):
                if n:
                    pe.wait_ge(free[bank], count(n, i, per))

            def transposes(bank, pieces):
                for o, src in pieces:
                    ins = pe.transpose(ps[:, bank, o:o + P], src, ident)
                ins.then_inc(full[bank], 1)

            def x_transposes(which, n):
                if which == 0:
                    pe.wait_ge(x_half_landed if n == 0 else x_landed[n], 16)
                else:
                    pe.wait_ge(resid_done, 2 * (NDC * (1 if which == 1 else 3) - NDC + n + 1))
                for b in range(2):
                    if which == n == 0 and b == 1:
                        pe.wait_ge(gains_landed, 16)
                        pe.transpose(ps[:, 6, 0:KD], vec_rows[0:KD, :], consts[0:KD, 0:KD]).then_inc(vecs_full, 1)
                        pe.wait_ge(x_landed[0], 16)
                    to_bank(4 + b, operand_use("x", which, b, n))
                    transposes(4 + b, [(kk * TOK + t * P, x[:, t, (4 * n + 2 * b + kk) * P:][:, 0:P])
                                       for kk in range(2) for t in range(NT)])

            def x_operand(which, j):
                pe.wait_ge(free[4 + j % 2], operand_use("x", which, j % 2, j // 2) + 1)

            def gu_transposes(f, n, i=None):
                pe.wait_ge(gu_done, count(2 * (NFC * f + n + 1), i, 2))
                for b in range(2):
                    to_bank(4 + b, operand_use("gu", f, b, n), i, 1)
                    transposes(4 + b, [(kk * TOK + t * P, gu[:, t, (2 * b + kk) * P:][:, 0:P])
                                       for kk in range(2) for t in range(NT)])

            def gu_operand(f, j):
                pe.wait_ge(free[4 + j % 2], operand_use("gu", f, j % 2, j // 2) + 1)

            def vector_transposes():
                pe.wait_ge(small_landed, 16 * 10)
                pe.transpose(ps[:, 7, 0:NVEC], vec_rows[0:NVEC, :], consts[0:NVEC, 0:NVEC]).then_inc(vecs_full, 1)

            def warm_up(n):
                for _ in range(WARM[n]):
                    ins = mm(ps[:, 7, :], junk[:, 0:P], junk[:, 0:CH], start=True, stop=True)
                ins.then_inc(warm_done, 1)
                pe.wait_ge(warm_done, n + 1)

            def ffn(f):
                which = 0 if f == 0 else 2
                c = FFN0[f]
                before = {j: [lambda j=j: x_operand(which, j)] for j in range(JD)}
                if f == 0:
                    x_transposes(0, 0)
                    warm_up(1)
                    after = {2 * n - 2: [lambda n=n: x_transposes(0, n)] for n in range(1, NDC)}
                else:
                    after = {3: [lambda: x_transposes(2, NDC - 1)]}
                job(c, JD, hT_hi, hT_lo, 0, after=after, before=before)
                c += JD
                with pe.Fori(0, NFC - 1) as i:
                    job(c, JD, hT_hi, hT_lo, 1, i, 2 * JD)
                    pe.wait_ge(silu_done, count(2 * (NFC * f + 1), i, 2))
                    job(c + JD, JD, hT_hi, hT_lo, 0, i, 2 * JD, after={3: [lambda: gu_transposes(f, 0, i)]})
                c += 2 * JD * (NFC - 1)
                job(c, JD, hT_hi, hT_lo, 1)
                c += JD
                pe.wait_ge(silu_done, 2 * NFC * (f + 1))
                for n in range(NDC):
                    if n == 0:
                        before = {0: [lambda: gu_operand(f, JF - 4), lambda: gu_operand(f, JF - 3)]}
                        before.update({j: [lambda j=j: gu_operand(f, j)] for j in (JF - 2, JF - 1)})
                        after = {3: [lambda: gu_transposes(f, NFC - 1)]}
                        if f == 0:
                            after[6] = [vector_transposes]
                    else:
                        before = {}
                        if f == 0:
                            after = {3: [lambda: x_transposes(1, n - 1)]}
                        else:
                            after = {3: [lambda: pe.wait_ge(resid_done, 2 * (3 * NDC + n))]}
                    last = f == 1 and n == NDC - 1
                    job(c + JF * n, JF - SLOTS * last, guT_hi, guT_lo, n % 2, before=before, after=after,
                        ends=not last)
                    if last:
                        for t in range(NT):
                            for j in range(JF - SLOTS, JF):
                                ends = j == JF - 1
                                signal = group_done if t == NT - 1 else first_tile_done if ends else None
                                group(c + JF * n + j, None, 0, guT_hi, guT_lo, GK * j, [2, 3], False, ends,
                                      tiles=[t], signal=signal)

            def q_transposes(n):
                bank, u = USE["q", n]
                if n == 0:
                    pe.wait_ge(q_roped, NT)
                to_bank(bank, u)
                transposes(bank, [(kk * TOK + t * P, p_q[:, t, (2 * n + kk) * P:][:, 0:P])
                                  for kk in range(2) for t in range(NT)])

            def kvd_transposes(n):
                bank, u = USE["kvd", n]
                pe.wait_ge(kvd_ready, NT)
                to_bank(bank, u)
                transposes(bank, [(kk * TOK + t * P, kvd[:, t, n // 2, 2 * (n % 2) + kk, :])
                                  for kk in range(2) for t in range(NT)])

            def gates():
                bank, u = USE["gates",]
                pe.wait_ge(gate_w_lo, 1)
                to_bank(bank, u)
                for k in range(KD):
                    o = ps[0:NG, bank, 0:TOK]
                    mm(o, wg_hi[:, k, :], hT_hi[:, k, :], start=k == 0, stop=False)
                    mm(o, wg_lo[:, k, :], hT_hi[:, k, :], start=False, stop=False)
                    ins = mm(o, wg_hi[:, k, :], hT_lo[:, k, :], start=False, stop=k == KD - 1)
                ins.then_inc(full[bank], 1)

            def gate_transposes():
                bank, u = USE["gatesT",]
                to_bank(bank, u)
                for t in range(NT):
                    ins = pe.transpose(ps[:, bank, t * NG:t * NG + NG], gT[0:NG, t * P:t * P + P],
                                       consts[0:NG, 0:NG])
                ins.then_inc(full[bank], 1)

            def kT_transposes(jp):
                bank, u = USE["kT", jp]
                pe.wait_ge(ks_roped, 2)
                to_bank(bank, u)
                transposes(bank, [(br * TOK + t * P, p_kv[:, t, br * CH + jp * P:][:, 0:P])
                                  for br in range(2) for t in range(NT)])

            def scores(m):
                t, h = divmod(m, HEADS)
                j, r = divmod(h, GRP)
                jp, par = divmod(j, 2)
                nk = (t + 1) * P
                rows_ = slice(par * HD, par * HD + HD)
                bank, u = USE["QK", m]
                if m == 0:
                    pe.wait_ge(masks_ready, 1)
                    for key in (("q", 2), ("q", 3), ("kT", 0), ("kT", 1)):
                        pe.wait_ge(free[USE[key][0]], USE[key][1] + 1)
                to_bank(bank, u)
                o = ps[:, bank, 0:2 * nk].rearrange("p (b n) -> p b n", b=2)
                mm(o, qT[rows_, jp * GRP + r, t * P:t * P + P], kT[rows_, jp, :, 0:nk], start=True, stop=False)
                mm(o[:, :, nk - P:nk], ident_b[:, :], causal_b[:, :, :], start=False, stop=True).then_inc(full[bank], 1)

            def prob_transposes(m):
                t = m // HEADS
                qk_bank, qk_u = USE["QK", m]
                bank, u = USE["PT", m]
                pe.wait_ge(free[qk_bank], qk_u + 1)
                to_bank(bank, u)
                transposes(bank, [(n * P, prob[:, m % 2, n * P:n * P + P]) for n in range(2 * (t + 1))])

            def weighted_values(m):
                t, h = divmod(m, HEADS)
                j, r = divmod(h, GRP)
                pe.wait_ge(free[4], USE["PT", m][1] + 1)
                bank, u = USE["O", m // GRP]
                if r == 0:
                    to_bank(bank, u)
                for br in range(2):
                    for kt in range(t + 1):
                        ins = mm(ps[:, bank, r * P + br * HD:][:, 0:HD],
                                 probT[:, m % 2, (br * (t + 1) + kt) * P:][:, 0:P],
                                 p_kv[:, kt, br * CH + KV * HD + j * HD:][:, 0:HD], start=kt == 0, stop=kt == t)
                if r == GRP - 1:
                    ins.then_inc(full[bank], 1)

            def conv_transposes(key):
                kind, n = key
                bank, u = USE[key]
                if kind == "cu":
                    pe.wait_ge(u_ready, 2 if n >= 2 else 4)
                    src = p_h
                else:
                    pe.wait_ge(proj_done, 2 * ((CB_UP if n >= 2 else CB_LO) + 1))
                    src = p_b
                to_bank(bank, u)
                transposes(bank, [(kk * TOK + t * P, src[:, t, (2 * n + kk) * P:][:, 0:P])
                                  for kk in range(2) for t in range(NT)])

            def tick(m):
                if m >= 2:
                    weighted_values(m - 2)
                if 1 <= m <= 2 * HEADS:
                    prob_transposes(m - 1)
                if m < 2 * HEADS:
                    scores(m)
                if m in EXTRA:
                    if EXTRA[m][0] == "kvd":
                        kvd_transposes(EXTRA[m][1])
                    else:
                        conv_transposes(EXTRA[m])

            def conv_square_sum():
                bank, u = USE["css",]
                pe.wait_ge(ysum_ready, 1)
                to_bank(bank, u)
                for t in range(NT):
                    for c in range(2):
                        ins = mm(ps[:, bank, t:t + 1], uT[:, c, t * P:t * P + P], ones, start=c == 0, stop=c == 1)
                ins.then_inc(full[bank], 1)

            def hid_transposes():
                bank, u = USE["hidT",]
                pe.wait_ge(hid_ready, 1)
                to_bank(bank, u)
                transposes(bank, [(n * P, scr[:, n * P:n * P + P]) for n in range(2)])

            def compressed_kv():
                bank, u = USE["kcvc",]
                pe.wait_ge(free[USE["hidT",][0]], USE["hidT",][1] + 1)
                to_bank(bank, u)
                for f in range(2):
                    mm(ps[:, bank, 0:HD], w2k[:, f, :, :].rearrange("p a d -> p (a d)"), hidkT[:, f, :],
                       start=f == 0, stop=f == 1)
                for jp in range(2):
                    for f in range(2):
                        ins = mm(ps[:, bank, HD * (jp + 1):][:, 0:HD],
                                 hidvT[:, f, 2 * jp:2 * jp + 2, :, :].rearrange("p j h n -> p (j h n)"), w2v[:, f, :],
                                 start=f == 0, stop=f == 1)
                ins.then_inc(full[bank], 1)

            def compressed_scores():
                bank, u = USE["cs",]
                pe.wait_ge(free[USE["kcvc",][0]], USE["kcvc",][1] + 1)
                to_bank(bank, u)
                mm(ps[:, bank, :].rearrange("p (t n) -> p t n", t=NT), ident_b[:, :],
                   cmask_b[:, :, :, :].rearrange("p t h n -> p t (h n)"), start=True, stop=True,
                   skip_group_check=True)
                for t in range(NT):
                    for q in range(HEADS // 2):
                        ins = mm(ps[:, bank, (t * (HEADS // 2) + q) * 2 * NCP:][:, 0:2 * NCP],
                                 qT[:, q, t * P:t * P + P], kcT[:, q // GRP, :, :].rearrange("p a n -> p (a n)"),
                                 start=False, stop=True, skip_group_check=True)
                ins.then_inc(full[bank], 1)

            def compressed_prob_transposes(t):
                bank, u = USE["pcT", t]
                pe.wait_ge(cexp_ready, 1)
                to_bank(bank, u)
                flat = pc[:, t, :, :].rearrange("p h n -> p (h n)")
                transposes(bank, [(n * P, flat[:, n * P:n * P + P]) for n in range(2)])

            def compressed_values(n):
                t, par = divmod(n, 2)
                rows_ = slice(par * HD, par * HD + HD)
                bank, u = USE["Oc", n]
                pe.wait_ge(free[USE["pcT", t][0]], USE["pcT", t][1] + 1)
                to_bank(bank, u)
                for jp in range(2):
                    ins = mm(ps[:, bank, jp * TOK:jp * TOK + TOK], pcT[rows_, t, jp, :],
                             vcb[rows_, jp, :, :].rearrange("p h d -> p (h d)"), start=True, stop=True)
                ins.then_inc(full[bank], 1)

            def att_transposes(n):
                pe.wait_ge(y_att_ready, 1)
                for b in range(2):
                    bank, u = USE["aT", n, b]
                    to_bank(bank, u)
                    transposes(bank, [(kk * TOK + t * P, y_att[:, t, (4 * n + 2 * b + kk) * P:][:, 0:P])
                                      for kk in range(2) for t in range(NT)])

            def mixer():
                after = {}

                def put(c, *fs):
                    after.setdefault(c, []).extend(fs)

                put(MIX0 + 3, lambda: x_transposes(1, NDC - 1))
                put(started(KS) + 0, gates)
                put(started(KS) + 3, gate_transposes)
                put(started(KW) + 2, lambda: q_transposes(0), lambda: q_transposes(1))
                put(started(KW) + 5, lambda: q_transposes(2), lambda: q_transposes(3))
                put(started(KC) + 6, lambda: kT_transposes(0), lambda: kT_transposes(1))
                for m in range(2 * HEADS + 2):
                    put(TICK0 + m, lambda m=m: tick(m))
                put(started(CC_LO) + 3, lambda: conv_transposes(("cb", 0)), lambda: conv_transposes(("cb", 1)))
                put(OUT0 - 3, lambda: conv_transposes(("cu", 0)), lambda: conv_transposes(("cu", 1)))
                o = OUT0
                put(o + 5, conv_square_sum)
                put(o + 6, hid_transposes)
                put(o + 7, compressed_kv)
                put(o + 8, compressed_scores)
                put(o + 10, lambda: compressed_prob_transposes(0), lambda: compressed_prob_transposes(1))
                put(o + 12, lambda: compressed_values(0), lambda: compressed_values(1))
                put(o + 13, lambda: compressed_values(2), lambda: compressed_values(3))
                put(o + 14, lambda: att_transposes(0), lambda: att_transposes(1))
                for n in range(NDC - 1):
                    put(AT[("out", NDC + n + 1), 1], lambda n=n: x_transposes(2, n))

                for (job, j), c in AT.items():
                    n = job[-1]
                    if job[0] == "in":
                        if j == 0 and n >= 2:
                            pe.wait_ge(proj_done, 2 * (n - 1))
                        if n == 0:
                            x_operand(1, j)
                        banks = [2 * (n % 2), 2 * (n % 2) + 1]
                        group(c, None, 0, hT_hi, hT_lo, GK * j, banks, j == 0, j == JD - 1)
                    elif job[0] == "cmp":
                        if j == 0:
                            pe.wait_ge(proj_done, 2 * (CB_LO + 1))
                            pe.wait_ge(blk_lo_ready, 2)
                        group(c, None, 0, blk_hi, blk_lo, GK * j, [2], j == 0, j == JD - 1)
                    else:
                        if j == 0:
                            if n == 0:
                                pe.wait_ge(u_ready, 4)
                            elif n == 1:
                                pe.wait_ge(gelu_in, 1)
                            else:
                                pe.wait_ge(resid_done, 2 * (NDC + n - 1))
                        if n == 0:
                            pe.wait_ge(ycT_lo_ready, 2 * (j + 1))
                        if n == NDC:
                            bank, u = USE["aT", j // 2, j % 2]
                            pe.wait_ge(free[bank], u + 1)
                        hi, lo, k = (ycT_hi, ycT_lo, CONV_K_ORDER[j]) if n < NDC else (aT_hi, aT_lo, j)
                        group(c, None, 0, hi, lo, GK * k, [2 * (n % 2), 2 * (n % 2) + 1], j == 0, j == JH - 1)
                    for f in after.get(c, ()):
                        f()

            pe.wait_ge(warm_ready, 1)
            warm_up(0)
            pe.wait_ge(ident_landed, 16)
            ffn(0)
            mixer()
            ffn(1)

        @block.scalar
        def _(act):
            steps = [0]

            def seq(ins):
                ins.then_inc(act_step, 1)
                steps[0] += 1
                act.wait_ge(act_step, steps[0])

            act.dma_start(consts[:, C_ID:C_ID + P], a["shape_consts"][:, C_ID:C_ID + P]).then_inc(ident_landed, 16)
            act.dma_start(vec_rows[V_FFN1:V_FFN1 + KD, :],
                          a["ffn1_norm"].rearrange("l (k p) -> (l k) p", p=P)).then_inc(gains_landed, 16)
            def vectors():
                act.wait_ge(vecs_full, 2)
                act.activation(vecs[:, KD:NVEC], ps[:, 7, KD:NVEC], ACT.Copy).then_inc(vecs_ready, 1)
                act.wait_ge(vecs_ready, 2)

            def hi(c, i=None, per=0):
                act.wait_ge(landed[c % SLOTS], landed_value(c, i, per))
                if c >= SLOTS:
                    act.wait_ge(group_done, count(c - SLOTS + 1, i, per))
                act.activation(w_hi[:, c % SLOTS, :, :], raw[:, c % SLOTS, :, :], ACT.Copy).then_inc(hi_ready, 1)

            def job(c, n, i=None, per=0, after={}):
                for j in range(n):
                    hi(c + j, i, per)
                    for f in after.get(j, ()):
                        f()

            def scaled_operand(dst, tile0, vec0, banks):
                for b, (bank, n) in enumerate(banks):
                    act.wait_ge(full[bank], n + 1)
                    for kk in range(2):
                        k = tile0 + 2 * b + kk
                        ins = act.activation(dst[:, k, :], ps[:, bank, kk * TOK:kk * TOK + TOK], ACT.Copy,
                                             scale=vecs[:, vec0 + k:vec0 + k + 1])
                    ins.then_inc(operand_hi, 1)

            def x_operand(which, n, b=None):
                vec0 = (V_FFN1, V_MIX, V_FFN2)[which]
                for b in range(2) if b is None else (b,):
                    scaled_operand(hT_hi, 4 * n + 2 * b, vec0, [(4 + b, operand_use("x", which, b, n))])

            def square(phase, n, src_ready):
                src_ready()
                for t in range(NT):
                    ins = act.activation(junk[:, t * CH:t * CH + CH], x[:, t, n * CH:n * CH + CH], ACT.Square,
                                         accum_out=ssq[:, phase, t, n:n + 1])
                    seq(ins)
                act.sem_inc(ssq_done, 1)

            def x_square(phase, n, resid):
                square(phase, n, lambda: act.wait_ge(resid_done, resid))

            def root(phase):
                act.wait_ge(var_done, phase + 1)
                act.activation(var[:, phase, :], var[:, phase, :], ACT.Sqrt).then_inc(root_done, 1)

            def silu(f, n, c, i=None):
                act.wait_ge(group_done, count(c, i, 2 * JD))
                act.wait_ge(rs_done, (RS_FFN2 if f else RS_FFN1) + 1)
                for b in range(2):
                    act.wait_ge(full[4 + b], count(operand_use("gu", f, b, n), i, 1))
                for t in range(NT):
                    act.activation(gu[:, t, :], ps[:, t, :], ACT.Silu,
                                   scale=rs[:, RS_FFN2 if f else RS_FFN1, t:t + 1]).then_inc(silu_done, 1)

            def gu_operand(f, n, i=None):
                for b in range(2):
                    act.wait_ge(full[4 + b], count(operand_use("gu", f, b, n) + 1, i, 1))
                    k = 4 * n + 2 * b
                    dst = guT_hi[:, k:k + 2, :] if i is None else guT_hi[:, bass.ds(i * 4 + k, 2), :]
                    act.activation(dst, ps[:, 4 + b, :].rearrange("p (k t) -> p k t", k=2),
                                   ACT.Copy).then_inc(operand_hi, 1)

            def ffn(f):
                c = FFN0[f]
                phase = RS_FFN2 if f else RS_FFN1
                if f == 0:
                    def x_ready(n):
                        act.wait_ge(x_landed[n], 16)
                        if n == 0:
                            act.wait_ge(x_half_landed, 16)
                            act.wait_ge(warm_done, 2)

                    sq = [lambda n=n: square(RS_FFN1, n, lambda: x_ready(n)) for n in range(NDC)]
                    op = [lambda n=n: x_operand(0, n) for n in range(NDC)]
                    x_operand(0, 0, 0)
                    after = {0: [lambda: x_operand(0, 0, 1)], 1: [sq[0]], 2: [op[1]], 3: [sq[1]], 4: [op[2]],
                             5: [sq[2]], 6: [op[3], sq[3]], 7: [lambda: root(RS_FFN1)]}
                else:
                    after = {1: [lambda: x_square(RS_FFN2, NDC - 1, 6 * NDC)],
                             4: [lambda: root(RS_FFN2)], 5: [lambda: x_operand(2, NDC - 1)]}
                job(c, JD, after=after)
                c += JD
                with act.Fori(0, NFC - 1) as i:
                    job(c, JD, i, 2 * JD, after={1: [lambda: silu(f, 0, c, i)]})
                    job(c + JD, JD, i, 2 * JD, after={5: [lambda: gu_operand(f, 0, i)]})
                c += 2 * JD * (NFC - 1)
                job(c, JD, after={1: [lambda: silu(f, NFC - 1, c)]})
                c += JD
                for n in range(NDC):
                    if n == 0:
                        after = {5: [lambda: gu_operand(f, NFC - 1)]}
                        if f == 0:
                            after[8] = [vectors]
                    elif f == 0:
                        after = {3: [lambda: x_square(RS_MIX, n - 1, 2 * n)], 5: [lambda: x_operand(1, n - 1)]}
                    else:
                        after = {3: [lambda: x_square(RS_FINAL, n - 1, 2 * (3 * NDC + n))]}
                    job(c + JF * n, JF, after=after)

            def projected(jb):
                act.wait_ge(group_done, done("in", jb))
                if jb == 0:
                    act.wait_ge(rs_done, RS_MIX + 1)
                if jb == CB_UP:
                    act.wait_ge(blk_lo_ready, 2)
                for t in range(NT):
                    src = ps[:, 2 * (jb % 2) + t, :]
                    if jb in (Q0, Q1):
                        dst = p_q[:, t, jb * CH:jb * CH + CH].rearrange("p (r two d) -> p two r d", r=GRP, two=2)
                        src = src.rearrange("p (two r d) -> p two r d", r=GRP, two=2)
                    else:
                        buf, half = {KS: (p_kv, 0), KW: (p_kv, 1), KC: (p_kvc, 0), CC_UP: (p_cc, 0), CH_UP: (p_h, 1),
                                     CB_UP: (p_b, 1), CH_LO: (p_h, 0), CB_LO: (p_b, 0)}[jb]
                        dst = buf[:, t, half * CH:half * CH + CH]
                    act.activation(dst, src, ACT.Copy, scale=rs[:, RS_MIX, t:t + 1]).then_inc(proj_done, 1)

            def q_operand(n):
                bank, u = USE["q", n]
                act.wait_ge(full[bank], u + 1)
                act.activation(qT[:, 2 * n:2 * n + 2, :], ps[:, bank, :].rearrange("p (k t) -> p k t", k=2),
                               ACT.Copy, scale=-HD ** -0.5).then_inc(free[bank], 1)

            def kT2_operand(n):
                bank, u = USE["kvd", n]
                v, j0 = n // 2, 2 * (n % 2)
                act.wait_ge(full[bank], u + 1)
                src = ps[:, bank, :].rearrange("p (j t) -> p j t", j=2)
                act.activation(kT2[0:HD, v, j0:j0 + 2, :], src[0:HD, :, :], ACT.Copy)
                act.activation(kT2[HD:P, v, j0:j0 + 2, 0:TOK - 1], src[HD:P, :, 1:TOK],
                               ACT.Copy).then_inc(free[bank], 1)

            def kT_operand(jp):
                bank, u = USE["kT", jp]
                act.wait_ge(full[bank], u + 1)
                act.activation(kT[:, jp, :, :], ps[:, bank, :].rearrange("p (b t) -> p b t", b=2),
                               ACT.Copy).then_inc(free[bank], 1)

            def gate_w_load():
                act.wait_ge(group_done, MIX0)
                act.dma_start(w_gate[:, :, :], w_in[:, :, GATE_COL:GATE_COL + NG]).then_inc(gate_w_landed, 16)

            def gate_weights():
                act.wait_ge(gate_w_landed, 16)
                act.activation(wg_hi[:, :, :], w_gate[:, :, :], ACT.Copy).then_inc(gate_w_hi, 1)

            def gate_rows():
                bank, u = USE["gates",]
                act.wait_ge(full[bank], u + 1)
                act.activation(gT[0:NG, :], ps[0:NG, bank, 0:TOK], ACT.Copy).then_inc(free[bank], 1)

            def blocks_hi(h):
                act.wait_ge(blk_ready, 2)
                k = slice(8 * h, 8 * h + 8)
                act.activation(blk_hi[:, k, :], blk_f[:, k, :], ACT.Copy).then_inc(blk_hi_ready, 1)

            def gate_exp():
                act.wait_ge(gates_scaled, 1)
                act.activation(den[:, :, :, :], den[:, :, :, :], ACT.Exp, scale=-1.0).then_inc(gates_exp, 1)

            def exps(m):
                t = m // HEADS
                nk = (t + 1) * P
                bank, u = USE["QK", m]
                act.wait_ge(mins_ready, m + 1)
                if m >= 2:
                    act.wait_ge(full[4], USE["PT", m - 2][1] + 1)
                for br in range(2):
                    ins = act.activation(prob[:, m % 2, br * nk:br * nk + nk], ps[:, bank, br * nk:br * nk + nk],
                                         ACT.Exp, bias=mins[:, m, br:br + 1], scale=-1.0,
                                         accum_out=sums[:, m, br:br + 1])
                ins.then_inc(free[bank], 1)

            def u_operand(n):
                bank, u = USE["cu", n]
                act.wait_ge(full[bank], u + 1)
                if n == 2:
                    act.wait_ge(pads_zero, 2)
                act.activation(uT[:, 2 * n:2 * n + 2, 2:TOK + 2], ps[:, bank, :].rearrange("p (k t) -> p k t", k=2),
                               ACT.Copy).then_inc(free[bank], 1)
                act.wait_ge(free[bank], u + 1)
                for c in (2 * n, 2 * n + 1):
                    act.activation(cv(c), uT[:, c, 0:TOK], ACT.Copy,
                                   scale=vecs[:, V_CONVW + c:V_CONVW + c + 1]).then_inc(tap0_ready, 1)

            def conv_squares(n):
                act.wait_ge(conv_ready, {2: 1, 3: 2, 0: 3, 1: 4}[n])
                act.activation(uT[:, 2 * n:2 * n + 2, 0:TOK], cv_pair(n), ACT.Square).then_inc(ysq_ready, 1)

            def conv_operand(n):
                act.wait_ge(conv_ready, {2: 1, 3: 2, 0: 3, 1: 4}[n])
                for c in (2 * n, 2 * n + 1):
                    act.activation(ycT_hi[:, c, :], cv(c), ACT.Copy,
                                   scale=vecs[:, V_GC + c:V_GC + c + 1]).then_inc(ycT_hi_ready, 1)

            def gelu_copy():
                act.wait_ge(group_done, done("cmp"))
                for v in range(2):
                    ins = act.activation(scr[v * HD:v * HD + HD, 0:CMP_HID],
                                         ps[v * HD:v * HD + HD, 2, v * CMP_HID:(v + 1) * CMP_HID], ACT.Copy)
                ins.then_inc(gelu_in, 1)

            def gelu():
                act.wait_ge(gelu_in, 2)
                act.activation(scr[:, CH:CH + CMP_HID], scr[:, CH:CH + CMP_HID], ACT.Exp,
                               scale=-1.5957691216057308).then_inc(gelu_exp, 1)

            def compressed_exp():
                act.wait_ge(cdiff_ready, 2)
                act.activation(pc[:, :, :, :], pc[:, :, :, :], ACT.Exp, scale=-1.0).then_inc(cexp_ready, 1)

            def compressed_operand(t):
                bank, u = USE["pcT", t]
                act.wait_ge(full[bank], u + 1)
                act.activation(pcT[:, t, :, :], ps[:, bank, 0:TOK].rearrange("p (k t) -> p k t", k=2),
                               ACT.Copy).then_inc(free[bank], 1)

            def att_square():
                act.wait_ge(y_att_ready, 1)
                for t in range(NT):
                    seq(act.activation(junk[:, :], y_att[:, t, :], ACT.Square, accum_out=ssq[:, RS_ATT, t, 0:1]))
                act.sem_inc(ssq_done, 1)

            def att_operand(n):
                scaled_operand(aT_hi, 4 * n, V_GA, [USE["aT", n, b] for b in range(2)])

            def mixer():
                after = {}

                def put(c, *fs):
                    after.setdefault(c, []).extend(fs)

                put(MIX0 + 1, lambda: x_square(RS_MIX, NDC - 1, 2 * NDC))
                put(MIX0 + 4, lambda: root(RS_MIX), gate_w_load)
                put(MIX0 + 5, lambda: x_operand(1, NDC - 1))
                for jb in range(10):
                    put(started(jb) + JD + 1, lambda jb=jb: projected(jb))
                put(started(Q1) + 2, gate_weights)
                put(started(KS) + 3, gate_rows)
                put(started(KS) + 7, gate_exp)
                put(started(KW) + 4, lambda: q_operand(0), lambda: q_operand(1))
                put(started(KW) + 7, lambda: q_operand(2), lambda: q_operand(3))
                put(started(KC) + 8, lambda: kT_operand(0), lambda: kT_operand(1))
                for m in range(2 * HEADS):
                    put(TICK0 + 2 + m, lambda m=m: exps(m))
                    if m in EXTRA:
                        kind, n = EXTRA[m]
                        if kind == "kvd":
                            put(TICK0 + 2 + m, lambda n=n: kT2_operand(n))
                        elif kind == "cu":
                            put(TICK0 + 2 + m, lambda n=n: u_operand(n))
                        else:
                            put(TICK0 + 3 + m, lambda n=n: conv_squares(n), lambda n=n: conv_operand(n))
                for h in range(2):
                    put(started(CB_UP) + 1 + h, lambda h=h: blocks_hi(h))
                o = OUT0
                put(o - 1, lambda: u_operand(0))
                put(o, lambda: u_operand(1))
                put(o + 1, gelu_copy)
                put(o + 3, lambda: conv_operand(0), lambda: conv_operand(1))
                put(o + 4, lambda: conv_squares(0), lambda: conv_squares(1))
                put(o + 5, gelu)
                put(o + 6, lambda: root(RS_CONV))
                put(o + 10, compressed_exp)
                put(o + 12, lambda: compressed_operand(0), lambda: compressed_operand(1))
                put(o + 16, lambda: att_operand(0), lambda: att_operand(1))
                put(o + 18, att_square)
                put(o + 19, lambda: root(RS_ATT))
                for n in range(NDC - 1):
                    put(AT[("out", NDC + n + 1), 3], lambda n=n: x_operand(2, n))
                    put(AT[("out", NDC + n + 1), 3] + 1, lambda n=n: x_square(RS_FFN2, n, 2 * (2 * NDC + n + 1)))
                return after

            act.wait_ge(warm_ready, 1)
            seq(act.activation(junk[:, CH:CH + 1], junk[:, 0:1], ACT.Sqrt))
            act.wait_ge(vecs_full, 1)
            act.activation(vecs[:, 0:KD], ps[:, 6, 0:KD], ACT.Copy).then_inc(vecs_ready, 1)
            act.wait_ge(vecs_ready, 1)
            ffn(0)
            mix_after = mixer()
            for c in range(MIX0, FFN0[1]):
                hi(c)
                for f in mix_after.pop(c, ()):
                    f()
            for c in sorted(mix_after):
                for f in mix_after[c]:
                    f()
            ffn(1)
            seq(act.activation(junk[:, 0:1], ones, ACT.Sqrt))
            for t in range(NT):
                act.wait_ge(resid_done, 8 * NDC - NT + t + 1)
                act.activation(junk[:, t * CH:t * CH + CH], x[:, t, DM - CH:DM], ACT.Square,
                               accum_out=ssq[:, RS_FINAL, t, NDC - 1:NDC]).then_inc(final_ssq[t], 1)
                act.wait_ge(final_var[t], 1)
                v = var[:, RS_FINAL, t:t + 1]
                act.activation(v, v, ACT.Sqrt).then_inc(final_root[t], 1)
                act.wait_ge(final_rs[t], 1)
                act.wait_ge(xg_ready, 2 * NDC - NT + t + 1)
                for q in range(2):
                    cols = slice((2 + q) * CH, (3 + q) * CH)
                    act.activation(y_fin[:, t, cols], y_fin[:, t, cols], ACT.Copy,
                                   scale=rs[:, RS_FINAL, t:t + 1]).then_inc(final_act, 1)

        @block.vector
        def _(dve):
            steps = [0]

            def seq(ins):
                ins.then_inc(dve_step, 1)
                steps[0] += 1
                dve.wait_ge(dve_step, steps[0])

            tt = nc.vector.tensor_tensor
            stt = nc.vector.scalar_tensor_tensor

            def lo(c, i=None, per=0):
                dve.wait_ge(hi_ready, count(c + 1, i, per))
                s = c % SLOTS
                tt(w_lo[:, s, :, :], raw[:, s, :, :], w_hi[:, s, :, :].bitcast(F32),
                   ALU.subtract).then_inc(lo_ready, 1)

            def job(c, n, i=None, per=0, after={}):
                for j in range(n):
                    lo(c + j, i, per)
                    for f in after.get(j, ()):
                        f()

            OP_X = {0: 0, 1: 2 * (NDC + NFC), 2: 2 * (NDC + NFC + NDC + 2)}
            OP_GU = [2 * NDC, OP_X[2] + 2 * NDC]
            OP_ATT = 2 * (NDC + NFC + NDC)

            def scaled_operand(hi_t, lo_t, tile0, vec0, banks, op0):
                for b, bank in enumerate(banks):
                    dve.wait_ge(operand_hi, op0 + b + 1)
                    for kk in range(2):
                        k = tile0 + 2 * b + kk
                        ins = stt(out=lo_t[:, k, :], in0=ps[:, bank, kk * TOK:kk * TOK + TOK],
                                  scalar=vecs[:, vec0 + k:vec0 + k + 1], in1=hi_t[:, k, :].bitcast(F32),
                                  op0=ALU.mult, op1=ALU.subtract)
                    ins.then_inc(free[bank], 1)

            def x_operand(which, n, b=None):
                vec0 = (V_FFN1, V_MIX, V_FFN2)[which]
                for b in range(2) if b is None else (b,):
                    scaled_operand(hT_hi, hT_lo, 4 * n + 2 * b, vec0, (4 + b,), OP_X[which] + 2 * n + b)

            def variance(phase, width, ssq_count, cols=NDC):
                dve.wait_ge(ssq_done, ssq_count)
                if cols > 1:
                    seq(nc.vector.tensor_reduce(var[:, phase, :], ssq[:, phase, :, 0:cols], axis=AX.X, op=ALU.add))
                    src = var[:, phase, :]
                else:
                    src = ssq[:, phase, :, 0]
                nc.vector.tensor_scalar(var[:, phase, :], src, 1.0 / width, EPS, ALU.mult,
                                        ALU.add).then_inc(var_done, 1)

            def inverse_root(phase):
                dve.wait_ge(root_done, phase + 1)
                nc.vector.reciprocal(rs[:, phase, :], var[:, phase, :]).then_inc(rs_done, 1)
                dve.wait_ge(rs_done, phase + 1)

            def up(f, n, done, i=None):
                dve.wait_ge(group_done, count(done, i, 2 * JD))
                dve.wait_ge(silu_done, count(2 * (NFC * f + n + 1), i, 2))
                for t in range(NT):
                    stt(out=gu[:, t, :], in0=ps[:, 2 + t, :], scalar=rs[:, RS_FFN2 if f else RS_FFN1, t:t + 1],
                        in1=gu[:, t, :], op0=ALU.mult, op1=ALU.mult).then_inc(gu_done, 1)

            def gu_operand(f, n, i=None):
                for b in range(2):
                    dve.wait_ge(operand_hi, count(OP_GU[f] + 2 * n + b + 1, i, 2))
                    k = 4 * n + 2 * b
                    sl = slice(k, k + 2) if i is None else bass.ds(i * 4 + k, 2)
                    tt(guT_lo[:, sl, :], ps[:, 4 + b, :].rearrange("p (k t) -> p k t", k=2),
                       guT_hi[:, sl, :].bitcast(F32), ALU.subtract).then_inc(free[4 + b], 1)

            def residual(n, done, pair, scale):
                dve.wait_ge(group_done, done)
                for t in range(NT):
                    xs = x[:, t, n * CH:n * CH + CH]
                    stt(out=xs, in0=ps[:, 2 * pair + t, :], scalar=scale(t), in1=xs,
                        op0=ALU.mult, op1=ALU.add).then_inc(resid_done, 1)

            half = lambda t: 0.5

            def final_gains(n):
                dve.wait_ge(g_fin_landed, 16)
                dve.wait_ge(resid_done, 2 * (3 * NDC + n + 1))
                for t in range(NT):
                    cols = slice(n * CH, n * CH + CH)
                    tt(y_fin[:, t, cols], x[:, t, cols], g_fin[:, cols], ALU.mult).then_inc(xg_ready, 1)

            def ffn(f):
                c = FFN0[f]
                if f == 0:
                    x_operand(0, 0, 0)
                    op = [lambda n=n: x_operand(0, n) for n in range(NDC)]
                    after = {0: [lambda: x_operand(0, 0, 1)], 2: [op[1]], 4: [op[2]],
                             6: [op[3], lambda: variance(RS_FFN1, DM, NDC)],
                             7: [lambda: inverse_root(RS_FFN1)]}
                else:
                    after = {1: [lambda: residual(NDC - 1, FFN0[1], 1, att_scale)],
                             3: [lambda: variance(RS_FFN2, DM, 3 * NDC + 1)],
                             5: [lambda: x_operand(2, NDC - 1)], 6: [lambda: inverse_root(RS_FFN2)]}
                job(c, JD, after=after)
                c += JD
                with dve.Fori(0, NFC - 1) as i:
                    job(c, JD, i, 2 * JD)
                    job(c + JD, JD, i, 2 * JD, after={1: [lambda: up(f, 0, c + JD, i)],
                                                      5: [lambda: gu_operand(f, 0, i)]})
                c += 2 * JD * (NFC - 1)
                job(c, JD)
                c += JD
                for n in range(NDC):
                    if n == 0:
                        after = {1: [lambda: up(f, NFC - 1, c)], 5: [lambda: gu_operand(f, NFC - 1)]}
                    else:
                        after = {1: [lambda: residual(n - 1, c + JF * n, (n - 1) % 2, half)]}
                        if f == 0:
                            after[5] = [lambda: x_operand(1, n - 1)]
                        else:
                            after[5] = [lambda: final_gains(n - 1)]
                    job(c + JF * n, JF, after=after)

            def rope(x_lo, x_hi, x_all, s_lo, s_hi, s_all, cos, sin, shape_half, shape_all, last_out=None,
                     last_in=None):
                seq(tt(s_lo, x_hi, sin[0].to_broadcast(shape_half), ALU.mult))
                seq(tt(s_hi, x_lo, sin[1].to_broadcast(shape_half), ALU.mult))
                seq(tt(x_all, x_all, cos.to_broadcast(shape_all), ALU.mult))
                if last_out is None:
                    return tt(x_all, x_all, s_all, ALU.add)
                return tt(last_out, last_in(x_all), last_in(s_all), ALU.add)

            def rope_q(t):
                if t == 0:
                    dve.wait_ge(proj_done, 2 * (Q1 + 1))
                v = p_q[:, t, :].rearrange("p (h d) -> p h d", d=HD)
                s = scr[:, :].rearrange("p (h d) -> p h d", d=HD)
                sh, sa = [P, HEADS, HD // 2], [P, HEADS, HD]
                sin = [sin_t[:, t, 0:HD // 2].unsqueeze(1), sin_t[:, t, HD // 2:HD].unsqueeze(1)]
                seq_ins = rope(v[:, :, 0:HD // 2], v[:, :, HD // 2:HD], v, s[:, :, 0:HD // 2], s[:, :, HD // 2:HD], s,
                               cos_t[:, t, :].unsqueeze(1), sin, sh, sa)
                seq_ins.then_inc(q_roped, 1)
                dve.wait_ge(q_roped, t + 1)

            def rope_kc(t):
                if t == 0:
                    dve.wait_ge(proj_done, 2 * (KC + 1))
                v = p_kvc[:, t, 0:KV * HD].rearrange("p (h d) -> p h d", d=HD)
                s = scr[:, 0:KV * HD].rearrange("p (h d) -> p h d", d=HD)
                sh, sa = [P, KV, HD // 2], [P, KV, HD]
                sin = [sin_t[:, t, 0:HD // 2].unsqueeze(1), sin_t[:, t, HD // 2:HD].unsqueeze(1)]
                twice = lambda u: u.unsqueeze(2).to_broadcast([P, KV, 2, HD])
                dst = kvd[:, t, :, :, :].rearrange("p v j (a d) -> p v j a d", a=2)
                rope(v[:, :, 0:HD // 2], v[:, :, HD // 2:HD], v, s[:, :, 0:HD // 2], s[:, :, HD // 2:HD], s,
                     cos_t[:, t, :].unsqueeze(1), sin, sh, sa, dst[:, 0, :, :, :], twice)
                vv = p_kvc[:, t, KV * HD:2 * KV * HD].rearrange("p (h d) -> p h d", d=HD)
                nc.vector.tensor_copy(dst[:, 1, :, :, :], twice(vv)).then_inc(kvd_ready, 1)
                dve.wait_ge(kvd_ready, t + 1)

            def rope_ks(br, t):
                if t == 0:
                    dve.wait_ge(proj_done, 2 * (KS + br + 1))
                v = p_kv[:, t, br * CH:br * CH + KV * HD].rearrange("p (h d) -> p h d", d=HD)
                s = scr[:, 0:KV * HD].rearrange("p (h d) -> p h d", d=HD)
                sh, sa = [P, KV, HD // 2], [P, KV, HD]
                sin = [sin_t[:, t, 0:HD // 2].unsqueeze(1), sin_t[:, t, HD // 2:HD].unsqueeze(1)]
                ins = rope(v[:, :, 0:HD // 2], v[:, :, HD // 2:HD], v, s[:, :, 0:HD // 2], s[:, :, HD // 2:HD], s,
                           cos_t[:, t, :].unsqueeze(1), sin, sh, sa)
                if t:
                    ins.then_inc(ks_roped, 1)
                    dve.wait_ge(ks_roped, br + 1)
                else:
                    seq(ins)

            def blocks(v):
                for n in (2 * v, 2 * v + 1):
                    bank, u = USE["kvd", n]
                    dve.wait_ge(free[bank], u + 1)
                dve.wait_ge(pads_zero, 1)
                toks = kT2[:, v, :, :].rearrange("p j (n s w) -> p s j n w", s=8, w=2)
                for h in range(2):
                    pe_col = (V_PEK, V_PEV)[v] + 8 * h
                    o = blk_f[:, 8 * h:8 * h + 8, v * KV * NCP:(v + 1) * KV * NCP].rearrange(
                        "p k (j n) -> p k j n", j=KV)[:, :, :, 0:NCMP]
                    pos = vecs[:, pe_col:pe_col + 8].unsqueeze(2).unsqueeze(3).to_broadcast([P, 8, KV, NCMP])
                    ins = tt(o, toks[:, :, :, h:h + NCMP, 0], pos, ALU.add)
                ins.then_inc(blk_ready, 1)
                if v == 1:
                    dve.wait_ge(blk_ready, 2)
                    nc.vector.memset(uT[:, :, 0:2], 0.0).then_inc(pads_zero, 1)

            def gate_weights():
                dve.wait_ge(gate_w_hi, 1)
                tt(wg_lo[:, :, :], w_gate[:, :, :], wg_hi[:, :, :].bitcast(F32), ALU.subtract).then_inc(gate_w_lo, 1)

            def blocks_lo(h):
                dve.wait_ge(blk_hi_ready, h + 1)
                k = slice(8 * h, 8 * h + 8)
                tt(blk_lo[:, k, :], blk_f[:, k, :], blk_hi[:, k, :].bitcast(F32),
                   ALU.subtract).then_inc(blk_lo_ready, 1)

            def gates_in():
                bank, u = USE["gatesT",]
                dve.wait_ge(full[bank], u + 1)
                for t in range(NT):
                    ins = nc.vector.tensor_scalar(den[:, t, :, :].rearrange("p h g -> p (h g)"),
                                                  ps[:, bank, t * NG:t * NG + NG], rs[:, RS_MIX, t:t + 1], None,
                                                  ALU.mult)
                ins.then_inc(gates_scaled, 1)
                dve.wait_ge(gates_scaled, 1)
                dve.sem_inc(free[bank], 1)

            def gates_den():
                dve.wait_ge(gates_exp, 1)
                seq(nc.vector.tensor_scalar(den[:, :, :, :], den[:, :, :, :], 1.0, None, ALU.add))

            def score_min(m):
                t = m // HEADS
                nk = (t + 1) * P
                bank, u = USE["QK", m]
                dve.wait_ge(full[bank], u + 1)
                nc.vector.tensor_reduce(mins[:, m, :], ps[:, bank, 0:2 * nk].rearrange("p (b n) -> p b n", b=2),
                                        axis=AX.X, op=ALU.min).then_inc(mins_ready, 1)

            def prob_operand(m):
                t = m // HEADS
                n = 2 * (t + 1) * P
                bank, u = USE["PT", m]
                dve.wait_ge(full[bank], u + 1)
                nc.vector.tensor_copy(probT[:, m % 2, 0:n], ps[:, bank, 0:n]).then_inc(free[bank], 1)

            def gate_over_sum(n):
                t, j = divmod(n, KV)
                m = GRP * n
                bank, u = USE["QK", m + GRP - 1]
                dve.wait_ge(free[bank], u + 1)
                seq(tt(coef[:, :, :], den[:, t, GRP * j:GRP * j + GRP, 1:3], sums[:, m:m + GRP, :], ALU.mult))
                seq(nc.vector.reciprocal(coef[:, :, :], coef[:, :, :]))

            def weighted(n):
                t, j = divmod(n, KV)
                bank, u = USE["O", n]
                dve.wait_ge(full[bank], u + 1)
                s = scr[:, 0:CH].rearrange("p (h b d) -> p h b d", h=GRP, b=2)
                o = ps[:, bank, :].rearrange("p (h b d) -> p h b d", h=GRP, b=2)
                tt(s, o, coef[:, :, :].unsqueeze(3).to_broadcast([P, GRP, 2, HD]), ALU.mult).then_inc(free[bank], 1)
                dve.wait_ge(free[bank], u + 1)
                seq(tt(y_att[:, t, j * TOK:(j + 1) * TOK].rearrange("p (h d) -> p h d", h=GRP),
                       s[:, :, 0, :], s[:, :, 1, :], ALU.add))

            def conv_input_upper():
                dve.wait_ge(proj_done, 2 * (CH_UP + 1))
                for t in range(NT):
                    xs = p_h[:, t, CH:2 * CH]
                    tt(xs, p_cc[:, t, :], xs, ALU.mult).then_inc(u_ready, 1)

            def conv_input_lower():
                dve.wait_ge(proj_done, 2 * (CH_LO + 1))
                dve.wait_ge(group_done, done("in", CC_LO))
                for t in range(NT):
                    xs = p_h[:, t, 0:CH]
                    stt(out=xs, in0=ps[:, t, :], scalar=rs[:, RS_MIX, t:t + 1], in1=xs, op0=ALU.mult,
                        op1=ALU.mult).then_inc(u_ready, 1)

            def conv_taps(tiles):
                for n in sorted({c // 2 for c in tiles}):
                    bank, u = USE["cu", n]
                    dve.wait_ge(free[bank], u + 1)
                w = lambda tap, c: vecs[:, V_CONVW + tap * CT + c:V_CONVW + tap * CT + c + 1]
                for tap in (1, 2):
                    for c in tiles:
                        if tap == 1:
                            dve.wait_ge(tap0_ready, (c + 4) % CT + 1)
                        ins = stt(out=cv(c), in0=uT[:, c, tap:tap + TOK], scalar=w(tap, c), in1=cv(c),
                                  op0=ALU.mult, op1=ALU.add)
                    seq(ins)

            def conv_gate(n):
                bank, u = USE["cb", n]
                dve.wait_ge(full[bank], u + 1)
                tt(cv_pair(n), ps[:, bank, :].rearrange("p (k t) -> p k t", k=2), cv_pair(n),
                   ALU.mult).then_inc(conv_ready, 1)
                dve.wait_ge(conv_ready, {2: 1, 3: 2, 0: 3, 1: 4}[n])
                dve.sem_inc(free[bank], 1)

            def conv_operand(n):
                for q, c in enumerate((2 * n, 2 * n + 1)):
                    dve.wait_ge(ycT_hi_ready, {2: 0, 3: 2, 0: 4, 1: 6}[n] + q + 1)
                    stt(out=ycT_lo[:, c, :], in0=cv(c), scalar=vecs[:, V_GC + c:V_GC + c + 1],
                        in1=ycT_hi[:, c, :].bitcast(F32), op0=ALU.mult, op1=ALU.subtract).then_inc(ycT_lo_ready, 1)

            def conv_variance():
                bank, u = USE["css",]
                dve.wait_ge(full[bank], u + 1)
                nc.vector.tensor_scalar(var[:, RS_CONV, :], ps[:, bank, 0:NT], 1.0 / CONV, EPS, ALU.mult,
                                        ALU.add).then_inc(var_done, 1)
                dve.wait_ge(var_done, RS_CONV + 1)
                dve.sem_inc(free[bank], 1)

            hx, hq = scr[:, 0:CMP_HID], scr[:, CH:CH + CMP_HID]

            def gelu_cube():
                dve.wait_ge(gelu_in, 1)
                seq(tt(hq, hx, hx, ALU.mult))
                seq(nc.vector.tensor_scalar(hq, hq, 0.044715, 1.0, ALU.mult, ALU.add))
                tt(hq, hq, hx, ALU.mult).then_inc(gelu_in, 1)

            def gelu_out():
                dve.wait_ge(gelu_exp, 1)
                seq(nc.vector.tensor_scalar(hq, hq, 1.0, None, ALU.add))
                seq(nc.vector.reciprocal(hq, hq))
                tt(hx, hx, hq, ALU.mult).then_inc(hid_ready, 1)

            def hidden_operand():
                bank, u = USE["hidT",]
                dve.wait_ge(full[bank], u + 1)
                src = ps[:, bank, 0:2 * P].rearrange("p (f m) -> p f m", f=2)
                nc.vector.tensor_copy(hidkT[:, :, :], src[:, 0:2, 0:KV * NCP])
                for f in range(2):
                    v = src[:, f, KV * NCP:2 * KV * NCP].rearrange("p (j n) -> p j n", j=KV)
                    ins = nc.vector.tensor_copy(hidvT[:, f, :, :, :], v.unsqueeze(2).to_broadcast([P, KV, GRP, NCP]))
                ins.then_inc(free[bank], 1)

            def compressed_operands():
                bank, u = USE["kcvc",]
                dve.wait_ge(full[bank], u + 1)
                seq(nc.vector.memset(kcT[:, :, :, :], 0.0))
                for par in range(2):
                    rows_ = slice(par * HD, par * HD + HD)
                    kc = ps[:, bank, 0:KV * NCP].rearrange("p (jp a n) -> p jp a n", jp=2, a=2)
                    nc.vector.tensor_copy(kcT[rows_, :, par, :], kc[rows_, :, par, :])
                sel = consts[:, C_BMASK:C_BMASK + GRP].unsqueeze(2).to_broadcast([P, GRP, HD])
                for jp in range(2):
                    v = ps[:, bank, HD * (jp + 1):][:, 0:HD]
                    ins = tt(vcb[:, jp, :, :], v.unsqueeze(1).to_broadcast([P, GRP, HD]), sel, ALU.mult)
                ins.then_inc(free[bank], 1)

            def compressed_min():
                bank, u = USE["cs",]
                dve.wait_ge(full[bank], u + 1)
                lows = cmin[:, :, :].rearrange("p t h -> p (t h)")
                seq(nc.vector.tensor_reduce(lows, ps[:, bank, :].rearrange("p (h n) -> p h n", n=NCP), axis=AX.X,
                                            op=ALU.min))
                s = ps[:, bank, :].rearrange("p (q r two n) -> p two q r n", r=GRP, two=2, n=NCP)
                low = lows.rearrange("p (q r two) -> p two q r", r=GRP, two=2)
                dst = pc[:, :, :, :].rearrange("p t (jp two r) n -> p two (t jp) r n", two=2, r=GRP)
                for par in range(2):
                    tt(dst[:, par, :, :, :], s[:, par, :, :, :], low[:, par, :, :].unsqueeze(3).to_broadcast(
                        [P, 4, GRP, NCP]), ALU.subtract).then_inc(cdiff_ready, 1)
                dve.wait_ge(cdiff_ready, 2)
                dve.sem_inc(free[bank], 1)

            def compressed_coef(t):
                dve.wait_ge(cexp_ready, 1)
                seq(nc.vector.tensor_reduce(csum[:, t, :], pc[:, t, :, :], axis=AX.X, op=ALU.add))
                seq(tt(csum[:, t, :], csum[:, t, :], den[:, t, :, 0], ALU.mult))
                seq(nc.vector.reciprocal(csum[:, t, :], csum[:, t, :]))
                seq(nc.vector.tensor_scalar(csum[:, t, :], csum[:, t, :], consts[:, C_VALID + t:C_VALID + t + 1], None,
                                            ALU.mult))

            def compressed_weighted(n):
                t, par = divmod(n, 2)
                bank, u = USE["Oc", n]
                dve.wait_ge(full[bank], u + 1)
                s = scr[:, 0:CH].rearrange("p (jp r d) -> p jp r d", jp=2, d=HD)
                o = ps[:, bank, :].rearrange("p (jp r d) -> p jp r d", jp=2, d=HD)
                c = csum[:, t, :].rearrange("p (jp two r) -> p two jp r", two=2, r=GRP)[:, par, :, :]
                tt(s, o, c.unsqueeze(3).to_broadcast([P, 2, GRP, HD]), ALU.mult).then_inc(free[bank], 1)
                dve.wait_ge(free[bank], u + 1)
                y = y_att[:, t, :].rearrange("p (jp two m) -> p two jp m", two=2, m=GRP * HD)[:, par, :, :]
                ins = tt(y, y, scr[:, 0:CH].rearrange("p (jp m) -> p jp m", jp=2), ALU.add)
                if n == 3:
                    ins.then_inc(y_att_ready, 1)
                else:
                    seq(ins)

            def att_operand(n):
                scaled_operand(aT_hi, aT_lo, 4 * n, V_GA, [USE["aT", n, b][0] for b in range(2)], OP_ATT + 2 * n)

            conv_scale = lambda t: rs[:, RS_CONV, t:t + 1]
            att_scale = lambda t: rs[:, RS_ATT, t:t + 1]

            def mixer():
                after = {}

                def put(c, *fs):
                    after.setdefault(c, []).extend(fs)

                put(MIX0 + 1, lambda: residual(NDC - 1, MIX0, 1, half))
                put(MIX0 + 3, lambda: variance(RS_MIX, DM, 2 * NDC))
                put(MIX0 + 5, lambda: x_operand(1, NDC - 1))
                put(MIX0 + 6, lambda: inverse_root(RS_MIX))
                put(started(Q1) + 3, gate_weights)
                put(started(KS) + 3, lambda: rope_q(0))
                put(started(KS) + 6, lambda: rope_q(1))
                put(started(KS) + 7, gates_in)
                put(started(KW) + 1, gates_den)
                for t in range(NT):
                    put(started(KW) + 3 + t, lambda t=t: rope_ks(0, t))
                    put(started(KC) + 3 + t, lambda t=t: rope_ks(1, t))
                for m in range(2 * HEADS + 2):
                    c = TICK0 + 2 + m
                    if 1 <= m <= 2 * HEADS:
                        put(c, lambda m=m: prob_operand(m - 1))
                    if m < 2 * HEADS:
                        put(c, lambda m=m: score_min(m))
                    if m >= GRP and m % GRP == 0:
                        put(c, lambda n=m // GRP - 1: gate_over_sum(n))
                    if m >= 2 and (m - 2) % GRP == GRP - 1:
                        put(c, lambda n=(m - 2) // GRP: weighted(n))
                    if m in EXTRA and EXTRA[m][0] == "cb":
                        put(c, lambda n=EXTRA[m][1]: conv_gate(n))
                        put(c + 2, lambda n=EXTRA[m][1]: conv_operand(n))
                put(started(CC_UP) + 3, lambda: rope_kc(0))
                put(started(CC_UP) + 5, lambda: rope_kc(1))
                for h in range(2):
                    put(started(CB_UP) - 1 + h, lambda v=h: blocks(v))
                    put(started(CB_UP) + 2 + h, lambda h=h: blocks_lo(h))
                put(started(CB_UP) + 4, conv_input_upper)
                put(TICK0 + 3 + max(m for m in EXTRA if EXTRA[m][0] == "cu"), lambda: conv_taps([4, 5, 6, 7]))
                o = OUT0
                put(o - 4, conv_input_lower)
                put(o, lambda: conv_taps([0, 1]))
                put(o + 1, lambda: conv_taps([2, 3]))
                put(o + 2, lambda: conv_gate(0), lambda: conv_gate(1))
                put(o + 3, lambda: conv_operand(0), lambda: conv_operand(1))
                put(o + 4, gelu_cube)
                put(o + 5, gelu_out)
                put(o + 6, conv_variance, lambda: inverse_root(RS_CONV))
                put(o + 7, lambda: residual(0, done("out", 0), 0, conv_scale), hidden_operand)
                put(o + 8, compressed_operands)
                put(o + 10, compressed_min)
                put(o + 11, lambda: compressed_coef(0), lambda: compressed_coef(1))
                put(o + 13, lambda: compressed_weighted(0), lambda: compressed_weighted(1))
                put(o + 14, lambda: compressed_weighted(2), lambda: compressed_weighted(3))
                put(o + 16, lambda: att_operand(0), lambda: att_operand(1))
                put(o + 19, lambda: variance(RS_ATT, CONV, 2 * NDC + 1, cols=1))
                put(o + 20, lambda: inverse_root(RS_ATT))
                for n in range(1, 2 * NDC - 1):
                    put(done("out", n) + (0 if n == 1 else 1), lambda n=n: residual(
                        n % NDC, done("out", n), n % 2, conv_scale if n < NDC else att_scale))
                for n in range(NDC - 1):
                    put(AT[("out", NDC + n + 1), 3], lambda n=n: x_operand(2, n))
                return after

            nc.vector.memset(junk[:, 0:CH], 0.0).then_inc(warm_ready, 1)
            ffn(0)
            mix_after = mixer()
            for c in range(MIX0, FFN0[1]):
                lo(c)
                for f in mix_after.pop(c, ()):
                    f()
            for c in sorted(mix_after):
                for f in mix_after[c]:
                    f()
            ffn(1)
            for t in range(NT):
                if t == 0:
                    dve.wait_ge(first_tile_done, 1)
                else:
                    dve.wait_ge(group_done, END)
                xs = x[:, t, DM - CH:DM]
                stt(out=xs, in0=ps[:, 2 + t, :], scalar=0.5, in1=xs, op0=ALU.mult,
                    op1=ALU.add).then_inc(resid_done, 1)
                dve.wait_ge(resid_done, 8 * NDC - NT + t + 1)
                tt(y_fin[:, t, DM - CH:DM], xs, g_fin[:, DM - CH:DM], ALU.mult).then_inc(xg_ready, 1)
                dve.wait_ge(final_ssq[t], 1)
                v = var[:, RS_FINAL, t:t + 1]
                seq(nc.vector.tensor_reduce(v, ssq[:, RS_FINAL, t, :], axis=AX.X, op=ALU.add))
                nc.vector.tensor_scalar(v, v, 1.0 / DM, EPS, ALU.mult, ALU.add).then_inc(final_var[t], 1)
                dve.wait_ge(final_root[t], 1)
                nc.vector.reciprocal(rs[:, RS_FINAL, t:t + 1], v).then_inc(final_rs[t], 1)
                dve.wait_ge(final_rs[t], 1)
                for q in range(2):
                    cols = slice(q * CH, (q + 1) * CH)
                    nc.vector.tensor_scalar(y_fin[:, t, cols], y_fin[:, t, cols], rs[:, RS_FINAL, t:t + 1], None,
                                            ALU.mult).then_inc(final_dve, 1)


def shape_constants():
    import numpy as np
    c = np.zeros((P, NCONST), np.float32)
    row = np.arange(P)
    c[:, C_ID:C_ID + P] = np.eye(P, dtype=np.float32)
    c[:, C_CAUSAL:C_CAUSAL + P] = np.where(row[None, :] > row[:, None], BIG, 0.0)
    for t in range(NT):
        pos = t * P + row
        end = np.arange(NCP) * CMP_STRIDE + CMP_BLOCK - 1
        masked = (end[None, :] > pos[:, None]) | (np.arange(NCP) >= NCMP)[None, :]
        c[:, C_CMASK + t * NCP:C_CMASK + (t + 1) * NCP] = np.where(masked, BIG, 0.0)
        c[:, C_VALID + t] = pos >= CMP_BLOCK - 1
        inv = np.float32(10000.0) ** (-np.arange(0, HD, 2, dtype=np.float32) / np.float32(HD))
        ang = pos.astype(np.float32)[:, None] * inv[None, :]
        cos, sin = np.cos(ang), np.sin(ang)
        c[:, C_COS + t * HD:C_COS + (t + 1) * HD] = np.concatenate([cos, cos], 1)
        c[:, C_SIN + t * HD:C_SIN + (t + 1) * HD] = np.concatenate([-sin, sin], 1)
    for h in range(GRP):
        c[:, C_BMASK + h] = (row // NCP) % GRP == h
    c[:, C_ONE] = 1.0
    return c


_INS = ['x', 'ffn1_norm', 'ffn1_wg', 'ffn1_wu', 'ffn1_wd', 'mix_norm', 'w_in', 'conv_w', 'cmp_k_w1', 'cmp_k_w2',
        'cmp_k_pe', 'cmp_v_w1', 'cmp_v_w2', 'cmp_v_pe', 'conv_out_norm', 'attn_out_norm', 'w_out', 'ffn2_norm',
        'ffn2_wg', 'ffn2_wu', 'ffn2_wd', 'final_norm']


def kernel(**inputs):
    import numpy as _np
    import concourse.bacc as _bacc
    from concourse import mybir as _mybir
    from concourse.bass_utils import run_bass_kernel_spmd as _run

    nc = _bacc.Bacc("TRN2", target_bir_lowering=False, num_devices=1)
    arrays, args = {}, {}
    for name in _INS + ["shape_consts"]:
        v = shape_constants() if name == "shape_consts" else _np.ascontiguousarray(inputs[name])
        arrays[f"in_{name}_dram"] = v
        args[name] = nc.dram_tensor(f"in_{name}_dram", v.shape, _mybir.dt.from_np(v.dtype), kind="ExternalInput").ap()
    out = nc.dram_tensor("out_0_dram", (1, TOK, DM), _mybir.dt.from_np(_np.dtype("float32")),
                         kind="ExternalOutput").ap()
    build_program(nc, args, out)
    r = _run(nc, [arrays], core_ids=[0])
    return r.results[0]["out_0_dram"]
```
